# Optimizing a Trainium2 kernel written in Bass

```python
import math
import jax, jax.numpy as jnp
from jax import lax
import numpy as np

D_MODEL = 1024
BATCH = 1
SEQ = 1024
DEPTH = 1

SSM_WIDTH = 512
SSM_GROUP = 16
SSM_GROUPS = SSM_WIDTH // SSM_GROUP
SSM_STATE = 64
STEP_MIN = 0.001
STEP_MAX = 0.1
RET_HEADS = 4
RET_DK = 128
RET_DV = 256
RET_QK_WIDTH = RET_HEADS * RET_DK
RET_V_WIDTH = RET_HEADS * RET_DV
RET_CHUNK = 128
ROPE_BASE = 10000.0
D_FF = 4 * D_MODEL
EPS = 1e-6
IN_WIDTH = SSM_WIDTH + 2 * RET_QK_WIDTH + 2 * RET_V_WIDTH + 2 * D_MODEL
IN_SPLITS = (
    SSM_WIDTH,
    SSM_WIDTH + RET_QK_WIDTH,
    SSM_WIDTH + 2 * RET_QK_WIDTH,
    SSM_WIDTH + 2 * RET_QK_WIDTH + RET_V_WIDTH,
    SSM_WIDTH + 2 * RET_QK_WIDTH + 2 * RET_V_WIDTH,
    SSM_WIDTH + 2 * RET_QK_WIDTH + 2 * RET_V_WIDTH + D_MODEL,
)

kernel_name = "hybrid_s5_retention_gated_trunk"

def rmsnorm(x, g):
    x32 = x.astype(jnp.float32)
    y = x32 * lax.rsqrt(jnp.mean(x32 * x32, axis=-1, keepdims=True) + EPS)
    return (y * g.astype(jnp.float32)).astype(x.dtype)

def cmul(ar, ai, br, bi):
    return ar * br - ai * bi, ar * bi + ai * br

def s5_branch(u, lam_re, lam_im, b_re, b_im, c_re, c_im, d_skip, log_step, w_glu, b_glu):
    bsz, seq, _ = u.shape
    f32 = jnp.float32
    u32 = u.astype(f32)
    ug = u32.reshape(bsz, seq, SSM_GROUPS, SSM_GROUP)
    lr = lam_re.astype(f32)
    li = lam_im.astype(f32)
    step = jnp.exp(log_step.astype(f32))[:, None]
    mag = jnp.exp(lr * step)
    a_r = mag * jnp.cos(li * step)
    a_i = mag * jnp.sin(li * step)
    nr, ni = a_r - 1.0, a_i
    den = lr * lr + li * li
    kr = (nr * lr + ni * li) / den
    ki = (ni * lr - nr * li) / den
    bb_r, bb_i = cmul(kr[..., None], ki[..., None], b_re.astype(f32), b_im.astype(f32))
    bu_r = jnp.einsum('blgc,gpc->blgp', ug, bb_r)
    bu_i = jnp.einsum('blgc,gpc->blgp', ug, bb_i)
    a_r_seq = jnp.broadcast_to(a_r[None, None], (1, seq, SSM_GROUPS, SSM_STATE))
    a_i_seq = jnp.broadcast_to(a_i[None, None], (1, seq, SSM_GROUPS, SSM_STATE))

    def combine(e1, e2):
        a1r, a1i, b1r, b1i = e1
        a2r, a2i, b2r, b2i = e2
        ar_, ai_ = cmul(a2r, a2i, a1r, a1i)
        br_, bi_ = cmul(a2r, a2i, b1r, b1i)
        return ar_, ai_, br_ + b2r, bi_ + b2i

    _, _, h_r, h_i = lax.associative_scan(combine, (a_r_seq, a_i_seq, bu_r, bu_i), axis=1)
    y = (jnp.einsum('gcp,blgp->blgc', c_re.astype(f32), h_r)
         - jnp.einsum('gcp,blgp->blgc', c_im.astype(f32), h_i))
    y = y.reshape(bsz, seq, SSM_WIDTH) + d_skip.astype(f32) * u32
    y = jax.nn.gelu(y)
    y = y * jax.nn.sigmoid(y @ w_glu.astype(f32) + b_glu.astype(f32))
    return y.astype(u.dtype)

def rotary(t, pos):
    dk = t.shape[-1]
    inv_freq = ROPE_BASE ** (-jnp.arange(0, dk, 2, dtype=jnp.float32) / dk)
    ang = pos[:, None] * inv_freq[None, :]
    cos, sin = jnp.cos(ang), jnp.sin(ang)
    t1, t2 = t[..., : dk // 2], t[..., dk // 2:]
    return jnp.concatenate([t1 * cos - t2 * sin, t1 * sin + t2 * cos], axis=-1)

def retention_branch(q, k, v, g):
    bsz, seq, _ = q.shape
    f32 = jnp.float32
    n_chunks = seq // RET_CHUNK
    pos = jnp.arange(seq, dtype=f32)
    qh = q.astype(f32).reshape(bsz, seq, RET_HEADS, RET_DK).transpose(0, 2, 1, 3)
    kh = k.astype(f32).reshape(bsz, seq, RET_HEADS, RET_DK).transpose(0, 2, 1, 3)
    vh = v.astype(f32).reshape(bsz, seq, RET_HEADS, RET_DV).transpose(0, 2, 1, 3)
    qh = rotary(qh, pos)
    kh = rotary(kh, pos) * (RET_DK ** -0.5)
    qc = qh.reshape(bsz, RET_HEADS, n_chunks, RET_CHUNK, RET_DK)
    kc = kh.reshape(bsz, RET_HEADS, n_chunks, RET_CHUNK, RET_DK)
    vc = vh.reshape(bsz, RET_HEADS, n_chunks, RET_CHUNK, RET_DV)
    log_gamma = jnp.log(1.0 - 2.0 ** (-5.0 - jnp.arange(RET_HEADS, dtype=f32)))
    idx = jnp.arange(RET_CHUNK, dtype=f32)
    rel = idx[:, None] - idx[None, :]
    inner_decay = jnp.where(rel[None] >= 0,
                            jnp.exp(jnp.maximum(rel, 0.0)[None] * log_gamma[:, None, None]),
                            0.0)
    scores = jnp.einsum('bhncd,bhnsd->bhncs', qc, kc) * inner_decay[None, :, None]
    inner = jnp.einsum('bhncs,bhnse->bhnce', scores, vc)
    zeta = jnp.exp((RET_CHUNK - 1.0 - idx)[None, :] * log_gamma[:, None])
    kv = jnp.einsum('bhnsd,hs,bhnse->bhnde', kc, zeta, vc)
    chunk_decay = jnp.exp(RET_CHUNK * log_gamma)[None, :, None, None]

    def step(state, kv_i):
        return chunk_decay * state + kv_i, state

    _, r_prev = lax.scan(step, jnp.zeros((bsz, RET_HEADS, RET_DK, RET_DV), f32),
                         jnp.moveaxis(kv, 2, 0))
    r_prev = jnp.moveaxis(r_prev, 0, 2)
    xi = jnp.exp((idx + 1.0)[None, :] * log_gamma[:, None])
    cross = jnp.einsum('bhncd,hc,bhnde->bhnce', qc, xi, r_prev)
    o = (inner + cross).reshape(bsz, RET_HEADS, seq, RET_DV)
    o = o * lax.rsqrt(jnp.mean(o * o, axis=-1, keepdims=True) + EPS)
    o = o.transpose(0, 2, 1, 3).reshape(bsz, seq, RET_V_WIDTH)
    return (o * jax.nn.silu(g.astype(f32))).astype(q.dtype)

def setup_inputs(seed: int = 0) -> dict:
    key = jax.random.key(seed)
    ks = jax.random.split(key, 24)
    f32 = jnp.float32
    nrm = lambda k, shape, scale: jax.random.normal(k, shape, f32) * scale
    G, P, C = SSM_GROUPS, SSM_STATE, SSM_GROUP
    x = jax.random.normal(ks[0], (BATCH, SEQ, D_MODEL), f32)
    w_in = nrm(ks[1], (DEPTH, D_MODEL, IN_WIDTH), D_MODEL ** -0.5)
    lam_re = -0.5 + nrm(ks[2], (DEPTH, G, P), 0.01)
    lam_im = math.pi * jnp.broadcast_to(jnp.arange(P, dtype=f32), (DEPTH, G, P)) + nrm(ks[3], (DEPTH, G, P), 0.01)
    b_re = nrm(ks[4], (DEPTH, G, P, C), (2.0 * C) ** -0.5)
    b_im = nrm(ks[5], (DEPTH, G, P, C), (2.0 * C) ** -0.5)
    c_re = nrm(ks[6], (DEPTH, G, C, P), (2.0 * P) ** -0.5)
    c_im = nrm(ks[7], (DEPTH, G, C, P), (2.0 * P) ** -0.5)
    d_skip = nrm(ks[8], (DEPTH, SSM_WIDTH), 1.0)
    log_step = jax.random.uniform(ks[9], (DEPTH, G), f32, math.log(STEP_MIN), math.log(STEP_MAX))
    w_glu = nrm(ks[10], (DEPTH, SSM_WIDTH, SSM_WIDTH), SSM_WIDTH ** -0.5)
    b_glu = nrm(ks[11], (DEPTH, SSM_WIDTH), 0.01)
    w_proj_ssm = nrm(ks[12], (DEPTH, SSM_WIDTH, D_MODEL), SSM_WIDTH ** -0.5)
    w_proj_ret = nrm(ks[13], (DEPTH, RET_V_WIDTH, D_MODEL), RET_V_WIDTH ** -0.5)
    w_out = nrm(ks[14], (DEPTH, D_MODEL, D_MODEL), D_MODEL ** -0.5)
    norm_mix = 1.0 + nrm(ks[15], (DEPTH, D_MODEL), 0.02)
    norm_mlp = 1.0 + nrm(ks[16], (DEPTH, D_MODEL), 0.02)
    w_up = nrm(ks[17], (DEPTH, D_MODEL, D_FF), D_MODEL ** -0.5)
    w_down = nrm(ks[18], (DEPTH, D_FF, D_MODEL), D_FF ** -0.5)
    norm_final = 1.0 + nrm(ks[19], (D_MODEL,), 0.02)
    return {"x": x, "w_in": w_in, "lam_re": lam_re, "lam_im": lam_im,
            "b_re": b_re, "b_im": b_im, "c_re": c_re, "c_im": c_im,
            "d_skip": d_skip, "log_step": log_step, "w_glu": w_glu, "b_glu": b_glu,
            "w_proj_ssm": w_proj_ssm, "w_proj_ret": w_proj_ret, "w_out": w_out,
            "norm_mix": norm_mix, "norm_mlp": norm_mlp, "w_up": w_up, "w_down": w_down,
            "norm_final": norm_final}

def reference(x, w_in, lam_re, lam_im, b_re, b_im, c_re, c_im, d_skip, log_step,
              w_glu, b_glu, w_proj_ssm, w_proj_ret, w_out, norm_mix, norm_mlp,
              w_up, w_down, norm_final):
    h = x
    for l in range(DEPTH):
        z = rmsnorm(h, norm_mix[l])
        proj = z @ w_in[l]
        u, q, k, v, g, gate_a, gate_b = jnp.split(proj, IN_SPLITS, axis=-1)
        y_a = s5_branch(u, lam_re[l], lam_im[l], b_re[l], b_im[l], c_re[l], c_im[l],
                        d_skip[l], log_step[l], w_glu[l], b_glu[l])
        y_b = retention_branch(q, k, v, g)
        merged = (jax.nn.sigmoid(gate_a) * (y_a @ w_proj_ssm[l])
                  + jax.nn.sigmoid(gate_b) * (y_b @ w_proj_ret[l]))
        h = h + merged @ w_out[l]
        z = rmsnorm(h, norm_mlp[l])
        h = h + jnp.square(jax.nn.relu(z @ w_up[l])) @ w_down[l]
    return rmsnorm(h, norm_final)


_drawn_inputs = setup_inputs


def setup_inputs(seed=0):
    import zlib

    import numpy as np

    out = dict(_drawn_inputs(seed))
    spreads = {}
    factors = {'lam_re': 64.0,
     'lam_im': 37.744,
     'b_re': 52.496,
     'b_im': 53.168,
     'c_re': 53.048,
     'c_im': 53.04,
     'log_step': 38.336,
     'b_glu': 45.957,
     'norm_mix': 3.938,
     'norm_mlp': 3.286,
     'norm_final': 8.182}
    for name, (base, spread) in spreads.items():
        noise = np.random.default_rng([zlib.crc32(name.encode()), seed]).standard_normal(out[name].shape)
        drawn = base * np.exp(spread * noise) if base else spread * noise
        out[name] = __import__('jax').numpy.asarray(drawn.astype(out[name].dtype))
    for name, factor in factors.items():
        out[name] = (out[name] * factor).astype(out[name].dtype)
    return out
```

```python
from contextlib import ExitStack

import concourse.bass as bass
from concourse import mybir

F32 = mybir.dt.float32
F32R = mybir.dt.float32r
BF16 = mybir.dt.bfloat16
I32 = mybir.dt.int32
ALU = mybir.AluOpType
ACT = mybir.ActivationFunctionType

P = 128
SEQ = 1024
D = 1024
KT = D // P
NCH = SEQ // P
HALF = 512
FF = 4096
FB = 512
N_FB = FF // FB
SSM = 512
GROUPS, STATE, CH = 32, 64, 16
T = P // CH
NT = SEQ // T
MT = SSM // P
PAIRS = GROUPS // 2
QP = PAIRS // MT
GB = 2 * QP
SUP = NT // T
HEADS, DK, DV = 4, 128, 256
EPS = 1e-6

COL_Q = SSM
COL_K = COL_Q + HEADS * DK
COL_V = COL_K + HEADS * DK
COL_G = COL_V + HEADS * DV
COL_GATE = COL_G + HEADS * DV

LD_U, LD_GATE, LD_GLU, LD_PA, LD_RET, LD_PB, LD_OUT, LD_MLP = 0, 4, 20, 22, 26, 50, 58, 66
GR_U, GR_GATE, GR_GLU, GR_PA, GR_RET, GR_PB, GR_OUT, GR_MLP = 0, 1, 5, 6, 8, 16, 18, 20
OUT_U, OUT_GATE, OUT_GLU, OUT_PA, OUT_RET, OUT_PB, OUT_OUT, OUT_MLP = 0, 8, 40, 48, 64, 128, 144, 160
SP_Z, SP_Y, SP_YA, SP_YB, SP_M, SP_Z2, SP_HID = 0, 16, 20, 28, 36, 52, 68

LN2 = (0.693359375, -2.12194440e-4)
MAGIC = 12582912.0


def parts(value, n):
    import math
    out = []
    for _ in range(n):
        if value == 0.0:
            out.append(0.0)
            continue
        e = math.floor(math.log2(abs(value))) - 10
        q = round(value / 2.0 ** e) * 2.0 ** e
        out.append(q)
        value -= q
    return out


PER_BATCH = 51
PER_HEAD = 10 * NCH


class Chain:

    def __init__(self, eng, sem):
        self.eng, self.sem, self.n, self.off, self.mark = eng, sem, 0, 0, 0

    def link(self, ins):
        self.n += 1
        ins.then_inc(self.sem, 1)
        self.eng.wait_ge(self.sem, self.off + self.n)

    def enter(self, i, per):
        self.off, self.mark, self.per = i * per, self.n, per

    def leave(self, trips):
        assert self.n - self.mark == self.per, (self.n - self.mark, self.per)
        self.n += (trips - 1) * self.per
        self.off = 0


def build(nc, t):
    with ExitStack() as ctx:
        def sb(name, shape, dt=F32, where=ctx):
            return where.enter_context(nc.sbuf_tensor(name, shape, dt))

        def sem(name):
            return ctx.enter_context(nc.semaphore(name))

        ident = sb("ident", [P, P])
        rs_bits = sb("rs_bits", [P, 1], I32)
        rs_tmp = sb("rs_tmp", [P, 3])
        stage = sb("stage", [P, 2, 2 * HALF])
        w_hi = sb("w_hi", [P, 2, KT, HALF], F32R)
        w_lo = sb("w_lo", [P, 2, KT, HALF], F32R)
        with ExitStack() as r:
            z_hi = sb("z_hi", [P, KT, SEQ], F32R, r)
            z_lo = sb("z_lo", [P, KT, SEQ], F32R, r)
        with ExitStack() as r:
            h_res = sb("h_res", [P, NCH, D], F32, r)
            hid_hi = sb("hid_hi", [P, FB // P, SEQ], F32R, r)
            hid_lo = sb("hid_lo", [P, FB // P, SEQ], F32R, r)
        hold = sb("region1", [P, 2 * KT * SEQ])

        ph = ExitStack()
        bbr = sb("bbr", [P, PAIRS, CH], F32, ph)
        bbi = sb("bbi", [P, PAIRS, CH], F32, ph)
        ctr = sb("ctr", [P, PAIRS, CH], F32, ph)
        cti = sb("cti", [P, PAIRS, CH], F32, ph)
        pwr = sb("pwr", [P, T + 1, PAIRS], F32, ph)
        pwi = sb("pwi", [P, T + 1, PAIRS], F32, ph)
        rpr = sb("rpr", [P, T, PAIRS], F32, ph)
        rpi = sb("rpi", [P, T, PAIRS], F32, ph)
        p8r = sb("p8r", [P, T, PAIRS], F32, ph)
        p8i = sb("p8i", [P, T, PAIRS], F32, ph)
        p64r = sb("p64r", [P, 4, PAIRS], F32, ph)
        p64i = sb("p64i", [P, 4, PAIRS], F32, ph)
        dskip = sb("dskip", [P, MT], F32, ph)
        bglu = sb("bglu", [P, MT], F32, ph)
        y_raw = sb("y_raw", [P, MT, SEQ], F32, ph)
        with ExitStack() as r:
            x_in = sb("x_in", [P, 2, D], F32, r)
            z_tmp = sb("z_tmp", [P, 2, HALF], F32, r)
            x_junk = sb("x_junk", [P, D], BF16, r)
            ss1 = sb("ss1", [P, NCH], F32, r)
            rs1 = sb("rs1", [P, NCH, 2], F32, r)
            nmix = sb("nmix", [P, KT], F32, r)
            u_all = sb("u_all", [P, MT, T, NT], F32, r)
            c_raw = sb("c_raw", [P, 2, MT, P], F32, r)
            b_raw = sb("b_raw", [P, 2, PAIRS, CH], F32, r)
            coef = sb("coef", [P, 40, PAIRS], F32, r)
            ibits = sb("ibits", [P, 2, PAIRS], I32, r)
        with ExitStack() as r:
            u_blk = sb("u_blk", [P, GB, NT], F32, r)
            toep = sb("toep", [P, GB, P], F32, r)
            car = sb("car", [P, QP, T + 1, CH], F32, r)
            can = sb("can", [P, QP, T + 1, CH], F32, r)
            abr = sb("abr", [P, QP, T, CH], F32, r)
            abi = sb("abi", [P, QP, T, CH], F32, r)
            abt = sb("abt", [P, 2, QP, P], F32, r)
            hst = sb("hst", [P, 2, QP, NT + 1], F32, r)
            y_blk = sb("y_blk", [P, GB, NT], F32, r)
            u_back = sb("u_back", [P, SEQ], F32, r)
            ta = sb("ta", [P, SEQ], F32, r)
            tb = sb("tb", [P, SEQ], F32, r)
            gate_t = sb("gate_t", [P, 2, HALF], F32, r)
        with ExitStack() as r:
            y_hi = sb("y_hi", [P, MT, SEQ], F32R, r)
            y_lo = sb("y_lo", [P, MT, SEQ], F32R, r)
            glu_s = sb("glu_s", [P, MT, HALF], F32, r)
            ga_t = sb("ga_t", [P, 2, HALF], F32, r)
        ph.close()
        with ExitStack() as r:
            yb_raw = sb("yb_raw", [P, KT, SEQ], F32, r)
            rope = sb("rope", [P, NCH, P], F32, r)
            gam = sb("gam", [P, 3 * HEADS], F32, r)
            mask = sb("mask", [P, HEADS, P], F32, r)
            silu_g = sb("silu_g", [P, NCH, DV], F32, r)
            sig_t = sb("sig_t", [P, 2, DV], F32, r)
            qk = sb("qk", [P, 2, 2, DK], F32, r)
            vv = sb("vv", [P, 2, DV], F32, r)
            rot = sb("rot", [P, 2, 2, DK // 2], F32, r)
            rc = sb("rc", [P, 2, 2, DK // 2], F32, r)
            rsn = sb("rsn", [P, 2, 2, DK // 2], F32, r)
            kvk = sb("kvk", [P, 2, DK], F32, r)
            qkt = sb("qkt", [P, 2, P], F32, r)
            prob = sb("prob", [P, P], F32, r)
            state = sb("state", [P, DV], F32, r)
            yb = sb("yb", [P, DV], F32, r)
            o_junk = sb("o_junk", [P, DV], BF16, r)
            oss = sb("oss", [P, 2], F32, r)
            ors = sb("ors", [P, 2], F32, r)
        with ExitStack() as r:
            m_hi = sb("m_hi", [P, KT, SEQ], F32R, r)
            m_lo = sb("m_lo", [P, KT, SEQ], F32R, r)
            nmlp = sb("nmlp", [P, KT], F32, r)
            ss2 = sb("ss2", [P, NCH], F32, r)
            rs2 = sb("rs2", [P, NCH, 2], F32, r)
            with ExitStack() as q:
                gb_t = sb("gb_t", [P, 2, HALF], F32, q)
                ma_t = sb("ma_t", [P, HALF], F32, q)
            with ExitStack() as q:
                zb = sb("zb", [P, D], F32, q)
                z2_tmp = sb("z2_tmp", [P, HALF], F32, q)
            with ExitStack() as q:
                relu = sb("relu", [P, 2, HALF], F32, q)
        acc = ctx.enter_context(nc.psum_tensor("acc", [P, 4, HALF], F32))
        aux = ctx.enter_context(nc.psum_tensor("aux", [P, 4, HALF], F32))

        u_dram = nc.dram_tensor("u_dram", (MT, P, T, NT), F32, kind="Internal").ap()
        y_dram = nc.dram_tensor("y_dram", (MT, P, T, NT), F32, kind="Internal").ap()
        gate_dram = nc.dram_tensor("gate_dram", (2 * KT, P, SEQ), F32, kind="Internal").ap()
        ma_dram = nc.dram_tensor("ma_dram", (KT, P, SEQ), F32, kind="Internal").ap()
        out_rows = t["out"][0].rearrange("(c p) d -> p c d", p=P)
        x_rows = t["x"][0].rearrange("(c p) d -> p c d", p=P)

        const_in = sem("const_in")
        par_in = sem("par_in")
        ret_in = sem("ret_in")
        x_ready = [sem(f"x_ready{i}") for i in range(2)]
        raw = [sem(f"raw{i}") for i in range(2)]
        raw_qkv = [sem(f"raw_qkv{i}") for i in range(2)]
        hi_pool = sem("hi_pool")
        w_ready = sem("w_ready")
        out_ready = sem("out_ready")
        out_free = sem("out_free")
        hi_done = sem("hi_done")
        lo_done = sem("lo_done")
        chain_v = sem("chain_v")
        tick_pool = sem("tick_pool")
        tick_act = sem("tick_act")
        ss_done = sem("ss_done")
        z_scaled = sem("z_scaled")
        z_turned = sem("z_turned")
        z_normed = sem("z_normed")
        u_out = sem("u_out")
        ct_turned = sem("ct_turned")
        ct_ready = sem("ct_ready")
        zeroed = sem("zeroed")
        prep = sem("prep")
        ab_turned = sem("ab_turned")
        ab_ready = sem("ab_ready")
        kern = sem("kern")
        kern_ready = sem("kern_ready")
        toep_in = sem("toep_in")
        u_blk_in = sem("u_blk_in")
        x_state = sem("x_state")
        scanned = sem("scanned")
        y_prod = sem("y_prod")
        y_copied = sem("y_copied")
        y_sent = sem("y_sent")
        y_back = sem("y_back")
        gelu_arg = sem("gelu_arg")
        gelu_sig = sem("gelu_sig")
        y_done = sem("y_done")
        gate_sent = [sem(f"gate_sent{i}") for i in range(2)]
        glu_sig = sem("glu_sig")
        ga_in = [sem(f"ga_in{i}") for i in range(2)]
        ma_sent = [sem(f"ma_sent{i}") for i in range(2)]
        sig_g = sem("sig_g")
        rotated = sem("rotated")
        qk_turned = sem("qk_turned")
        qkt_ready = sem("qkt_ready")
        scores = sem("scores")
        prob_ready = sem("prob_ready")
        kv_ready = sem("kv_ready")
        state_ready = sem("state_ready")
        o_ready = sem("o_ready")
        o_ss = sem("o_ss")
        yb_ready = sem("yb_ready")
        yb_turned = sem("yb_turned")
        yb_stored = sem("yb_stored")
        nmlp_in = sem("nmlp_in")
        gb_in = [sem(f"gb_in{i}") for i in range(2)]
        ma_in = sem("ma_in")
        merged = sem("merged")
        xr_in = [sem(f"xr_in{i}") for i in range(NCH)]
        h_ss = sem("h_ss")
        z2_scaled = sem("z2_scaled")
        z2_turned = sem("z2_turned")
        z2_normed = sem("z2_normed")
        relu_made = sem("relu_made")
        squared = sem("squared")
        nf_in = sem("nf_in")
        f_ss = sem("f_ss")
        f_done = sem("f_done")
        stored = sem("stored")

        nf = stage[:, 0, :]

        block = ctx.enter_context(nc.Block())

        @block.sync
        def _(sp):
            def load(n, src, k=2, waits=None):
                s = n % 2 if waits is None else waits[1]
                if waits is not None:
                    sp.wait_ge(w_ready, waits[0])
                elif n >= 2:
                    sp.wait_ge(w_ready, n - 1)
                sp.dma_start(stage[:, s, :].rearrange("p (k c) -> p k c", k=k), src).then_inc(raw[s], 16)

            w_in = t["w_in"][0].rearrange("(k p) c -> p k c", p=P)

            sp.dma_start(ident[:], t["ident"]).then_inc(const_in, 16)
            sp.dma_start(nmix[:], t["norm_mix"].rearrange("a (k p) -> p (a k)", p=P), allow_slow_non_contiguous=True).then_inc(const_in, 16)
            for c in range(2):
                sp.dma_start(x_in[:, c, :], x_rows[:, c, :]).then_inc(x_ready[c], 16)
            for i in range(2):
                load(i, w_in[:, 2 * i:2 * i + 2, 0:HALF])
            for c in range(2, NCH):
                sp.wait_ge(z_turned, 2 * (c - 1))
                sp.dma_start(x_in[:, c % 2, :], x_rows[:, c, :]).then_inc(x_ready[c % 2], 16)
            for gp in range(2):
                rows = slice(gp * STATE, (gp + 1) * STATE)
                sp.dma_start(coef[rows, 0, :], t["lam_re"][0, gp::2, :].rearrange("g p -> p g"),
                             allow_slow_non_contiguous=True).then_inc(par_in, 16)
                sp.dma_start(coef[rows, 1, :], t["lam_im"][0, gp::2, :].rearrange("g p -> p g"),
                             allow_slow_non_contiguous=True).then_inc(par_in, 16)
                ls = t["log_step"]
                sp.dma_start(coef[rows, 2, :], bass.AP(tensor=ls.tensor, offset=gp, ap=[[0, STATE], [2, PAIRS]]),
                             allow_slow_non_contiguous=True).then_inc(par_in, 16)
                for ri, name in enumerate(("b_re", "b_im")):
                    sp.dma_start(b_raw[rows, ri, :, :], t[name][0, gp::2, :, :].rearrange("g p c -> p g c"))\
                      .then_inc(par_in, 16)
                for ri, name in enumerate(("c_re", "c_im")):
                    sp.dma_start(c_raw[:, ri, :, gp * STATE:(gp + 1) * STATE],
                                 t[name][0].rearrange("(m g) c p -> (g c) m p", m=MT)).then_inc(par_in, 16)
            sp.dma_start(dskip[:], t["d_skip"].rearrange("a (m p) -> p (a m)", p=P), allow_slow_non_contiguous=True).then_inc(par_in, 16)
            sp.dma_start(bglu[:], t["b_glu"].rearrange("a (m p) -> p (a m)", p=P), allow_slow_non_contiguous=True).then_inc(par_in, 16)
            for i in range(2, 4):
                load(i, w_in[:, 2 * i:2 * i + 2, 0:HALF])
            with sp.Fori(0, 2) as it:
                for b in range(2):
                    for i in range(4):
                        n = LD_GATE + 4 * b + i
                        load(n, w_in[:, 2 * i:2 * i + 2, bass.ds(COL_GATE + it * (2 * HALF) + b * HALF, HALF)],
                             waits=(it * 8 + (n - 1), n % 2))
            w_glu = t["w_glu"][0].rearrange("(k p) c -> p k c", p=P)
            for i in range(2):
                load(LD_GLU + i, w_glu[:, 2 * i:2 * i + 2, :])
            w_pa = t["w_proj_ssm"][0].rearrange("(k p) c -> p k c", p=P)
            for j in range(2):
                for i in range(2):
                    load(LD_PA + 2 * j + i, w_pa[:, 2 * i:2 * i + 2, j * HALF:(j + 1) * HALF])
            with sp.Fori(0, HEADS) as h:
                for i in range(2):
                    n = LD_RET + i
                    load(n, w_in[:, 4 * i:4 * i + 4, bass.ds(COL_G + h * DV, DV)], k=4,
                         waits=(h * 6 + (n - 1), n % 2))
                for i in range(4):
                    n = LD_RET + 2 + i
                    sp.wait_ge(w_ready, h * 6 + (n - 1))
                    dst = stage[:, n % 2, :].rearrange("p (k c) -> p k c", k=2)
                    for d0, c0, w in ((0, COL_Q, DK), (DK, COL_K, DK), (2 * DK, COL_V, DV)):
                        sp.dma_start(dst[:, :, d0:d0 + w], w_in[:, 2 * i:2 * i + 2, bass.ds(c0 + h * w, w)])\
                          .then_inc(raw_qkv[n % 2], 16)
            w_pb = t["w_proj_ret"][0].rearrange("(k p) c -> p k c", p=P)
            w_o = t["w_out"][0].rearrange("(k p) c -> p k c", p=P)
            for base, w in ((LD_PB, w_pb), (LD_OUT, w_o)):
                for j in range(2):
                    for i in range(4):
                        load(base + 4 * j + i, w[:, 2 * i:2 * i + 2, j * HALF:(j + 1) * HALF])
            w_up = t["w_up"][0].rearrange("(k p) c -> p k c", p=P)
            w_dn = t["w_down"][0].rearrange("(k p) c -> p k c", p=P)
            with sp.Fori(0, N_FB) as f:
                for i in range(4):
                    n = LD_MLP + i
                    load(n, w_up[:, 2 * i:2 * i + 2, bass.ds(f * FB, FB)], waits=(f * 8 + (n - 1), n % 2))
                for i in range(4):
                    n = LD_MLP + 4 + i
                    load(n, w_dn[:, bass.ds(f * (FB // P) + i, 1), :], k=1, waits=(f * 8 + (n - 1), n % 2))
            sp.wait_ge(w_ready, LD_MLP + 8 * N_FB)
            nfin = t["norm_final"]
            sp.dma_start(nf, bass.AP(tensor=nfin.tensor, offset=0, ap=[[0, P], [1, D]])).then_inc(nf_in, 16)
            for c in range(NCH):
                sp.wait_ge(f_done, c + 1)
                sp.dma_start(out_rows[:, c, :], h_res[:, c, :]).then_inc(stored, 16)
            sp.wait_ge(stored, 16 * NCH)

        @block.gpsimd
        def _(pool):
            def split(ready, count, s, slot, u0, n_done, freed=None):
                if freed is not None:
                    pool.wait_ge(out_ready, freed)
                pool.wait_ge(ready, count)
                if not isinstance(n_done, int):
                    pool.sem_inc(tick_pool, 1)
                dst_hi = w_hi[:, slot, u0:u0 + 2, :].rearrange("p k c -> p (k c)")
                dst_lo = w_lo[:, slot, u0:u0 + 2, :].rearrange("p k c -> p (k c)")
                nc.gpsimd.tensor_copy(dst_hi, stage[:, s, :]).then_inc(hi_pool, 1)
                pool.wait_ge(hi_pool, n_done)
                nc.gpsimd.tensor_tensor(dst_lo, stage[:, s, :], dst_hi.bitcast(F32), ALU.subtract)\
                  .then_inc(w_ready, 1)

            def regular(n, gr, i, seen, freed):
                split(raw[n % 2], 16 * (seen + 1), n % 2, gr % 2, 2 * i, n + 1, freed=freed if i == 0 else None)

            for i in range(4):
                regular(LD_U + i, GR_U, i, i // 2, None)
            with pool.Fori(0, 2) as it:
                for b in range(2):
                    for i in range(4):
                        n = LD_GATE + 4 * b + i
                        freed = (it * 15 + 1, it * 16 + OUT_GATE)[b]
                        split(raw[n % 2], it * 64 + 16 * (n // 2 + 1), n % 2, (GR_GATE + b) % 2, 2 * i, it * 8 + (n + 1),
                              freed=freed if i == 0 else None)
            for i in range(2):
                regular(LD_GLU + i, GR_GLU, i, (LD_GLU + i) // 2, OUT_GLU - 8)
            for j in range(2):
                for i in range(2):
                    n = LD_PA + 2 * j + i
                    regular(n, GR_PA + j, i, n // 2, OUT_GLU + 8 * j)
            with pool.Fori(0, HEADS) as h:
                for i in range(2):
                    n = LD_RET + i
                    split(raw[n % 2], h * 16 + 16 * (LD_RET // 2 + 1), n % 2, GR_RET % 2, 2 * i, h * 6 + (n + 1),
                          freed=h * 16 + (OUT_RET - 8) if i == 0 else None)
                for i in range(4):
                    n = LD_RET + 2 + i
                    split(raw_qkv[n % 2], h * 96 + 48 * (i // 2 + 1), n % 2, (GR_RET + 1) % 2, 2 * i, h * 6 + (n + 1),
                          freed=h * 16 + OUT_RET if i == 0 else None)
            g_slot = LD_RET // 2 + HEADS
            for base, gr in ((LD_PB, GR_PB), (LD_OUT, GR_OUT)):
                for j in range(2):
                    for i in range(4):
                        n = base + 4 * j + i
                        regular(n, gr + j, i, g_slot + (n - LD_PB) // 2, OUT_PB + 8 * (gr + j - GR_PB) - 8)
            with pool.Fori(0, N_FB) as f:
                for b in range(2):
                    for i in range(4):
                        n = LD_MLP + 4 * b + i
                        split(raw[n % 2], f * 64 + 16 * (g_slot + (n - LD_PB) // 2 + 1), n % 2, (GR_MLP + b) % 2,
                              2 * i, f * 8 + (n + 1), freed=f * 24 + (OUT_MLP - 8 + 8 * b) if i == 0 else None)

        @block.tensor
        def _(pe):
            def three(out, s_hi, s_lo, m_hi_, m_lo_, first, last):
                nc.tensor.matmul(out, s_hi, m_hi_, start=first, stop=False)
                nc.tensor.matmul(out, s_hi, m_lo_, start=False, stop=False)
                return nc.tensor.matmul(out, s_lo, m_hi_, start=False, stop=last)

            def wait_bank(n):
                pe.wait_ge(out_free, n - 3)

            def features(n, slot, units, col, a_hi, a_lo, half, w_wait=None):
                if n >= 4:
                    wait_bank(n)
                for k in range(units):
                    if w_wait is not None and k % 2 == 0:
                        pe.wait_ge(w_ready, w_wait + k // 2)
                    mm = three(acc[:, n % 4, :], w_hi[:, slot, k, col:col + P], w_lo[:, slot, k, col:col + P],
                               a_hi[:, k, half * HALF:(half + 1) * HALF], a_lo[:, k, half * HALF:(half + 1) * HALF],
                               k == 0, k == units - 1)
                mm.then_inc(out_ready, 1)
                return mm

            pe.wait_ge(const_in, 32)
            for c in range(NCH):
                for b in range(2):
                    if b == 0:
                        pe.wait_ge(z_scaled, c + 1)
                    n = 2 * c + b
                    if n >= 4:
                        pe.wait_ge(z_normed, n - 3)
                    for q in range(4):
                        k = 4 * b + q
                        mm = nc.tensor.transpose(aux[:, n % 4, q * P:(q + 1) * P], x_in[:, c % 2, k * P:(k + 1) * P],
                                                 ident[:])
                    mm.then_inc(z_turned, 1)

            for half in range(2):
                for m in range(MT):
                    n = OUT_U + half * MT + m
                    if m == 0:
                        pe.wait_ge(lo_done, SP_Z + 8 * (half + 1))
                    features(n, GR_U % 2, KT, m * P, z_hi, z_lo, half, w_wait=LD_U + 1 if n == 0 else None)

            pe.wait_ge(par_in, 16 * 16)
            pe.wait_ge(z_normed, 2 * NCH)
            for ri in range(2):
                for m in range(MT):
                    mm = nc.tensor.transpose(aux[:, ri, m * P:(m + 1) * P], c_raw[:, ri, m, :], ident[:])
            mm.then_inc(ct_turned, 1)

            with pe.Fori(0, 2) as it:
                for b in range(2):
                    def gate(o):
                        d, half = o // 2, o % 2
                        n = OUT_GATE + 8 * b + o
                        slot = (GR_GATE + b) % 2
                        pe.wait_ge(out_free, it * 16 + (n - 3))
                        for k in range(KT):
                            if o == 0 and k % 2 == 0:
                                pe.wait_ge(w_ready, it * 8 + (LD_GATE + 4 * b + k // 2 + 1))
                            mm = three(acc[:, n % 4, :], w_hi[:, slot, k, d * P:(d + 1) * P],
                                       w_lo[:, slot, k, d * P:(d + 1) * P],
                                       z_hi[:, k, half * HALF:(half + 1) * HALF],
                                       z_lo[:, k, half * HALF:(half + 1) * HALF], k == 0, k == KT - 1)
                        mm.then_inc(out_ready, 1)

                    def done(x):
                        return it * 2 + (b + x)

                    gate(0)
                    gate(1)
                    pe.wait_ge(prep, done(1))
                    pe.wait_ge(ct_ready, 1)
                    for ri, src in enumerate((abr, abi)):
                        for q in range(QP):
                            mm = nc.tensor.transpose(aux[:, ri, q * P:(q + 1) * P],
                                                     src[:, q, :, :].rearrange("p t c -> p (t c)"), ident[:])
                    mm.then_inc(ab_turned, 1)
                    for g in range(GB):
                        q, gp = g // 2, g % 2
                        rows = slice(gp * STATE, (gp + 1) * STATE)
                        out = aux[0:CH, 2 + gp, q * P:(q + 1) * P]
                        nc.tensor.matmul(out, abr[rows, q, T - 1, :],
                                         car[rows, q, 0:T, :].rearrange("p t c -> p (t c)"), start=True, stop=False)
                        mm = nc.tensor.matmul(out, abi[rows, q, T - 1, :],
                                              can[rows, q, 0:T, :].rearrange("p t c -> p (t c)"),
                                              start=False, stop=True)
                    mm.then_inc(kern, 1)
                    gate(2)
                    pe.wait_ge(ab_ready, done(1))
                    pe.wait_ge(u_blk_in, it * 256 + 128 * (b + 1))
                    for g in range(GB):
                        q, gp = g // 2, g % 2
                        for ri in range(2):
                            mm = nc.tensor.matmul(aux[gp * STATE:(gp + 1) * STATE, ri, q * P:(q + 1) * P],
                                                  abt[:, ri, q, gp * STATE:(gp + 1) * STATE], u_blk[:, g, :],
                                                  start=True, stop=True)
                    mm.then_inc(x_state, 1)
                    for o in range(3, 7):
                        gate(o)
                    pe.wait_ge(scanned, done(1))
                    pe.wait_ge(toep_in, it * 224 + 112 * (b + 1))
                    for g in range(GB):
                        q, gp = g // 2, g % 2
                        rows = slice(gp * STATE, (gp + 1) * STATE)
                        out = aux[:, 2 + gp, q * P:(q + 1) * P]
                        nc.tensor.matmul(out, toep[:, gp * QP + q, :], u_blk[:, g, :], start=True, stop=False)
                        nc.tensor.matmul(out, car[rows, q, 1:T + 1, :].rearrange("p t c -> p (t c)"),
                                         hst[rows, 0, q, 0:NT], start=False, stop=False)
                        mm = nc.tensor.matmul(out, can[rows, q, 1:T + 1, :].rearrange("p t c -> p (t c)"),
                                              hst[rows, 1, q, 0:NT], start=False, stop=True)
                    mm.then_inc(y_prod, 1)
                    gate(7)

            for half in range(2):
                for m in range(MT):
                    n = OUT_GLU + half * MT + m
                    if n == OUT_GLU:
                        pe.wait_ge(lo_done, SP_Y + MT)
                    features(n, GR_GLU % 2, MT, m * P, y_hi, y_lo, half, w_wait=LD_GLU + 1 if n == OUT_GLU else None)
            for j in range(2):
                for half in range(2):
                    for d in range(4):
                        n = OUT_PA + 8 * j + 4 * half + d
                        if j == 0 and d == 0:
                            pe.wait_ge(lo_done, SP_YA + 4 * (half + 1))
                        features(n, (GR_PA + j) % 2, MT, d * P, y_hi, y_lo, half,
                                 w_wait=LD_PA + 2 * j + 1 if half == 0 and d == 0 else None)

            pe.wait_ge(ret_in, 48)
            sg, sq = GR_RET % 2, (GR_RET + 1) % 2
            wg_hi = w_hi[:, sg, 0:4, :].rearrange("p u (a c) -> p (u a) c", a=2)
            wg_lo = w_lo[:, sg, 0:4, :].rearrange("p u (a c) -> p (u a) c", a=2)

            def g_part(h, c, k):
                n = OUT_RET + c
                if k == 0:
                    pe.wait_ge(out_free, h * 16 + (n - 3))
                if c == 0 and k % 4 == 0:
                    pe.wait_ge(w_ready, h * 6 + (LD_RET + k // 4 + 1))
                mm = three(acc[:, n % 4, 0:DV], z_hi[:, k, c * P:(c + 1) * P], z_lo[:, k, c * P:(c + 1) * P],
                           wg_hi[:, k, :], wg_lo[:, k, :], k == 0, k == KT - 1)
                if k == KT - 1:
                    mm.then_inc(out_ready, 1)

            def qkv_part(h, c, k):
                n = OUT_RET + NCH + c
                if k == 0:
                    pe.wait_ge(out_free, h * 16 + (n - 3))
                if c == 0 and k % 2 == 0:
                    pe.wait_ge(w_ready, h * 6 + (LD_RET + 2 + k // 2 + 1))
                mm = three(acc[:, n % 4, :], z_hi[:, k, c * P:(c + 1) * P], z_lo[:, k, c * P:(c + 1) * P],
                           w_hi[:, sq, k, :], w_lo[:, sq, k, :], k == 0, k == KT - 1)
                if k == KT - 1:
                    mm.then_inc(out_ready, 1)

            def head(h, more):
                def cnt(c):
                    return h * 8 + (c + 1)

                def turn_qk(c):
                    pe.wait_ge(rotated, cnt(c))
                    if c >= 2:
                        pe.wait_ge(yb_stored, cnt(c - 2))
                    nc.tensor.transpose(aux[:, 0, 0:P], rot[:, 0, :, :].rearrange("p a b -> p (a b)"), ident[:])
                    nc.tensor.transpose(aux[:, 0, P:2 * P], kvk[:, c % 2, :], ident[:]).then_inc(qk_turned, 1)

                def score(c):
                    pe.wait_ge(qkt_ready, cnt(c))
                    nc.tensor.matmul(aux[:, 1, 0:P], qkt[:, 1, :], qkt[:, 0, :], start=True, stop=True)\
                      .then_inc(scores, 1)
                    if c >= 1:
                        pe.wait_ge(state_ready, cnt(c - 1))
                    nc.tensor.matmul(aux[:, 3, 0:DV], kvk[:, c % 2, :], vv[:, c % 2, :], start=True, stop=True)\
                      .then_inc(kv_ready, 1)

                def attend(c):
                    pe.wait_ge(prob_ready, cnt(c))
                    if c >= 1:
                        pe.wait_ge(yb_ready, cnt(c - 1))
                    mm = nc.tensor.matmul(aux[:, 2, 0:DV], prob[:], vv[:, c % 2, :], start=True, stop=(c == 0))
                    if c >= 1:
                        mm = nc.tensor.matmul(aux[:, 2, 0:DV], qkt[:, 0, :], state[:], start=False, stop=True)
                    mm.then_inc(o_ready, 1)

                def turn_yb(c):
                    pe.wait_ge(yb_ready, cnt(c))
                    for e in range(2):
                        mm = nc.tensor.transpose(aux[:, 0, e * P:(e + 1) * P], yb[:, e * P:(e + 1) * P], ident[:])
                    mm.then_inc(yb_turned, 1)

                for s in range(NCH + 3):
                    for k in range(KT):
                        if s < NCH:
                            qkv_part(h, s, k)
                        elif more:
                            for i in (2 * k, 2 * k + 1):
                                c = 2 * (s - NCH) + i // KT
                                g_part(h + 1, c, i % KT)
                        if k == 0 and s >= 3:
                            turn_yb(s - 3)
                        if k == 1 and 2 <= s <= NCH + 1:
                            attend(s - 2)
                        if k == 4 and 1 <= s <= NCH:
                            turn_qk(s - 1)
                        if k == 6 and 1 <= s <= NCH:
                            score(s - 1)
                if more:
                    for c in (6, 7):
                        for k in range(KT):
                            g_part(h + 1, c, k)

            for c in range(NCH):
                for k in range(KT):
                    g_part(0, c, k)
            with pe.Fori(0, HEADS - 1) as h:
                head(h, True)
            head(HEADS - 1, False)

            for j in range(2):
                for d in range(4):
                    for half in range(2):
                        n = OUT_PB + 8 * j + 2 * d + half
                        slot = (GR_PB + j) % 2
                        wait_bank(n)
                        for k in range(KT):
                            if n == OUT_PB:
                                pe.wait_ge(lo_done, SP_YB + k + 1)
                            if d == 0 and half == 0 and k % 2 == 0:
                                pe.wait_ge(w_ready, LD_PB + 4 * j + k // 2 + 1)
                            mm = three(acc[:, n % 4, :], w_hi[:, slot, k, d * P:(d + 1) * P],
                                       w_lo[:, slot, k, d * P:(d + 1) * P], z_hi[:, k, half * HALF:(half + 1) * HALF],
                                       z_lo[:, k, half * HALF:(half + 1) * HALF], k == 0, k == KT - 1)
                        mm.then_inc(out_ready, 1)

            def turn_z2(c):
                pe.wait_ge(z2_scaled, c + 1)
                for b in range(2):
                    n = 2 * c + b
                    if n >= 4:
                        pe.wait_ge(z2_normed, n - 3)
                    for q in range(4):
                        k = 4 * b + q
                        mm = nc.tensor.transpose(aux[:, n % 4, q * P:(q + 1) * P], zb[:, k * P:(k + 1) * P], ident[:])
                    mm.then_inc(z2_turned, 1)

            for j in range(2):
                for c in range(NCH):
                    n = OUT_OUT + 8 * j + c
                    slot = (GR_OUT + j) % 2
                    wait_bank(n)
                    for k in range(KT):
                        if j == 0 and c == 0:
                            pe.wait_ge(lo_done, SP_M + 2 * k + 2)
                        if c == 0 and k % 2 == 0:
                            pe.wait_ge(w_ready, LD_OUT + 4 * j + k // 2 + 1)
                        mm = three(acc[:, n % 4, :], m_hi[:, k, c * P:(c + 1) * P], m_lo[:, k, c * P:(c + 1) * P],
                                   w_hi[:, slot, k, :], w_lo[:, slot, k, :], k == 0, k == KT - 1)
                    mm.then_inc(out_ready, 1)
                    if j == 1 and c >= 1:
                        turn_z2(c - 1)
            turn_z2(NCH - 1)

            with pe.Fori(0, N_FB) as f:
                pe.wait_ge(lo_done, SP_Z2 + 8)
                for half in range(2):
                    for q in range(FB // P):
                        n = OUT_MLP + 4 * half + q
                        slot = GR_MLP % 2
                        if half == 1 and q == 0:
                            pe.wait_ge(lo_done, SP_Z2 + 16)
                        pe.wait_ge(out_free, f * 24 + (n - 3))
                        for k in range(KT):
                            if half == 0 and q == 0 and k % 2 == 0:
                                pe.wait_ge(w_ready, f * 8 + (LD_MLP + k // 2 + 1))
                            mm = three(acc[:, n % 4, :], w_hi[:, slot, k, q * P:(q + 1) * P],
                                       w_lo[:, slot, k, q * P:(q + 1) * P], m_hi[:, k, half * HALF:(half + 1) * HALF],
                                       m_lo[:, k, half * HALF:(half + 1) * HALF], k == 0, k == KT - 1)
                        mm.then_inc(out_ready, 1)
                for j in range(2):
                    for c in range(NCH):
                        n = OUT_MLP + 8 + 8 * j + c
                        slot = (GR_MLP + 1) % 2
                        pe.wait_ge(out_free, f * 24 + (n - 3))
                        if j == 0 and c % 4 == 0:
                            pe.wait_ge(lo_done, f * 8 + (SP_HID + c + 4))
                        for q in range(FB // P):
                            if j == 0 and c == 0:
                                pe.wait_ge(w_ready, f * 8 + (LD_MLP + 4 + q + 1))
                            mm = three(acc[:, n % 4, :], hid_hi[:, q, c * P:(c + 1) * P],
                                       hid_lo[:, q, c * P:(c + 1) * P], w_hi[:, slot, 2 * q + j, :],
                                       w_lo[:, slot, 2 * q + j, :], q == 0, q == FB // P - 1)
                        mm.then_inc(out_ready, 1)

        @block.scalar
        def _(act):
            def hi_split(dst, src):
                nc.scalar.activation(dst, src, ACT.Copy).then_inc(hi_done, 1)

            for c in range(NCH):
                act.wait_ge(x_ready[c % 2], 16 * (c // 2 + 1))
                if c >= 1:
                    act.wait_ge(ss_done, c)
                nc.scalar.activation(x_junk[:], x_in[:, c % 2, :], ACT.Square, accum_out=ss1[:, c:c + 1])\
                  .then_inc(ss_done, 1)
                if c >= 1:
                    for b in range(2):
                        n = 2 * (c - 1) + b
                        act.wait_ge(z_normed, n + 1)
                        hi_split(z_hi[:, 4 * b:4 * b + 4, (c - 1) * P:c * P],
                                 z_tmp[:, n % 2, :].rearrange("p (k s) -> p k s", k=4))
            for b in range(2):
                n = 2 * (NCH - 1) + b
                act.wait_ge(z_normed, n + 1)
                hi_split(z_hi[:, 4 * b:4 * b + 4, (NCH - 1) * P:NCH * P],
                         z_tmp[:, n % 2, :].rearrange("p (k s) -> p k s", k=4))
            for n in range(8):
                half, m = n // MT, n % MT
                act.wait_ge(out_ready, OUT_U + n + 1)
                w = NT // 2
                ch_ins = nc.scalar.activation(u_all[:, m, :, half * w:(half + 1) * w],
                                              acc[:, n % 4, :].rearrange("p (c j) -> p j c", j=T), ACT.Copy)
                ch_ins.then_inc(out_free, 1)
                if half == 1:
                    act.wait_ge(out_free, OUT_U + n + 1)
                    act.dma_start(u_dram[m], u_all[:, m, :, :]).then_inc(u_out, 16)
            act.wait_ge(ct_turned, 1)
            for ri, dst in enumerate((ctr, cti)):
                for gp in range(2):
                    rows = slice(gp * STATE, (gp + 1) * STATE)
                    src = aux[rows, ri, :].rearrange("p (m q e c) -> p m q e c", q=QP, e=2, c=CH)[:, :, :, gp, :]
                    ins = nc.scalar.activation(dst[rows, :, :].rearrange("p (m q) c -> p m q c", m=MT), src, ACT.Copy)
                    ins.then_inc(ct_ready, 1) if ri == 1 and gp == 1 else None
            act.wait_ge(u_out, 16 * MT)
            with act.Fori(0, 2) as it:
                for b in range(2):
                    def done(x):
                        return it * 2 + (b + x)

                    def gate(o):
                        d, half = o // 2, o % 2
                        n = 8 * b + o
                        act.wait_ge(out_ready, it * 16 + (OUT_GATE + n + 1))
                        if n >= 2:
                            act.wait_ge(gate_sent[o % 2], it * 128 + 16 * (n // 2))
                        nc.scalar.activation(gate_t[:, o % 2, :], acc[:, n % 4, :], ACT.Sigmoid).then_inc(out_free, 1)
                        act.wait_ge(out_free, it * 16 + (OUT_GATE + n + 1))
                        row = it * 8 + (4 * b + d)
                        act.dma_start(gate_dram[bass.ds(row, 1), :, half * HALF:(half + 1) * HALF]
                                      .rearrange("a p s -> p (a s)"), gate_t[:, o % 2, :]).then_inc(gate_sent[o % 2], 16)

                    mt = it * 2 + b
                    act.wait_ge(prep, done(1))
                    for j in range(T):
                        act.dma_start(u_blk[j * CH:(j + 1) * CH, :, :],
                                      u_dram[bass.ds(mt, 1), :, j, :].rearrange("a (g c) n -> (a c) g n", c=CH))\
                           .then_inc(u_blk_in, 16)
                    act.dma_start(u_back[:], u_dram[bass.ds(mt, 1)].rearrange("a p j n -> (a p) (j n)"))\
                       .then_inc(y_back, 16)
                    gate(0)
                    gate(1)
                    act.wait_ge(ab_turned, done(1))
                    nc.scalar.activation(abt[:].rearrange("p r q s -> p r (q s)"), aux[:, 0:2, :], ACT.Copy)\
                      .then_inc(ab_ready, 1)
                    act.wait_ge(kern, done(1))
                    nc.scalar.activation(toep[0:CH, :, :].rearrange("p (b g) s -> p b (g s)", b=2),
                                         aux[0:CH, 2:4, :], ACT.Copy).then_inc(kern_ready, 1)
                    act.wait_ge(kern_ready, done(1))
                    for j in range(1, T):
                        act.dma_start(toep[j * CH:(j + 1) * CH, :, j * CH:P], toep[0:CH, :, 0:P - j * CH])\
                           .then_inc(toep_in, 16)
                    for o in range(2, 7):
                        gate(o)
                    act.wait_ge(y_prod, done(1))
                    nc.scalar.activation(y_blk[:].rearrange("p (q e) s -> p e q s", e=2),
                                         aux[:, 2:4, :].rearrange("p e (q s) -> p e q s", q=QP), ACT.Copy)\
                      .then_inc(y_copied, 1)
                    act.wait_ge(y_copied, done(1))
                    for j in range(T):
                        act.dma_start(y_dram[bass.ds(mt, 1), :, j, :].rearrange("a (g c) n -> (a c) g n", c=CH),
                                      y_blk[j * CH:(j + 1) * CH, :, :]).then_inc(y_sent, 16)
                    gate(7)
                    act.wait_ge(y_sent, it * 256 + 128 * (b + 1))
                    act.dma_start(y_blk[:].rearrange("p g s -> p (g s)"),
                                  y_dram[bass.ds(mt, 1)].rearrange("a p j n -> (a p) (j n)")).then_inc(y_back, 16)
                    act.wait_ge(gelu_arg, done(1))
                    nc.scalar.activation(tb[:], ta[:], ACT.Sigmoid, scale=1.5957691216057308).then_inc(gelu_sig, 1)
                for s in range(2):
                    act.wait_ge(gate_sent[s], it * 128 + 128)
            act.wait_ge(y_done, MT)
            for m in range(MT):
                hi_split(y_hi[:, m, :], y_raw[:, m, :])
            for half in range(2):
                for m in range(MT):
                    n = half * MT + m
                    act.wait_ge(out_ready, OUT_GLU + n + 1)
                    if half == 1:
                        act.wait_ge(out_free, OUT_GLU + m + 1)
                    nc.scalar.activation(glu_s[:, m, :], acc[:, n % 4, :], ACT.Sigmoid, bias=bglu[:, m:m + 1])\
                      .then_inc(glu_sig, 1)
                act.wait_ge(out_ready, OUT_GLU + MT * (half + 1))
                for m in range(MT):
                    n = half * MT + m
                    act.wait_ge(out_free, OUT_GLU + n + 1)
                    hi_split(y_hi[:, m, half * HALF:(half + 1) * HALF], y_raw[:, m, half * HALF:(half + 1) * HALF])
            order = [(j, half, d) for j in range(2) for half in range(2) for d in range(4)]

            def load_ga(n):
                j, half, d = order[n]
                act.dma_start(ga_t[:, n % 2, :], gate_dram[4 * j + d, :, half * HALF:(half + 1) * HALF])\
                   .then_inc(ga_in[n % 2], 16)

            load_ga(0)
            load_ga(1)
            for n, (j, half, d) in enumerate(order):
                act.wait_ge(out_free, OUT_PA + n + 1)
                act.dma_start(ma_dram[4 * j + d, :, half * HALF:(half + 1) * HALF], ga_t[:, n % 2, :])\
                   .then_inc(ma_sent[n % 2], 16)
                if n + 2 < len(order):
                    act.wait_ge(ma_sent[n % 2], 16 * (n // 2 + 1))
                    load_ga(n + 2)
            for s in range(2):
                act.wait_ge(ma_sent[s], 16 * len(order) // 2)
            act.wait_ge(lo_done, SP_YA + 8)
            act.wait_ge(out_ready, OUT_PA + 16)
            act.dma_start(rope[:], t["rope"].rearrange("(c p) f -> p c f", p=P)).then_inc(ret_in, 16)
            act.dma_start(gam[:], t["gam"]).then_inc(ret_in, 16)
            act.dma_start(mask[:], t["mask"]).then_inc(ret_in, 16)
            act.wait_ge(ret_in, 48)

            def g_sigmoid(h, c):
                n = OUT_RET + c
                act.wait_ge(out_ready, h * 16 + (n + 1))
                act.wait_ge(out_free, h * 16 + (n - 1))
                nc.scalar.activation(sig_t[:, c % 2, :], acc[:, n % 4, 0:DV], ACT.Sigmoid).then_inc(sig_g, 1)

            def head(h, more):
                def cnt(c):
                    return h * 8 + (c + 1)

                def take_qkv(c):
                    n = OUT_RET + NCH + c
                    act.wait_ge(out_ready, h * 16 + (n + 1))
                    act.sem_inc(tick_act, 1)
                    nc.scalar.activation(qk[:, c % 2, 0, :], acc[:, n % 4, 0:DK], ACT.Copy,
                                         scale=gam[:, bass.ds(h, 1)])
                    nc.scalar.activation(qk[:, c % 2, 1, :], acc[:, n % 4, DK:2 * DK], ACT.Copy,
                                         scale=gam[:, bass.ds(h + HEADS, 1)])
                    nc.scalar.activation(vv[:, c % 2, :], acc[:, n % 4, 2 * DK:], ACT.Copy).then_inc(out_free, 1)

                def take_yb(c):
                    act.wait_ge(yb_turned, cnt(c))
                    act.sem_inc(tick_act, 1)
                    nc.scalar.activation(yb_raw[:, bass.ds(h * 2, 2), c * P:(c + 1) * P],
                                         aux[:, 0, 0:2 * P].rearrange("p (e s) -> p e s", e=2), ACT.Copy)\
                      .then_inc(yb_stored, 1)

                def square_o(c):
                    act.wait_ge(o_ready, cnt(c))
                    nc.scalar.activation(o_junk[:], aux[:, 2, 0:DV], ACT.Square, accum_out=oss[:, c % 2:c % 2 + 1])\
                      .then_inc(o_ss, 1)

                def take_qkt(c):
                    act.wait_ge(qk_turned, cnt(c))
                    nc.scalar.activation(qkt[:].rearrange("p a s -> p (a s)"), aux[:, 0, 0:2 * P], ACT.Copy)\
                      .then_inc(qkt_ready, 1)

                act.wait_ge(out_free, h * 16 + (OUT_RET + NCH))
                for s in range(1, NCH + 4):
                    if s <= NCH:
                        take_qkv(s - 1)
                    if s >= 3 and s - 3 < NCH:
                        take_yb(s - 3)
                    if 2 <= s <= NCH + 1:
                        square_o(s - 2)
                    if more and s >= NCH and s < NCH + 3:
                        g_sigmoid(h + 1, 2 * (s - NCH))
                    if s <= NCH:
                        take_qkt(s - 1)
                    if more and s >= NCH:
                        for c in ((2 * (s - NCH) + 1,) if s < NCH + 3 else (6, 7)):
                            g_sigmoid(h + 1, c)

            for c in range(NCH):
                g_sigmoid(0, c)
            with act.Fori(0, HEADS - 1) as h:
                head(h, True)
            head(HEADS - 1, False)
            act.wait_ge(out_ready, OUT_PB)
            act.wait_ge(yb_stored, NCH * HEADS)
            for k in range(KT):
                hi_split(z_hi[:, k, :], yb_raw[:, k, :])
            act.wait_ge(lo_done, SP_YB + KT)
            act.dma_start(nmlp[:], t["norm_mlp"].rearrange("a (k p) -> p (a k)", p=P), allow_slow_non_contiguous=True).then_inc(nmlp_in, 16)

            def block_of(n):
                return n // 2, n % 2

            def load_gb(n):
                d, half = block_of(n)
                act.dma_start(gb_t[:, n % 2, :], gate_dram[KT + d, :, half * HALF:(half + 1) * HALF])\
                   .then_inc(gb_in[n % 2], 16)

            def load_ma(n):
                d, half = block_of(n)
                act.dma_start(ma_t[:], ma_dram[d, :, half * HALF:(half + 1) * HALF]).then_inc(ma_in, 16)

            load_gb(0)
            load_gb(1)
            load_ma(0)
            for n in range(16):
                d, half = block_of(n)
                act.wait_ge(merged, n + 1)
                if n + 1 < 16:
                    load_ma(n + 1)
                hi_split(m_hi[:, d, half * HALF:(half + 1) * HALF], gb_t[:, n % 2, :])
                if n + 2 < 16:
                    act.wait_ge(lo_done, SP_M + n + 1)
                    load_gb(n + 2)
            act.wait_ge(out_ready, OUT_OUT)
            act.wait_ge(lo_done, SP_M + 16)
            for c in range(NCH):
                act.dma_start(h_res[:, c, :], x_rows[:, c, :]).then_inc(xr_in[c], 16)

            for c in range(NCH):
                act.wait_ge(out_free, OUT_OUT + NCH + c + 1)
                if c >= 1:
                    act.wait_ge(z2_turned, 2 * c)
                nc.scalar.activation(zb[:], h_res[:, c, :], ACT.Square, accum_out=ss2[:, c:c + 1]).then_inc(h_ss, 1)
                for b in range(2):
                    n = 2 * c + b
                    act.wait_ge(z2_normed, n + 1)
                    hi_split(m_hi[:, 4 * b:4 * b + 4, c * P:(c + 1) * P],
                             z2_tmp[:].rearrange("p (k s) -> p k s", k=4))
            act.wait_ge(lo_done, SP_Z2 + 16)

            def mlp_block(f):
                act.wait_ge(out_free, f * 24 + OUT_MLP)
                for n in range(8):
                    half, q = n // 4, n % 4
                    act.wait_ge(out_ready, f * 24 + (OUT_MLP + n + 1))
                    act.wait_ge(lo_done, f * 8 + (SP_HID + n - 1))
                    nc.scalar.activation(relu[:, n % 2, :], acc[:, n % 4, :], ACT.Relu).then_inc(out_free, 1)
                    if n >= 1:
                        hidden_hi(f, n - 1)
                hidden_hi(f, 7)

            def hidden_hi(f, n):
                half, q = n // 4, n % 4
                act.wait_ge(squared, f * 8 + (n + 1))
                act.wait_ge(out_ready, f * 24 + (OUT_MLP - 4 + 4 * half))
                hi_split(hid_hi[:, q, half * HALF:(half + 1) * HALF], relu[:, n % 2, :])

            with act.Fori(0, N_FB) as f:
                mlp_block(f)
            for c in range(NCH):
                act.wait_ge(out_free, OUT_MLP + 24 * (N_FB - 1) + 16 + c + 1)
                if c >= 1:
                    act.wait_ge(f_ss, c)
                nc.scalar.activation(relu[:].rearrange("p a s -> p (a s)"), h_res[:, c, :], ACT.Square,
                                     accum_out=ss2[:, c:c + 1]).then_inc(f_ss, 1)

        @block.vector
        def _(dve):
            ch = Chain(dve, chain_v)
            link = ch.link
            V = nc.vector

            def lo_split(dst, src, hi):
                V.tensor_tensor(dst, src, hi.bitcast(F32), ALU.subtract).then_inc(lo_done, 1)

            def rstd(dst, tmp, a, width):
                half_bits, y, y2, m = rs_bits[:], rs_tmp[:, 0:1], rs_tmp[:, 1:2], rs_tmp[:, 2:3]
                V.tensor_scalar(m, a, -0.5 / width, -0.5 * EPS, ALU.mult, ALU.add)
                link(V.tensor_scalar(tmp, a, 1.0 / width, EPS, ALU.mult, ALU.add))
                link(V.tensor_scalar(half_bits, tmp.bitcast(I32), 1, None, ALU.arith_shift_right))
                link(V.tensor_scalar(y.bitcast(I32), half_bits, -1.0, 1597463007.0, ALU.mult, ALU.add))
                for step in range(3):
                    link(V.scalar_tensor_tensor(out=y2, in0=y, scalar=m, in1=y, op0=ALU.mult, op1=ALU.mult))
                    link(V.scalar_tensor_tensor(out=dst if step == 2 else y, in0=y2, scalar=1.5, in1=y,
                                                op0=ALU.add, op1=ALU.mult))

            def scale_x(c):
                dve.wait_ge(ss_done, c + 1)
                rstd(rs1[:, c, 0:1], rs1[:, c, 1:2], ss1[:, c:c + 1], D)
                V.tensor_scalar(x_in[:, c % 2, :], x_in[:, c % 2, :], rs1[:, c, 0:1], None, ALU.mult)\
                 .then_inc(z_scaled, 1)

            def norm_z(c):
                for b in range(2):
                    n = 2 * c + b
                    dve.wait_ge(z_turned, n + 1)
                    if n >= 2:
                        dve.wait_ge(lo_done, SP_Z + n - 1)
                    V.tensor_tensor(z_tmp[:, n % 2, :].rearrange("p (k s) -> p k s", k=4),
                                    aux[:, n % 4, :].rearrange("p (k s) -> p k s", k=4),
                                    nmix[:, 4 * b:4 * b + 4].unsqueeze(2).broadcast_to([P, 4, P]), ALU.mult)\
                     .then_inc(z_normed, 1)
                for b in range(2):
                    n = 2 * c + b
                    dve.wait_ge(hi_done, SP_Z + n + 1)
                    lo_split(z_lo[:, 4 * b:4 * b + 4, c * P:(c + 1) * P],
                             z_tmp[:, n % 2, :].rearrange("p (k s) -> p k s", k=4),
                             z_hi[:, 4 * b:4 * b + 4, c * P:(c + 1) * P])

            dve.wait_ge(const_in, 32)
            for c in range(NCH):
                scale_x(c)
                if c >= 1:
                    norm_z(c - 1)
            norm_z(NCH - 1)

            dve.wait_ge(par_in, 16 * 16)
            slot_of = {"lr": 0, "li": 1, "ls": 2}

            def cf(name):
                if name not in slot_of:
                    slot_of[name] = len(slot_of)
                return coef[:, slot_of[name], :]

            def ts(dst, src, s1, s2, o1, o2=None):
                if o2 is None:
                    link(V.tensor_scalar(dst, src, s1, None, o1))
                else:
                    link(V.tensor_scalar(dst, src, s1, s2, o1, o2))

            def tt(dst, a, b, op):
                link(V.tensor_tensor(dst, a, b, op))

            def stt(dst, a, s, b, o1, o2):
                link(V.scalar_tensor_tensor(out=dst, in0=a, scalar=s, in1=b, op0=o1, op1=o2))

            def exp(dst, src):
                x, k, r, k1, k2 = cf("ex"), cf("ek"), cf("er"), cf("ek1"), cf("ek2")
                ts(x, src, -175.0, 175.0, ALU.max, ALU.min)
                ts(k, x, 1.4426950408889634, MAGIC, ALU.mult, ALU.add)
                ts(k, k, MAGIC, None, ALU.subtract)
                stt(r, k, -LN2[0], x, ALU.mult, ALU.add)
                stt(r, k, -LN2[1], r, ALU.mult, ALU.add)
                ts(x, r, 1.0 / 5040, 1.0 / 720, ALU.mult, ALU.add)
                for c in (1.0 / 120, 1.0 / 24, 1.0 / 6, 0.5, 1.0):
                    tt(x, x, r, ALU.mult)
                    ts(x, x, c, None, ALU.add)
                tt(x, x, r, ALU.mult)
                ts(x, x, 1.0, None, ALU.add)
                ts(k1, k, 0.5, MAGIC, ALU.mult, ALU.add)
                ts(k1, k1, MAGIC, None, ALU.subtract)
                tt(k2, k, k1, ALU.subtract)
                for q, kk in enumerate((k1, k2)):
                    ts(ibits[:, q, :], kk, 127.0, 8388608.0, ALU.add, ALU.mult)
                    tt(x, x, ibits[:, q, :].bitcast(F32), ALU.mult)
                link(V.tensor_copy(dst, x))

            def sincos(s_dst, c_dst, src):
                import math
                th, k, r2, sp_, cp = cf("th"), cf("sk"), cf("r2"), cf("sp"), cf("cp")
                big = 2.0 * math.pi * 1024.0
                ts(k, src, 1.0 / big, MAGIC, ALU.mult, ALU.add)
                ts(k, k, MAGIC, None, ALU.subtract)
                first = True
                for c in parts(big, 4):
                    stt(th, k, -c, src if first else th, ALU.mult, ALU.add)
                    first = False
                ts(k, th, 2.0 / math.pi, MAGIC, ALU.mult, ALU.add)
                ts(k, k, MAGIC, None, ALU.subtract)
                for c in parts(math.pi / 2, 4):
                    stt(th, k, -c, th, ALU.mult, ALU.add)
                tt(r2, th, th, ALU.mult)
                ts(sp_, r2, -1.9515295891e-4, 8.3321608736e-3, ALU.mult, ALU.add)
                tt(sp_, sp_, r2, ALU.mult)
                ts(sp_, sp_, -1.6666654611e-1, None, ALU.add)
                tt(sp_, sp_, r2, ALU.mult)
                tt(sp_, sp_, th, ALU.mult)
                tt(sp_, sp_, th, ALU.add)
                ts(cp, r2, 2.443315711809948e-5, -1.388731625493765e-3, ALU.mult, ALU.add)
                tt(cp, cp, r2, ALU.mult)
                ts(cp, cp, 4.166664568298827e-2, None, ALU.add)
                tt(cp, cp, r2, ALU.mult)
                ts(cp, cp, -0.5, None, ALU.add)
                tt(cp, cp, r2, ALU.mult)
                ts(cp, cp, 1.0, None, ALU.add)
                f, n, sg, od = cf("qf"), cf("qn"), cf("qs"), cf("qo")
                ts(f, k, 0.25, -0.375, ALU.mult, ALU.add)
                ts(f, f, MAGIC, None, ALU.add)
                ts(f, f, MAGIC, None, ALU.subtract)
                stt(n, f, -4.0, k, ALU.mult, ALU.add)
                ts(sg, n, 2.0, None, ALU.is_ge)
                stt(od, sg, -2.0, n, ALU.mult, ALU.add)
                ts(sg, sg, -2.0, 1.0, ALU.mult, ALU.add)
                tt(f, cp, sp_, ALU.subtract)
                tt(f, f, od, ALU.mult)
                tt(n, cp, sp_, ALU.add)
                tt(n, n, od, ALU.mult)
                tt(f, sp_, f, ALU.add)
                tt(n, cp, n, ALU.subtract)
                tt(s_dst, f, sg, ALU.mult)
                tt(c_dst, n, sg, ALU.mult)

            lr, li = cf("lr"), cf("li")
            step, mag, ang = cf("step"), cf("mag"), cf("ang")
            exp(step, cf("ls"))
            tt(ang, lr, step, ALU.mult)
            exp(mag, ang)
            tt(ang, li, step, ALU.mult)
            sn, cs = cf("sn"), cf("cs")
            sincos(sn, cs, ang)
            link(V.memset(pwr[:, 0, :], 1.0))
            link(V.memset(pwi[:, 0, :], 0.0))
            tt(pwr[:, 1, :], mag, cs, ALU.mult)
            tt(pwi[:, 1, :], mag, sn, ALU.mult)
            nr, den, kr, ki, tm = cf("nr"), cf("den"), cf("kr"), cf("ki"), cf("tm")
            ts(nr, pwr[:, 1, :], 1.0, None, ALU.subtract)
            tt(den, lr, lr, ALU.mult)
            tt(tm, li, li, ALU.mult)
            tt(den, den, tm, ALU.add)
            link(V.reciprocal(den, den))
            tt(kr, nr, lr, ALU.mult)
            tt(tm, pwi[:, 1, :], li, ALU.mult)
            tt(kr, kr, tm, ALU.add)
            tt(kr, kr, den, ALU.mult)
            tt(ki, pwi[:, 1, :], lr, ALU.mult)
            tt(tm, nr, li, ALU.mult)
            tt(ki, ki, tm, ALU.subtract)
            tt(ki, ki, den, ALU.mult)

            def wide(a):
                return a.unsqueeze(2).broadcast_to([P, PAIRS, CH])

            br, bi = b_raw[:, 0, :, :], b_raw[:, 1, :, :]
            tt(bbr[:], br, wide(kr), ALU.mult)
            tt(bbi[:], bi, wide(ki), ALU.mult)
            tt(bbr[:], bbr[:], bbi[:], ALU.subtract)
            tt(bbi[:], br, wide(ki), ALU.mult)
            tt(bi, bi, wide(kr), ALU.mult)
            tt(bbi[:], bbi[:], bi, ALU.add)

            def cmul(dr, di, ar, ai, xr, xi):
                t1, t2, t3, t4 = cf("m1"), cf("m2"), cf("m3"), cf("m4")
                V.tensor_tensor(t1, ar, xr, ALU.mult)
                V.tensor_tensor(t2, ai, xi, ALU.mult)
                V.tensor_tensor(t3, ar, xi, ALU.mult)
                tt(t4, ai, xr, ALU.mult)
                V.tensor_tensor(dr, t1, t2, ALU.subtract)
                tt(di, t3, t4, ALU.add)

            for k in range(2, T + 1):
                cmul(pwr[:, k, :], pwi[:, k, :], pwr[:, k - 1, :], pwi[:, k - 1, :], pwr[:, 1, :], pwi[:, 1, :])
            for k in range(T):
                V.tensor_copy(rpr[:, k, :], pwr[:, T - 1 - k, :])
                V.tensor_copy(rpi[:, k, :], pwi[:, T - 1 - k, :])
            V.tensor_copy(p8r[:, 0, :], pwr[:, T, :])
            link(V.tensor_copy(p8i[:, 0, :], pwi[:, T, :]))
            for k in range(1, T):
                cmul(p8r[:, k, :], p8i[:, k, :], p8r[:, k - 1, :], p8i[:, k - 1, :], p8r[:, 0, :], p8i[:, 0, :])
            V.tensor_copy(p64r[:, 0, :], p8r[:, T - 1, :])
            link(V.tensor_copy(p64i[:, 0, :], p8i[:, T - 1, :]))
            for k in range(1, 4):
                cmul(p64r[:, k, :], p64i[:, k, :], p64r[:, k - 1, :], p64i[:, k - 1, :],
                     p64r[:, k - 1, :], p64i[:, k - 1, :])
            dve.wait_ge(u_out, 16 * MT)
            dve.wait_ge(ct_ready, 1)
            link(V.memset(toep[:].rearrange("p g s -> p (g s)"), 0.0))
            link(V.memset(hst[:, :, :, 0:1], 0.0))

            with dve.Fori(0, 2) as it:
                ch.enter(it, 2 * PER_BATCH)
                for b in range(2):
                    start = ch.n

                    def done(x):
                        return it * 2 + (b + x)

                    mt = it * 2 + b
                    q0 = mt * QP
                    qs = bass.ds(q0, QP)

                    def outer(dst, x, pw, n):
                        return V.tensor_tensor(dst, x[:, qs, :].unsqueeze(2).broadcast_to([P, QP, n, CH]),
                                               pw[:, 0:n, qs].rearrange("p t q -> p q t").unsqueeze(3)
                                               .broadcast_to([P, QP, n, CH]), ALU.mult)

                    t_a = ta[:, 0:QP * (T + 1) * CH].rearrange("p (q t c) -> p q t c", q=QP, c=CH)
                    t_b = tb[:, 0:QP * (T + 1) * CH].rearrange("p (q t c) -> p q t c", q=QP, c=CH)
                    outer(car[:], ctr, pwr, T + 1)
                    outer(t_a, cti, pwi, T + 1)
                    outer(can[:], ctr, pwi, T + 1)
                    link(outer(t_b, cti, pwr, T + 1))
                    V.tensor_tensor(car[:], car[:], t_a, ALU.subtract)
                    flat = can[:].rearrange("p q t c -> p (q t c)")
                    link(V.scalar_tensor_tensor(out=flat, in0=tb[:, 0:QP * (T + 1) * CH], scalar=-1.0, in1=flat,
                                                op0=ALU.mult, op1=ALU.subtract))
                    t_a = ta[:, 0:QP * T * CH].rearrange("p (q t c) -> p q t c", q=QP, c=CH)
                    t_b = tb[:, 0:QP * T * CH].rearrange("p (q t c) -> p q t c", q=QP, c=CH)
                    outer(abr[:], bbr, rpr, T)
                    outer(t_a, bbi, rpi, T)
                    outer(abi[:], bbr, rpi, T)
                    link(outer(t_b, bbi, rpr, T))
                    V.tensor_tensor(abr[:], abr[:], t_a, ALU.subtract)
                    V.tensor_tensor(abi[:], abi[:], t_b, ALU.add).then_inc(prep, 1)

                    dve.wait_ge(x_state, done(1))
                    hb = hst[:, :, :, 1:NT + 1]
                    link(V.tensor_copy(hb.rearrange("p r q n -> p (r q) n"),
                                       aux[:, 0:2, :].rearrange("p r (q n) -> p (r q) n", q=QP)))
                    blocks = hb.rearrange("p r q (s i) -> p r q s i", i=T)

                    def mac(dst_r, dst_i, ar, ai, xr, xi, shape, n, last=False):
                        names = "abc"[:len(shape)]
                        sizes = dict(zip(names, shape))
                        flat = f"p ({' '.join(names)}) -> p {' '.join(names)}"

                        def tmp(buf, o):
                            return buf[:, o:o + n].rearrange(flat, **sizes)

                        t1, t2, t3, t4 = tmp(ta, 0), tmp(ta, n), tmp(tb, 0), tmp(tb, n)
                        V.tensor_tensor(t1, xr, ar, ALU.mult)
                        V.tensor_tensor(t2, xi, ai, ALU.mult)
                        V.tensor_tensor(t3, xi, ar, ALU.mult)
                        link(V.tensor_tensor(t4, xr, ai, ALU.mult))
                        V.tensor_tensor(t1, t1, t2, ALU.subtract)
                        link(V.tensor_tensor(t3, t3, t4, ALU.add))
                        V.tensor_tensor(dst_r, dst_r, t1, ALU.add)
                        ins = V.tensor_tensor(dst_i, dst_i, t3, ALU.add)
                        if last:
                            ins.then_inc(scanned, 1)
                        else:
                            link(ins)

                    a8 = [p[:, 0, qs].unsqueeze(2).broadcast_to([P, QP, SUP]) for p in (p8r, p8i)]
                    for i in range(1, T):
                        mac(blocks[:, 0, :, :, i], blocks[:, 1, :, :, i], a8[0], a8[1],
                            blocks[:, 0, :, :, i - 1], blocks[:, 1, :, :, i - 1], [QP, SUP], QP * SUP)
                    for lv in range(4):
                        d = 1 << lv
                        w = SUP - d
                        a64 = [p[:, lv, qs].unsqueeze(2).broadcast_to([P, QP, w]) for p in (p64r, p64i)]
                        mac(blocks[:, 0, :, d:, T - 1], blocks[:, 1, :, d:, T - 1], a64[0], a64[1],
                            blocks[:, 0, :, 0:w, T - 1], blocks[:, 1, :, 0:w, T - 1], [QP, w], QP * w)
                    for q in range(QP):
                        w = SUP - 1
                        pq = [p[:, 0:T - 1, bass.ds(q0 + q, 1)].rearrange("p i a -> p a i").broadcast_to([P, w, T - 1])
                              for p in (p8r, p8i)]
                        prev = [blocks[:, r, q, 0:w, T - 1].unsqueeze(2).broadcast_to([P, w, T - 1]) for r in range(2)]
                        mac(blocks[:, 0, q, 1:, 0:T - 1], blocks[:, 1, q, 1:, 0:T - 1], pq[0], pq[1],
                            prev[0], prev[1], [w, T - 1], w * (T - 1), last=q == QP - 1)

                    dve.wait_ge(y_back, it * 64 + 32 * (b + 1))
                    y = y_blk[:].rearrange("p g s -> p (g s)")
                    link(V.scalar_tensor_tensor(out=y, in0=u_back[:], scalar=dskip[:, bass.ds(mt, 1)], in1=y,
                                                op0=ALU.mult, op1=ALU.add))
                    link(V.tensor_tensor(ta[:], y, y, ALU.mult))
                    link(V.tensor_scalar(ta[:], ta[:], 0.044715, 1.0, ALU.mult, ALU.add))
                    V.tensor_tensor(ta[:], ta[:], y, ALU.mult).then_inc(gelu_arg, 1)
                    dve.wait_ge(gelu_sig, done(1))
                    V.tensor_tensor(y_raw[:, bass.ds(mt, 1), :].rearrange("p a (n j) -> p (a j) n", j=T),
                                    y.rearrange("p (j n) -> p j n", j=T), tb[:].rearrange("p (j n) -> p j n", j=T),
                                    ALU.mult).then_inc(y_done, 1)
                    dve.wait_ge(y_done, done(1))
                    assert ch.n - start == PER_BATCH, ch.n - start
                ch.leave(2)

            for m in range(MT):
                dve.wait_ge(hi_done, SP_Y + m + 1)
                lo_split(y_lo[:, m, :], y_raw[:, m, :], y_hi[:, m, :])
            for half in range(2):
                hs = slice(half * HALF, (half + 1) * HALF)
                for m in range(MT):
                    n = half * MT + m
                    dve.wait_ge(glu_sig, n + 1)
                    V.tensor_tensor(y_raw[:, m, hs], y_raw[:, m, hs], glu_s[:, m, :], ALU.mult).then_inc(out_free, 1)
                    dve.wait_ge(out_free, OUT_GLU + n + 1)
                for m in range(MT):
                    n = half * MT + m
                    dve.wait_ge(hi_done, SP_YA + n + 1)
                    lo_split(y_lo[:, m, hs], y_raw[:, m, hs], y_hi[:, m, hs])
            for n in range(16):
                dve.wait_ge(out_ready, OUT_PA + n + 1)
                dve.wait_ge(ga_in[n % 2], 16 * (n // 2 + 1))
                V.tensor_tensor(ga_t[:, n % 2, :], acc[:, n % 4, :], ga_t[:, n % 2, :], ALU.mult).then_inc(out_free, 1)

            dve.wait_ge(ret_in, 48)

            def g_silu(h, c):
                n = OUT_RET + c
                dve.wait_ge(sig_g, h * 8 + (c + 1))
                V.tensor_tensor(silu_g[:, c, :], acc[:, n % 4, 0:DV], sig_t[:, c % 2, :], ALU.mult)\
                 .then_inc(out_free, 1)

            def head(h, more):
                def cnt(c):
                    return h * 8 + (c + 1)

                def rotate(c):
                    dve.wait_ge(out_free, h * 16 + (OUT_RET + NCH + c + 1))
                    src = qk[:, c % 2, :, :].rearrange("p a (b d) -> p (a b) d", b=2)
                    cos = rope[:, c, 0:DK // 2].unsqueeze(1).broadcast_to([P, 4, DK // 2])
                    sin = rope[:, c, DK // 2:].unsqueeze(1).broadcast_to([P, 4, DK // 2])
                    V.tensor_tensor(rc[:].rearrange("p a b d -> p (a b) d"), src, cos, ALU.mult)
                    link(V.tensor_tensor(rsn[:].rearrange("p a b d -> p (a b) d"), src, sin, ALU.mult))
                    for a, dst in ((0, rot[:, 0, :, :]),
                                   (1, kvk[:, c % 2, :].rearrange("p (b d) -> p b d", b=2))):
                        V.tensor_tensor(dst[:, 0, :], rc[:, a, 0, :], rsn[:, a, 1, :], ALU.subtract)
                        ins = V.tensor_tensor(dst[:, 1, :], rsn[:, a, 0, :], rc[:, a, 1, :], ALU.add)
                    ins.then_inc(rotated, 1)

                def decay(c):
                    dve.wait_ge(scores, cnt(c))
                    V.tensor_tensor(prob[:], aux[:, 1, 0:P], mask[:, bass.ds(h, 1), :].rearrange("p a s -> p (a s)"),
                                    ALU.mult).then_inc(prob_ready, 1)

                def norm_o(c):
                    dve.wait_ge(o_ready, cnt(c))
                    if c == 0:
                        V.tensor_copy(state[:], aux[:, 3, 0:DV]).then_inc(state_ready, 1)
                    else:
                        V.scalar_tensor_tensor(out=state[:], in0=state[:], scalar=gam[:, bass.ds(h + 2 * HEADS, 1)],
                                               in1=aux[:, 3, 0:DV], op0=ALU.mult, op1=ALU.add).then_inc(state_ready, 1)
                    dve.wait_ge(o_ss, cnt(c))
                    rstd(ors[:, 0:1], ors[:, 1:2], oss[:, c % 2:c % 2 + 1], DV)
                    V.scalar_tensor_tensor(out=yb[:], in0=aux[:, 2, 0:DV], scalar=ors[:, 0:1], in1=silu_g[:, c, :],
                                           op0=ALU.mult, op1=ALU.mult).then_inc(yb_ready, 1)
                    dve.wait_ge(yb_ready, cnt(c))

                for s in range(1, NCH + 2):
                    if s <= NCH:
                        rotate(s - 1)
                    if s >= 2:
                        norm_o(s - 2)
                    if more and s >= NCH:
                        g_silu(h + 1, 2 * (s - NCH))
                    if s <= NCH:
                        decay(s - 1)
                    if more and s >= NCH:
                        g_silu(h + 1, 2 * (s - NCH) + 1)
                if more:
                    for c in range(4, NCH):
                        g_silu(h + 1, c)

            for c in range(NCH):
                g_silu(0, c)
            with dve.Fori(0, HEADS - 1) as h:
                ch.enter(h, PER_HEAD)
                head(h, True)
                ch.leave(HEADS - 1)
            head(HEADS - 1, False)
            for k in range(KT):
                dve.wait_ge(hi_done, SP_YB + k + 1)
                lo_split(z_lo[:, k, :], yb_raw[:, k, :], z_hi[:, k, :])
            dve.wait_ge(out_free, OUT_PB)
            for n in range(16):
                d, half = n // 2, n % 2
                hs = slice(half * HALF, (half + 1) * HALF)
                dve.wait_ge(out_ready, OUT_PB + n + 1)
                dve.wait_ge(gb_in[n % 2], 16 * (n // 2 + 1))
                V.tensor_tensor(gb_t[:, n % 2, :], acc[:, n % 4, :], gb_t[:, n % 2, :], ALU.mult).then_inc(out_free, 1)
                dve.wait_ge(out_free, OUT_PB + n + 1)
                dve.wait_ge(ma_in, 16 * (n + 1))
                V.tensor_tensor(gb_t[:, n % 2, :], gb_t[:, n % 2, :], ma_t[:], ALU.add).then_inc(merged, 1)
                dve.wait_ge(hi_done, SP_M + n + 1)
                lo_split(m_lo[:, d, hs], gb_t[:, n % 2, :], m_hi[:, d, hs])
            def add_h(n, c, j):
                dve.wait_ge(out_ready, n + 1)
                hs = slice(j * HALF, (j + 1) * HALF)
                return V.tensor_tensor(h_res[:, c, hs], h_res[:, c, hs], acc[:, n % 4, :], ALU.add)

            for c in range(NCH):
                dve.wait_ge(xr_in[c], 16)
                add_h(OUT_OUT + c, c, 0).then_inc(out_free, 1)
            dve.wait_ge(nmlp_in, 16)

            def norm_z2(c):
                for b in range(2):
                    n = 2 * c + b
                    dve.wait_ge(z2_turned, n + 1)
                    dve.wait_ge(lo_done, SP_Z2 + n)
                    V.tensor_tensor(z2_tmp[:].rearrange("p (k s) -> p k s", k=4),
                                    aux[:, n % 4, :].rearrange("p (k s) -> p k s", k=4),
                                    nmlp[:, 4 * b:4 * b + 4].unsqueeze(2).broadcast_to([P, 4, P]), ALU.mult)\
                     .then_inc(z2_normed, 1)
                    dve.wait_ge(hi_done, SP_Z2 + n + 1)
                    lo_split(m_lo[:, 4 * b:4 * b + 4, c * P:(c + 1) * P],
                             z2_tmp[:].rearrange("p (k s) -> p k s", k=4),
                             m_hi[:, 4 * b:4 * b + 4, c * P:(c + 1) * P])

            for c in range(NCH):
                add_h(OUT_OUT + NCH + c, c, 1).then_inc(out_free, 1)
                if c >= 1:
                    norm_z2(c - 1)
                dve.wait_ge(h_ss, c + 1)
                rstd(rs2[:, c, 0:1], rs2[:, c, 1:2], ss2[:, c:c + 1], D)
                V.tensor_scalar(zb[:], h_res[:, c, :], rs2[:, c, 0:1], None, ALU.mult).then_inc(z2_scaled, 1)
            norm_z2(NCH - 1)

            with dve.Fori(0, N_FB) as f:
                dve.wait_ge(out_free, f * 24 + OUT_MLP)
                for n in range(8):
                    half, q = n // 4, n % 4
                    hs = slice(half * HALF, (half + 1) * HALF)
                    dve.wait_ge(out_free, f * 24 + (OUT_MLP + n + 1))
                    V.tensor_tensor(relu[:, n % 2, :], relu[:, n % 2, :], relu[:, n % 2, :], ALU.mult)\
                     .then_inc(squared, 1)
                    dve.wait_ge(hi_done, f * 8 + (SP_HID + n + 1))
                    lo_split(hid_lo[:, q, hs], relu[:, n % 2, :], hid_hi[:, q, hs])
                for j in range(2):
                    for c in range(NCH):
                        n = OUT_MLP + 8 + 8 * j + c
                        dve.wait_ge(out_ready, f * 24 + (n + 1))
                        hs = slice(j * HALF, (j + 1) * HALF)
                        V.tensor_tensor(h_res[:, c, hs], h_res[:, c, hs], acc[:, n % 4, :], ALU.add)\
                         .then_inc(out_free, 1)
            dve.wait_ge(out_free, OUT_MLP + 24 * N_FB)
            dve.wait_ge(nf_in, 16)
            for c in range(NCH):
                dve.wait_ge(f_ss, c + 1)
                rstd(rs2[:, c, 0:1], rs2[:, c, 1:2], ss2[:, c:c + 1], D)
                V.scalar_tensor_tensor(out=h_res[:, c, :], in0=h_res[:, c, :], scalar=rs2[:, c, 0:1], in1=nf,
                                       op0=ALU.mult, op1=ALU.mult).then_inc(f_done, 1)


_INS = ["x", "w_in", "lam_re", "lam_im", "b_re", "b_im", "c_re", "c_im", "d_skip", "log_step", "w_glu", "b_glu",
        "w_proj_ssm", "w_proj_ret", "w_out", "norm_mix", "norm_mlp", "w_up", "w_down", "norm_final"]


def tables():
    import numpy as np
    inv = (10000.0 ** (-np.arange(0, DK, 2, dtype=np.float64) / DK)).astype(np.float32)
    ang = (np.arange(SEQ, dtype=np.float32)[:, None] * inv[None, :]).astype(np.float64)
    rope = np.concatenate([np.cos(ang), np.sin(ang)], axis=1).astype(np.float32)
    lg = np.log(1.0 - 2.0 ** (-5.0 - np.arange(HEADS, dtype=np.float64)))
    idx = np.arange(P, dtype=np.float64)[:, None]
    gam = np.concatenate([np.exp((idx + 1) * lg), np.exp((P - 1 - idx) * lg) * DK ** -0.5,
                          np.exp(P * lg) * np.ones((P, 1))], axis=1).astype(np.float32)
    causal = (np.arange(P)[None, :] >= np.arange(P)[:, None]).astype(np.float64)
    mask = (causal[:, None, :] * np.exp(-P * lg)[None, :, None]).astype(np.float32)
    return {"rope": rope, "gam": gam, "mask": mask, "ident": np.eye(P, dtype=np.float32)}


def kernel(**inputs):
    import numpy as np
    import concourse.bacc as bacc
    from concourse.bass_utils import run_bass_kernel_spmd

    nc = bacc.Bacc("TRN2", target_bir_lowering=False, num_devices=1)
    arrays = {name: np.ascontiguousarray(inputs[name]) for name in _INS}
    arrays.update(tables())
    t = {name: nc.dram_tensor("in_" + name, a.shape, mybir.dt.from_np(a.dtype), kind="ExternalInput").ap()
         for name, a in arrays.items()}
    t["out"] = nc.dram_tensor("out", (1, SEQ, D), F32, kind="ExternalOutput").ap()
    build(nc, t)
    return run_bass_kernel_spmd(nc, [{"in_" + name: a for name, a in arrays.items()}], core_ids=[0]).results[0]["out"]
```

```python
from contextlib import ExitStack

import concourse.bass as bass
from concourse import mybir

F32 = mybir.dt.float32
F32R = mybir.dt.float32r
BF16 = mybir.dt.bfloat16
I32 = mybir.dt.int32
ALU = mybir.AluOpType
ACT = mybir.ActivationFunctionType

P = 128
SEQ = 1024
D = 1024
KT = D // P
NCH = SEQ // P
HALF = 512
FF = 4096
FB = 512
N_FB = FF // FB
SSM = 512
GROUPS, STATE, CH = 32, 64, 16
T = P // CH
NT = SEQ // T
MT = SSM // P
PAIRS = GROUPS // 2
QP = PAIRS // MT
GB = 2 * QP
SUP = NT // T
HEADS, DK, DV = 4, 128, 256
EPS = 1e-6

COL_Q = SSM
COL_K = COL_Q + HEADS * DK
COL_V = COL_K + HEADS * DK
COL_G = COL_V + HEADS * DV
COL_GATE = COL_G + HEADS * DV

LD_U, LD_GATE, LD_GLU, LD_PA, LD_RET, LD_PB, LD_OUT, LD_MLP = 0, 4, 20, 22, 26, 50, 58, 66
GR_U, GR_GATE, GR_GLU, GR_PA, GR_RET, GR_PB, GR_OUT, GR_MLP = 0, 1, 5, 6, 8, 16, 18, 20
OUT_U, OUT_GATE, OUT_GLU, OUT_PA, OUT_RET, OUT_PB, OUT_OUT, OUT_MLP = 0, 8, 40, 48, 64, 128, 144, 160
SP_Z, SP_Y, SP_YA, SP_YB, SP_M, SP_Z2, SP_HID = 0, 16, 20, 28, 36, 52, 68

LN2 = (0.693359375, -2.12194440e-4)
MAGIC = 12582912.0


def parts(value, n):
    import math
    out = []
    for _ in range(n):
        if value == 0.0:
            out.append(0.0)
            continue
        e = math.floor(math.log2(abs(value))) - 10
        q = round(value / 2.0 ** e) * 2.0 ** e
        out.append(q)
        value -= q
    return out


PER_BATCH = 51
PER_HEAD = 10 * NCH


class Chain:

    def __init__(self, eng, sem):
        self.eng, self.sem, self.n, self.off, self.mark = eng, sem, 0, 0, 0

    def link(self, ins):
        self.n += 1
        ins.then_inc(self.sem, 1)
        self.eng.wait_ge(self.sem, self.off + self.n)

    def enter(self, i, per):
        self.off, self.mark, self.per = i * per, self.n, per

    def leave(self, trips):
        assert self.n - self.mark == self.per, (self.n - self.mark, self.per)
        self.n += (trips - 1) * self.per
        self.off = 0


def build(nc, t):
    with ExitStack() as ctx:
        def sb(name, shape, dt=F32, where=ctx):
            return where.enter_context(nc.sbuf_tensor(name, shape, dt))

        def sem(name):
            return ctx.enter_context(nc.semaphore(name))

        ident = sb("ident", [P, P])
        rs_bits = sb("rs_bits", [P, 2], I32)
        rs_tmp = sb("rs_tmp", [P, 4, 2])
        stage = sb("stage", [P, 2, 2 * HALF])
        w_hi = sb("w_hi", [P, 2, KT, HALF], F32R)
        w_lo = sb("w_lo", [P, 2, KT, HALF], F32R)
        with ExitStack() as r:
            z_hi = sb("z_hi", [P, KT, SEQ], F32R, r)
            z_lo = sb("z_lo", [P, KT, SEQ], F32R, r)
        with ExitStack() as r:
            h_res = sb("h_res", [P, NCH, D], F32, r)
            hid_hi = sb("hid_hi", [P, FB // P, SEQ], F32R, r)
            hid_lo = sb("hid_lo", [P, FB // P, SEQ], F32R, r)
        ctx.enter_context(nc.sbuf_tensor("region1", [P, 2 * KT * SEQ], F32))

        ph = ExitStack()
        bbr = sb("bbr", [P, PAIRS, CH], F32, ph)
        bbi = sb("bbi", [P, PAIRS, CH], F32, ph)
        ctr = sb("ctr", [P, PAIRS, CH], F32, ph)
        cti = sb("cti", [P, PAIRS, CH], F32, ph)
        pwr = sb("pwr", [P, T + 1, PAIRS], F32, ph)
        pwi = sb("pwi", [P, T + 1, PAIRS], F32, ph)
        rpr = sb("rpr", [P, T, PAIRS], F32, ph)
        rpi = sb("rpi", [P, T, PAIRS], F32, ph)
        p8r = sb("p8r", [P, T, PAIRS], F32, ph)
        p8i = sb("p8i", [P, T, PAIRS], F32, ph)
        p64r = sb("p64r", [P, 4, PAIRS], F32, ph)
        p64i = sb("p64i", [P, 4, PAIRS], F32, ph)
        dskip = sb("dskip", [P, MT], F32, ph)
        bglu = sb("bglu", [P, MT], F32, ph)
        with ExitStack() as r:
            x_in = sb("x_in", [P, NCH, D], F32, r)
        with ExitStack() as r:
            u_all = sb("u_all", [P, MT, T, NT], F32, r)
        y_raw = sb("y_raw", [P, MT, SEQ], F32, ph)
        with ExitStack() as r:
            sb("x_upper", [P, NCH // 2, D], F32, r)
            z_tmp = sb("z_tmp", [P, 4, HALF], F32, r)
            diag1 = sb("diag1", [P, 2, P], F32, r)
            x_junk = sb("x_junk", [P, D], BF16, r)
            ss1 = sb("ss1", [P, NCH], F32, r)
            rs1 = sb("rs1", [P, NCH], F32, r)
            nmix = sb("nmix", [P, KT], F32, r)
            c_raw = sb("c_raw", [P, 2, MT, P], F32, r)
            b_raw = sb("b_raw", [P, 2, PAIRS, CH], F32, r)
            coef = sb("coef", [P, 40, PAIRS], F32, r)
            ibits = sb("ibits", [P, 2, PAIRS], I32, r)
        with ExitStack() as r:
            u_blk = sb("u_blk", [P, GB, NT], F32, r)
            toep = sb("toep", [P, GB, P], F32, r)
            car = sb("car", [P, QP, T + 1, CH], F32, r)
            can = sb("can", [P, QP, T + 1, CH], F32, r)
            abr = sb("abr", [P, QP, T, CH], F32, r)
            abi = sb("abi", [P, QP, T, CH], F32, r)
            abt = sb("abt", [P, 2, QP, P], F32, r)
            hst = sb("hst", [P, 2, QP, NT + 1], F32, r)
            y_blk = sb("y_blk", [P, GB, NT], F32, r)
            u_back = sb("u_back", [P, SEQ], F32, r)
            ta = sb("ta", [P, SEQ], F32, r)
            tb = sb("tb", [P, SEQ], F32, r)
            gate_t = sb("gate_t", [P, 2, HALF], F32, r)
        with ExitStack() as r:
            y_hl = sb("y_hl", [P, MT, 2, SEQ], F32R, r)
            y_hi, y_lo = y_hl[:, :, 0, :], y_hl[:, :, 1, :]
            glu_s = sb("glu_s", [P, MT, HALF], F32, r)
            ga_t = sb("ga_t", [P, 2, HALF], F32, r)
        ph.close()
        with ExitStack() as r:
            rope = sb("rope", [P, NCH, P], F32, r)
            gam = sb("gam", [P, 3 * HEADS], F32, r)
            mask = sb("mask", [P, HEADS, P], F32, r)
            silu_g = sb("silu_g", [P, NCH, DV], F32, r)
            sig_t = sb("sig_t", [P, 2, DV], F32, r)
            qk = sb("qk", [P, 2, 2, DK], F32, r)
            vv = sb("vv", [P, 2, DV], F32, r)
            rot = sb("rot", [P, 2, 2, DK // 2], F32, r)
            rc = sb("rc", [P, 2, 2, DK // 2], F32, r)
            rsn = sb("rsn", [P, 2, 2, DK // 2], F32, r)
            kvk = sb("kvk", [P, 2, DK], F32, r)
            qkt = sb("qkt", [P, 2, P], F32, r)
            prob = sb("prob", [P, P], F32, r)
            state = sb("state", [P, DV], F32, r)
            yb = sb("yb", [P, DV], F32, r)
            o_junk = sb("o_junk", [P, DV], BF16, r)
            oss = sb("oss", [P, 2], F32, r)
            ors = sb("ors", [P, 1], F32, r)
            yb_raw = sb("yb_raw", [P, KT, SEQ], F32, r)
        with ExitStack() as r:
            m_hi = sb("m_hi", [P, KT, SEQ], F32R, r)
            m_lo = sb("m_lo", [P, KT, SEQ], F32R, r)
            nmlp = sb("nmlp", [P, KT], F32, r)
            ss2 = sb("ss2", [P, NCH], F32, r)
            rs2 = sb("rs2", [P, NCH], F32, r)
            with ExitStack() as q:
                gb_t = sb("gb_t", [P, 2, HALF], F32, q)
                ma_t = sb("ma_t", [P, HALF], F32, q)
            with ExitStack() as q:
                h_junk = sb("h_junk", [P, D], BF16, q)
                z2_tmp = sb("z2_tmp", [P, 2, HALF], F32, q)
                diag2 = sb("diag2", [P, P], F32, q)
            with ExitStack() as q:
                sb("h_junk_again", [P, D], BF16, q)
                relu = sb("relu", [P, 2, HALF], F32, q)
        acc = ctx.enter_context(nc.psum_tensor("acc", [P, 4, HALF], F32))
        aux = ctx.enter_context(nc.psum_tensor("aux", [P, 4, HALF], F32))

        u_dram = nc.dram_tensor("u_dram", (MT, P, T, NT), F32, kind="Internal").ap()
        y_dram = nc.dram_tensor("y_dram", (MT, P, T, NT), F32, kind="Internal").ap()
        gate_dram = nc.dram_tensor("gate_dram", (2 * KT, P, SEQ), F32, kind="Internal").ap()
        ma_dram = nc.dram_tensor("ma_dram", (KT, P, SEQ), F32, kind="Internal").ap()
        out_rows = t["out"][0].rearrange("(c p) d -> p c d", p=P)
        x_rows = t["x"][0].rearrange("(c p) d -> p c d", p=P)

        const_in = sem("const_in")
        par_in = sem("par_in")
        ret_in = sem("ret_in")
        x_ready = [sem(f"x_ready{i}") for i in range(NCH)]
        raw = [sem(f"raw{i}") for i in range(2)]
        raw_qkv = [sem(f"raw_qkv{i}") for i in range(2)]
        hi_pool = sem("hi_pool")
        w_ready = sem("w_ready")
        out_ready = sem("out_ready")
        out_free = sem("out_free")
        hi_done = sem("hi_done")
        lo_done = sem("lo_done")
        chain_v = sem("chain_v")
        tick_pool = sem("tick_pool")
        tick_act = sem("tick_act")
        ss_done = sem("ss_done")
        diag_made = sem("diag_made")
        z_turned = sem("z_turned")
        z_normed = sem("z_normed")
        u_out = sem("u_out")
        ct_turned = sem("ct_turned")
        ct_ready = sem("ct_ready")
        zeroed = sem("zeroed")
        prep = sem("prep")
        ab_turned = sem("ab_turned")
        ab_ready = sem("ab_ready")
        kern = sem("kern")
        kern_ready = sem("kern_ready")
        toep_in = sem("toep_in")
        u_blk_in = sem("u_blk_in")
        x_state = sem("x_state")
        scanned = sem("scanned")
        y_prod = sem("y_prod")
        y_copied = sem("y_copied")
        y_sent = sem("y_sent")
        y_back = sem("y_back")
        gelu_arg = sem("gelu_arg")
        gelu_sig = sem("gelu_sig")
        y_done = sem("y_done")
        gate_sent = [sem(f"gate_sent{i}") for i in range(2)]
        glu_sig = sem("glu_sig")
        ga_in = [sem(f"ga_in{i}") for i in range(2)]
        ma_sent = [sem(f"ma_sent{i}") for i in range(2)]
        sig_g = sem("sig_g")
        rotated = sem("rotated")
        qk_turned = sem("qk_turned")
        qkt_ready = sem("qkt_ready")
        scores = sem("scores")
        prob_ready = sem("prob_ready")
        kv_ready = sem("kv_ready")
        state_ready = sem("state_ready")
        o_ready = sem("o_ready")
        o_ss = sem("o_ss")
        yb_ready = sem("yb_ready")
        yb_turned = sem("yb_turned")
        yb_stored = sem("yb_stored")
        nmlp_in = sem("nmlp_in")
        gb_in = [sem(f"gb_in{i}") for i in range(2)]
        ma_in = sem("ma_in")
        merged = sem("merged")
        xr_in = [sem(f"xr_in{i}") for i in range(NCH)]
        h_ss = sem("h_ss")
        diag2_made = sem("diag2_made")
        z2_turned = sem("z2_turned")
        z2_normed = sem("z2_normed")
        relu_made = sem("relu_made")
        squared = sem("squared")
        nf_in = sem("nf_in")
        f_ss = sem("f_ss")
        f_done = sem("f_done")
        stored = sem("stored")

        nf = stage[:, 0, :]

        block = ctx.enter_context(nc.Block())

        @block.sync
        def _(sp):
            def load(n, src, k=2, waits=None):
                s = n % 2 if waits is None else waits[1]
                if waits is not None:
                    sp.wait_ge(w_ready, waits[0])
                elif n >= 2:
                    sp.wait_ge(w_ready, n - 1)
                sp.dma_start(stage[:, s, :].rearrange("p (k c) -> p k c", k=k), src).then_inc(raw[s], 16)

            w_in = t["w_in"][0].rearrange("(k p) c -> p k c", p=P)

            sp.dma_start(ident[:], t["ident"]).then_inc(const_in, 16)
            sp.dma_start(nmix[:], t["norm_mix"].rearrange("a (k p) -> p (a k)", p=P), allow_slow_non_contiguous=True).then_inc(const_in, 16)
            for c in range(NCH):
                sp.dma_start(x_in[:, c, :], x_rows[:, c, :]).then_inc(x_ready[c], 16)
                if c in (1, 3):
                    i = c // 2
                    load(i, w_in[:, 2 * i:2 * i + 2, 0:HALF])
            for gp in range(2):
                rows = slice(gp * STATE, (gp + 1) * STATE)
                sp.dma_start(coef[rows, 0, :], t["lam_re"][0, gp::2, :].rearrange("g p -> p g"),
                             allow_slow_non_contiguous=True).then_inc(par_in, 16)
                sp.dma_start(coef[rows, 1, :], t["lam_im"][0, gp::2, :].rearrange("g p -> p g"),
                             allow_slow_non_contiguous=True).then_inc(par_in, 16)
                ls = t["log_step"]
                sp.dma_start(coef[rows, 2, :], bass.AP(tensor=ls.tensor, offset=gp, ap=[[0, STATE], [2, PAIRS]]),
                             allow_slow_non_contiguous=True).then_inc(par_in, 16)
                for ri, name in enumerate(("b_re", "b_im")):
                    sp.dma_start(b_raw[rows, ri, :, :], t[name][0, gp::2, :, :].rearrange("g p c -> p g c"))\
                      .then_inc(par_in, 16)
                for ri, name in enumerate(("c_re", "c_im")):
                    sp.dma_start(c_raw[:, ri, :, gp * STATE:(gp + 1) * STATE],
                                 t[name][0].rearrange("(m g) c p -> (g c) m p", m=MT)).then_inc(par_in, 16)
            sp.dma_start(dskip[:], t["d_skip"].rearrange("a (m p) -> p (a m)", p=P), allow_slow_non_contiguous=True).then_inc(par_in, 16)
            sp.dma_start(bglu[:], t["b_glu"].rearrange("a (m p) -> p (a m)", p=P), allow_slow_non_contiguous=True).then_inc(par_in, 16)
            for i in range(2, 4):
                load(i, w_in[:, 2 * i:2 * i + 2, 0:HALF])
            with sp.Fori(0, MT) as b:
                for i in range(4):
                    n = LD_GATE + i
                    load(n, w_in[:, 4 * (i % 2):4 * (i % 2) + 4,
                                 bass.ds(b * HALF + (COL_GATE + i // 2 * (HALF // 2)), HALF // 2)],
                         k=4, waits=(b * 4 + (n - 1), n % 2))
            w_glu = t["w_glu"][0].rearrange("(k p) c -> p k c", p=P)
            for i in range(2):
                load(LD_GLU + i, w_glu[:, 2 * i:2 * i + 2, :])
            w_pa = t["w_proj_ssm"][0].rearrange("(k p) c -> p k c", p=P)
            for j in range(2):
                for i in range(2):
                    load(LD_PA + 2 * j + i, w_pa[:, 2 * i:2 * i + 2, j * HALF:(j + 1) * HALF])
            with sp.Fori(0, HEADS) as h:
                for i in range(2):
                    n = LD_RET + i
                    load(n, w_in[:, 4 * i:4 * i + 4, bass.ds(COL_G + h * DV, DV)], k=4,
                         waits=(h * 6 + (n - 1), n % 2))
                for i in range(4):
                    n = LD_RET + 2 + i
                    sp.wait_ge(w_ready, h * 6 + (n - 1))
                    dst = stage[:, n % 2, :].rearrange("p (k c) -> p k c", k=2)
                    for d0, c0, w in ((0, COL_Q, DK), (DK, COL_K, DK), (2 * DK, COL_V, DV)):
                        sp.dma_start(dst[:, :, d0:d0 + w], w_in[:, 2 * i:2 * i + 2, bass.ds(c0 + h * w, w)])\
                          .then_inc(raw_qkv[n % 2], 16)
            w_pb = t["w_proj_ret"][0].rearrange("(k p) c -> p k c", p=P)
            w_o = t["w_out"][0].rearrange("(k p) c -> p k c", p=P)
            for base, w in ((LD_PB, w_pb), (LD_OUT, w_o)):
                for j in range(2):
                    for i in range(4):
                        load(base + 4 * j + i, w[:, 2 * i:2 * i + 2, j * HALF:(j + 1) * HALF])
            w_up = t["w_up"][0].rearrange("(k p) c -> p k c", p=P)
            w_dn = t["w_down"][0].rearrange("(k p) c -> p k c", p=P)
            with sp.Fori(0, N_FB) as f:
                for i in range(4):
                    n = LD_MLP + i
                    load(n, w_up[:, 2 * i:2 * i + 2, bass.ds(f * FB, FB)], waits=(f * 8 + (n - 1), n % 2))
                for i in range(4):
                    n = LD_MLP + 4 + i
                    load(n, w_dn[:, bass.ds(f * (FB // P) + i, 1), :], k=1, waits=(f * 8 + (n - 1), n % 2))
            sp.wait_ge(w_ready, LD_MLP + 8 * N_FB)
            nfin = t["norm_final"]
            sp.dma_start(nf, bass.AP(tensor=nfin.tensor, offset=0, ap=[[0, P], [1, D]])).then_inc(nf_in, 16)
            for c in range(NCH):
                sp.wait_ge(f_done, c + 1)
                sp.dma_start(out_rows[:, c, :], h_res[:, c, :]).then_inc(stored, 16)
            sp.wait_ge(stored, 16 * NCH)

        @block.gpsimd
        def _(pool):
            def split(ready, count, s, slot, u0, n_done, freed=None):
                if freed is not None:
                    pool.wait_ge(out_ready, freed)
                pool.wait_ge(ready, count)
                if not isinstance(n_done, int):
                    pool.sem_inc(tick_pool, 1)
                dst_hi = w_hi[:, slot, u0:u0 + 2, :].rearrange("p k c -> p (k c)")
                dst_lo = w_lo[:, slot, u0:u0 + 2, :].rearrange("p k c -> p (k c)")
                nc.gpsimd.tensor_copy(dst_hi, stage[:, s, :]).then_inc(hi_pool, 1)
                pool.wait_ge(hi_pool, n_done)
                nc.gpsimd.tensor_tensor(dst_lo, stage[:, s, :], dst_hi.bitcast(F32), ALU.subtract)\
                  .then_inc(w_ready, 1)

            def regular(n, gr, i, seen, freed):
                split(raw[n % 2], 16 * (seen + 1), n % 2, gr % 2, 2 * i, n + 1, freed=freed if i == 0 else None)

            for i in range(4):
                regular(LD_U + i, GR_U, i, i // 2, None)
            with pool.Fori(0, MT) as b:
                for i in range(4):
                    n = LD_GATE + i
                    freed = b * 8 + (OUT_GATE - 4 if i < 2 else OUT_GATE)
                    split(raw[n % 2], b * 32 + 16 * (n // 2 + 1), n % 2, (GR_GATE + i // 2) % 2, 2 * (i % 2),
                          b * 4 + (n + 1), freed=freed if i % 2 == 0 else None)
            for i in range(2):
                regular(LD_GLU + i, GR_GLU, i, (LD_GLU + i) // 2, OUT_GLU - 4)
            for j in range(2):
                for i in range(2):
                    n = LD_PA + 2 * j + i
                    regular(n, GR_PA + j, i, n // 2, OUT_GLU + 8 * j)
            with pool.Fori(0, HEADS) as h:
                for i in range(2):
                    n = LD_RET + i
                    split(raw[n % 2], h * 16 + 16 * (LD_RET // 2 + 1), n % 2, GR_RET % 2, 2 * i, h * 6 + (n + 1),
                          freed=h * 16 + (OUT_RET - 8) if i == 0 else None)
                for i in range(4):
                    n = LD_RET + 2 + i
                    split(raw_qkv[n % 2], h * 96 + 48 * (i // 2 + 1), n % 2, (GR_RET + 1) % 2, 2 * i, h * 6 + (n + 1),
                          freed=h * 16 + OUT_RET if i == 0 else None)
            g_slot = LD_RET // 2 + HEADS
            for base, gr in ((LD_PB, GR_PB), (LD_OUT, GR_OUT)):
                for j in range(2):
                    for i in range(4):
                        n = base + 4 * j + i
                        regular(n, gr + j, i, g_slot + (n - LD_PB) // 2, OUT_PB + 8 * (gr + j - GR_PB) - 8)
            with pool.Fori(0, N_FB) as f:
                for b in range(2):
                    for i in range(4):
                        n = LD_MLP + 4 * b + i
                        split(raw[n % 2], f * 64 + 16 * (g_slot + (n - LD_PB) // 2 + 1), n % 2, (GR_MLP + b) % 2,
                              2 * i, f * 8 + (n + 1), freed=f * 24 + (OUT_MLP - 8 + 8 * b) if i == 0 else None)

        @block.tensor
        def _(pe):
            def three(out, s_hi, s_lo, m_hi_, m_lo_, first, last):
                nc.tensor.matmul(out, s_hi, m_hi_, start=first, stop=False)
                nc.tensor.matmul(out, s_hi, m_lo_, start=False, stop=False)
                return nc.tensor.matmul(out, s_lo, m_hi_, start=False, stop=last)

            def wait_bank(n):
                pe.wait_ge(out_free, n - 3)

            def features(n, slot, units, col, a_hi, a_lo, half, w_wait=None):
                if n >= 4:
                    wait_bank(n)
                for k in range(units):
                    if w_wait is not None and k % 2 == 0:
                        pe.wait_ge(w_ready, w_wait + k // 2)
                    mm = three(acc[:, n % 4, :], w_hi[:, slot, k, col:col + P], w_lo[:, slot, k, col:col + P],
                               a_hi[:, k, half * HALF:(half + 1) * HALF], a_lo[:, k, half * HALF:(half + 1) * HALF],
                               k == 0, k == units - 1)
                mm.then_inc(out_ready, 1)
                return mm

            def quad(n0, slot, units, a_hi, a_lo, half, w_wait, a_wait=None, hooks={}):
                for k in range(units):
                    if k % 2 == 0:
                        pe.wait_ge(w_ready, w_wait + k // 2)
                    if a_wait is not None:
                        pe.wait_ge(lo_done, a_wait + k)
                    for m in range(4):
                        if k == 0 and n0 >= 4:
                            wait_bank(n0 + m)
                        mm = three(acc[:, (n0 + m) % 4, :], w_hi[:, slot, k, m * P:(m + 1) * P],
                                   w_lo[:, slot, k, m * P:(m + 1) * P], a_hi[:, k, half * HALF:(half + 1) * HALF],
                                   a_lo[:, k, half * HALF:(half + 1) * HALF], k == 0, k == units - 1)
                        if k == units - 1:
                            mm.then_inc(out_ready, 1)
                    if k in hooks:
                        turn_x(hooks[k])

            def turn_x(c):
                pe.wait_ge(diag_made, c + 1)
                for b in range(2):
                    n = 2 * c + b
                    if n >= 4:
                        pe.wait_ge(z_normed, n - 3)
                    for q in range(4):
                        k = 4 * b + q
                        mm = nc.tensor.matmul(aux[:, n % 4, q * P:(q + 1) * P], x_in[:, c, k * P:(k + 1) * P],
                                              diag1[:, c % 2, :], start=True, stop=True)
                    mm.then_inc(z_turned, 1)

            for c in range(5):
                turn_x(c)

            pe.wait_ge(lo_done, SP_Z + 8)
            quad(OUT_U, GR_U % 2, KT, z_hi, z_lo, 0, LD_U + 1, hooks={1: 5, 2: 6, 4: 7})
            for m in range(MT):
                if m == 0:
                    pe.wait_ge(lo_done, SP_Z + 16)
                features(OUT_U + MT + m, GR_U % 2, KT, m * P, z_hi, z_lo, 1)

            pe.wait_ge(par_in, 16 * 16)
            pe.wait_ge(z_normed, 2 * NCH)
            for ri in range(2):
                for m in range(MT):
                    mm = nc.tensor.transpose(aux[:, ri, m * P:(m + 1) * P], c_raw[:, ri, m, :], ident[:])
            mm.then_inc(ct_turned, 1)

            def batch(b, last):
                def gate(o):
                    d, half = o // 2, o % 2
                    n = OUT_GATE + o
                    slot = (GR_GATE + o // 4) % 2
                    wg = [w[:, slot, 0:4, :].rearrange("p u (a c) -> p (u a) c", a=2) for w in (w_hi, w_lo)]
                    cs = slice(d % 2 * P, (d % 2 + 1) * P)
                    pe.wait_ge(out_free, b * 8 + (n - 3))
                    for k in range(KT):
                        if o % 4 == 0 and k % 4 == 0:
                            pe.wait_ge(w_ready, b * 4 + (LD_GATE + o // 4 * 2 + k // 4 + 1))
                        mm = three(acc[:, n % 4, :], wg[0][:, k, cs], wg[1][:, k, cs],
                                   z_hi[:, k, half * HALF:(half + 1) * HALF],
                                   z_lo[:, k, half * HALF:(half + 1) * HALF], k == 0, k == KT - 1)
                    mm.then_inc(out_ready, 1)

                def turn_ab():
                    pe.wait_ge(prep, b + 1)
                    for ri, src in enumerate((abr, abi)):
                        for q in range(QP):
                            mm = nc.tensor.transpose(aux[:, ri, q * P:(q + 1) * P],
                                                     src[:, q, :, :].rearrange("p t c -> p (t c)"), ident[:])
                    mm.then_inc(ab_turned, 1)

                def impulse():
                    for g in range(GB):
                        q, gp = g // 2, g % 2
                        rows = slice(gp * STATE, (gp + 1) * STATE)
                        out = aux[0:CH, 2 + gp, q * P:(q + 1) * P]
                        nc.tensor.matmul(out, abr[rows, q, T - 1, :],
                                         car[rows, q, 0:T, :].rearrange("p t c -> p (t c)"), start=True, stop=False)
                        mm = nc.tensor.matmul(out, abi[rows, q, T - 1, :],
                                              can[rows, q, 0:T, :].rearrange("p t c -> p (t c)"),
                                              start=False, stop=True)
                    mm.then_inc(kern, 1)

                def add_state():
                    pe.wait_ge(ab_ready, b + 1)
                    pe.wait_ge(u_blk_in, b * 128 + 128)
                    for g in range(GB):
                        q, gp = g // 2, g % 2
                        for ri in range(2):
                            mm = nc.tensor.matmul(aux[gp * STATE:(gp + 1) * STATE, ri, q * P:(q + 1) * P],
                                                  abt[:, ri, q, gp * STATE:(gp + 1) * STATE], u_blk[:, g, :],
                                                  start=True, stop=True)
                    mm.then_inc(x_state, 1)

                def outputs():
                    pe.wait_ge(scanned, b + 1)
                    pe.wait_ge(toep_in, b * 112 + 112)
                    for g in range(GB):
                        q, gp = g // 2, g % 2
                        rows = slice(gp * STATE, (gp + 1) * STATE)
                        out = aux[:, 2 + gp, q * P:(q + 1) * P]
                        nc.tensor.matmul(out, toep[:, gp * QP + q, :], u_blk[:, g, :], start=True, stop=False)
                        nc.tensor.matmul(out, car[rows, q, 1:T + 1, :].rearrange("p t c -> p (t c)"),
                                         hst[rows, 0, q, 0:NT], start=False, stop=False)
                        mm = nc.tensor.matmul(out, can[rows, q, 1:T + 1, :].rearrange("p t c -> p (t c)"),
                                              hst[rows, 1, q, 0:NT], start=False, stop=True)
                    mm.then_inc(y_prod, 1)

                for o in range(8):
                    gate(o)
                    if o == 0:
                        turn_ab()
                    if o == 1:
                        add_state()
                        impulse()
                    if o == (5 if last else 6):
                        outputs()

            pe.wait_ge(ct_ready, 1)
            with pe.Fori(0, MT - 1) as b:
                batch(b, False)
            batch(MT - 1, True)

            quad(OUT_GLU, GR_GLU % 2, MT, y_hi, y_lo, 0, LD_GLU + 1, a_wait=SP_Y + 1)
            for m in range(MT):
                features(OUT_GLU + MT + m, GR_GLU % 2, MT, m * P, y_hi, y_lo, 1)
            for j in range(2):
                for half in range(2):
                    for d in range(4):
                        n = OUT_PA + 8 * j + 4 * half + d
                        if j == 0 and d == 0:
                            pe.wait_ge(lo_done, SP_YA + 4 * (half + 1))
                        features(n, (GR_PA + j) % 2, MT, d * P, y_hi, y_lo, half,
                                 w_wait=LD_PA + 2 * j + 1 if half == 0 and d == 0 else None)

            sg, sq = GR_RET % 2, (GR_RET + 1) % 2
            wg_hi = w_hi[:, sg, 0:4, :].rearrange("p u (a c) -> p (u a) c", a=2)
            wg_lo = w_lo[:, sg, 0:4, :].rearrange("p u (a c) -> p (u a) c", a=2)

            def g_part(h, c, k):
                n = OUT_RET + c
                if k == 0:
                    pe.wait_ge(out_free, h * 16 + (n - 3))
                if c == 0 and k % 4 == 0:
                    pe.wait_ge(w_ready, h * 6 + (LD_RET + k // 4 + 1))
                mm = three(acc[:, n % 4, 0:DV], z_hi[:, k, c * P:(c + 1) * P], z_lo[:, k, c * P:(c + 1) * P],
                           wg_hi[:, k, :], wg_lo[:, k, :], k == 0, k == KT - 1)
                if k == KT - 1:
                    mm.then_inc(out_ready, 1)

            def qkv_part(h, c, k):
                n = OUT_RET + NCH + c
                if k == 0:
                    pe.wait_ge(out_free, h * 16 + (n - 3))
                if c == 0 and k % 2 == 0:
                    pe.wait_ge(w_ready, h * 6 + (LD_RET + 2 + k // 2 + 1))
                mm = three(acc[:, n % 4, :], z_hi[:, k, c * P:(c + 1) * P], z_lo[:, k, c * P:(c + 1) * P],
                           w_hi[:, sq, k, :], w_lo[:, sq, k, :], k == 0, k == KT - 1)
                if k == KT - 1:
                    mm.then_inc(out_ready, 1)

            def head(h, more):
                def cnt(c):
                    return h * 8 + (c + 1)

                def turn_qk(c):
                    pe.wait_ge(rotated, cnt(c))
                    if c >= 2:
                        pe.wait_ge(yb_stored, cnt(c - 2))
                    nc.tensor.transpose(aux[:, 0, 0:P], rot[:, 0, :, :].rearrange("p a b -> p (a b)"), ident[:])
                    nc.tensor.transpose(aux[:, 0, P:2 * P], kvk[:, c % 2, :], ident[:]).then_inc(qk_turned, 1)

                def score(c):
                    pe.wait_ge(qkt_ready, cnt(c))
                    nc.tensor.matmul(aux[:, 1, 0:P], qkt[:, 1, :], qkt[:, 0, :], start=True, stop=True)\
                      .then_inc(scores, 1)
                    if c >= 1:
                        pe.wait_ge(state_ready, cnt(c - 1))
                    nc.tensor.matmul(aux[:, 3, 0:DV], kvk[:, c % 2, :], vv[:, c % 2, :], start=True, stop=True)\
                      .then_inc(kv_ready, 1)

                def attend(c):
                    pe.wait_ge(prob_ready, cnt(c))
                    if c >= 1:
                        pe.wait_ge(yb_ready, cnt(c - 1))
                    mm = nc.tensor.matmul(aux[:, 2, 0:DV], prob[:], vv[:, c % 2, :], start=True, stop=(c == 0))
                    if c >= 1:
                        mm = nc.tensor.matmul(aux[:, 2, 0:DV], qkt[:, 0, :], state[:], start=False, stop=True)
                    mm.then_inc(o_ready, 1)

                def turn_yb(c):
                    pe.wait_ge(yb_ready, cnt(c))
                    for e in range(2):
                        mm = nc.tensor.transpose(aux[:, 0, e * P:(e + 1) * P], yb[:, e * P:(e + 1) * P], ident[:])
                    mm.then_inc(yb_turned, 1)

                for s in range(NCH + 3):
                    for k in range(KT):
                        if s < NCH:
                            qkv_part(h, s, k)
                        elif more:
                            for i in (2 * k, 2 * k + 1):
                                c = 2 * (s - NCH) + i // KT
                                g_part(h + 1, c, i % KT)
                        if k == 0 and s >= 3:
                            turn_yb(s - 3)
                        if k == 1 and 2 <= s <= NCH + 1:
                            attend(s - 2)
                        if k == 4 and 1 <= s <= NCH:
                            turn_qk(s - 1)
                        if k == 6 and 1 <= s <= NCH:
                            score(s - 1)
                if more:
                    for c in (6, 7):
                        for k in range(KT):
                            g_part(h + 1, c, k)

            for c in range(NCH):
                for k in range(KT):
                    g_part(0, c, k)
            with pe.Fori(0, HEADS - 1) as h:
                head(h, True)
            head(HEADS - 1, False)

            for j in range(2):
                for d in range(4):
                    for half in range(2):
                        n = OUT_PB + 8 * j + 2 * d + half
                        slot = (GR_PB + j) % 2
                        wait_bank(n)
                        for k in range(KT):
                            if n == OUT_PB:
                                pe.wait_ge(lo_done, SP_YB + k + 1)
                            if d == 0 and half == 0 and k % 2 == 0:
                                pe.wait_ge(w_ready, LD_PB + 4 * j + k // 2 + 1)
                            mm = three(acc[:, n % 4, :], w_hi[:, slot, k, d * P:(d + 1) * P],
                                       w_lo[:, slot, k, d * P:(d + 1) * P], z_hi[:, k, half * HALF:(half + 1) * HALF],
                                       z_lo[:, k, half * HALF:(half + 1) * HALF], k == 0, k == KT - 1)
                        mm.then_inc(out_ready, 1)

            def turn_z2(c):
                pe.wait_ge(diag2_made, c + 1)
                for b in range(2):
                    n = 2 * c + b
                    if n >= 4:
                        pe.wait_ge(z2_normed, n - 3)
                    for q in range(4):
                        k = 4 * b + q
                        mm = nc.tensor.matmul(aux[:, n % 4, q * P:(q + 1) * P], h_res[:, c, k * P:(k + 1) * P],
                                              diag2[:], start=True, stop=True)
                    mm.then_inc(z2_turned, 1)

            for j in range(2):
                for c in range(NCH):
                    n = OUT_OUT + 8 * j + c
                    slot = (GR_OUT + j) % 2
                    wait_bank(n)
                    for k in range(KT):
                        if n == OUT_OUT:
                            pe.wait_ge(lo_done, SP_M + 2 * k + 2)
                        if c == 0 and k % 2 == 0:
                            pe.wait_ge(w_ready, LD_OUT + 4 * j + k // 2 + 1)
                        mm = three(acc[:, n % 4, :], m_hi[:, k, c * P:(c + 1) * P], m_lo[:, k, c * P:(c + 1) * P],
                                   w_hi[:, slot, k, :], w_lo[:, slot, k, :], k == 0, k == KT - 1)
                        if j == 1 and c >= 1 and k == 5:
                            turn_z2(c - 1)
                    mm.then_inc(out_ready, 1)
            turn_z2(NCH - 1)

            with pe.Fori(0, N_FB) as f:
                pe.wait_ge(lo_done, SP_Z2 + 8)
                for half in range(2):
                    for q in range(FB // P):
                        n = OUT_MLP + 4 * half + q
                        slot = GR_MLP % 2
                        if half == 1 and q == 0:
                            pe.wait_ge(lo_done, SP_Z2 + 16)
                        pe.wait_ge(out_free, f * 24 + (n - 3))
                        for k in range(KT):
                            if half == 0 and q == 0 and k % 2 == 0:
                                pe.wait_ge(w_ready, f * 8 + (LD_MLP + k // 2 + 1))
                            mm = three(acc[:, n % 4, :], w_hi[:, slot, k, q * P:(q + 1) * P],
                                       w_lo[:, slot, k, q * P:(q + 1) * P], m_hi[:, k, half * HALF:(half + 1) * HALF],
                                       m_lo[:, k, half * HALF:(half + 1) * HALF], k == 0, k == KT - 1)
                        mm.then_inc(out_ready, 1)
                for j in range(2):
                    for c in range(NCH):
                        n = OUT_MLP + 8 + 8 * j + c
                        slot = (GR_MLP + 1) % 2
                        pe.wait_ge(out_free, f * 24 + (n - 3))
                        if j == 0 and c % 4 == 0:
                            pe.wait_ge(lo_done, f * 8 + (SP_HID + c + 4))
                        for q in range(FB // P):
                            if j == 0 and c == 0:
                                pe.wait_ge(w_ready, f * 8 + (LD_MLP + 4 + q + 1))
                            mm = three(acc[:, n % 4, :], hid_hi[:, q, c * P:(c + 1) * P],
                                       hid_lo[:, q, c * P:(c + 1) * P], w_hi[:, slot, 2 * q + j, :],
                                       w_lo[:, slot, 2 * q + j, :], q == 0, q == FB // P - 1)
                        mm.then_inc(out_ready, 1)

        @block.scalar
        def _(act):
            def hi_split(dst, src):
                nc.scalar.activation(dst, src, ACT.Copy).then_inc(hi_done, 1)

            def square_x(c):
                act.wait_ge(x_ready[c], 16)
                if c >= 1:
                    act.wait_ge(ss_done, c)
                nc.scalar.activation(x_junk[:], x_in[:, c, :], ACT.Square, accum_out=ss1[:, c:c + 1])\
                  .then_inc(ss_done, 1)

            for c in range(4):
                square_x(c)
            for c in range(NCH):
                for b in range(2):
                    n = 2 * c + b
                    act.wait_ge(z_normed, n + 1)
                    hi_split(z_hi[:, 4 * b:4 * b + 4, c * P:(c + 1) * P],
                             z_tmp[:, n % 4, :].rearrange("p (k s) -> p k s", k=4))
                if c in (0, 2):
                    square_x(c + 4)
                    square_x(c + 5)
            for n in range(8):
                half, m = n // MT, n % MT
                act.wait_ge(out_ready, OUT_U + n + 1)
                w = NT // 2
                ch_ins = nc.scalar.activation(u_all[:, m, :, half * w:(half + 1) * w],
                                              acc[:, n % 4, :].rearrange("p (c j) -> p j c", j=T), ACT.Copy)
                ch_ins.then_inc(out_free, 1)
                if half == 1:
                    act.wait_ge(out_free, OUT_U + n + 1)
                    act.dma_start(u_dram[m], u_all[:, m, :, :]).then_inc(u_out, 16)
            act.wait_ge(ct_turned, 1)
            for ri, dst in enumerate((ctr, cti)):
                for gp in range(2):
                    rows = slice(gp * STATE, (gp + 1) * STATE)
                    src = aux[rows, ri, :].rearrange("p (m q e c) -> p m q e c", q=QP, e=2, c=CH)[:, :, :, gp, :]
                    ins = nc.scalar.activation(dst[rows, :, :].rearrange("p (m q) c -> p m q c", m=MT), src, ACT.Copy)
                    ins.then_inc(ct_ready, 1) if ri == 1 and gp == 1 else None
            act.wait_ge(u_out, 16 * MT)
            def load_u(b):
                for j in range(T):
                    act.dma_start(u_blk[j * CH:(j + 1) * CH, :, :],
                                  u_dram[bass.ds(b, 1), :, j, :].rearrange("a (g c) n -> (a c) g n", c=CH))\
                       .then_inc(u_blk_in, 16)

            def batch(b, last):
                def gate(o):
                    d, half = o // 2, o % 2
                    act.wait_ge(out_ready, b * 8 + (OUT_GATE + o + 1))
                    if o >= 2:
                        act.wait_ge(gate_sent[o % 2], b * 64 + 16 * (o // 2))
                    nc.scalar.activation(gate_t[:, o % 2, :], acc[:, o % 4, :], ACT.Sigmoid).then_inc(out_free, 1)
                    act.wait_ge(out_free, b * 8 + (OUT_GATE + o + 1))
                    act.dma_start(gate_dram[bass.ds(b * 4 + d, 1), :, half * HALF:(half + 1) * HALF]
                                  .rearrange("a p s -> p (a s)"), gate_t[:, o % 2, :]).then_inc(gate_sent[o % 2], 16)

                def store_y():
                    act.wait_ge(y_prod, b + 1)
                    nc.scalar.activation(y_blk[:].rearrange("p (q e) s -> p e q s", e=2),
                                         aux[:, 2:4, :].rearrange("p e (q s) -> p e q s", q=QP), ACT.Copy)\
                      .then_inc(y_copied, 1)
                    act.wait_ge(y_copied, b + 1)
                    for j in range(T):
                        act.dma_start(y_dram[bass.ds(b, 1), :, j, :].rearrange("a (g c) n -> (a c) g n", c=CH),
                                      y_blk[j * CH:(j + 1) * CH, :, :]).then_inc(y_sent, 16)

                gate(0)
                act.wait_ge(ab_turned, b + 1)
                nc.scalar.activation(abt[:].rearrange("p r q s -> p r (q s)"), aux[:, 0:2, :], ACT.Copy)\
                  .then_inc(ab_ready, 1)
                gate(1)
                act.wait_ge(kern, b + 1)
                nc.scalar.activation(toep[0:CH, :, :].rearrange("p (b g) s -> p b (g s)", b=2),
                                     aux[0:CH, 2:4, :], ACT.Copy).then_inc(kern_ready, 1)
                act.wait_ge(kern_ready, b + 1)
                for j in range(1, T):
                    act.dma_start(toep[j * CH:(j + 1) * CH, :, j * CH:P], toep[0:CH, :, 0:P - j * CH])\
                       .then_inc(toep_in, 16)
                for o in range(2, 6):
                    gate(o)
                if last:
                    store_y()
                    act.wait_ge(y_done, MT - 1)
                    for m in range(MT - 1):
                        hi_split(y_hi[:, m, :], y_raw[:, m, :])
                    gate(6)
                else:
                    gate(6)
                    store_y()
                    load_u(b + 1)
                act.wait_ge(y_sent, b * 128 + 128)
                act.dma_start(y_blk[:].rearrange("p g s -> p (g s)"),
                              y_dram[bass.ds(b, 1)].rearrange("a p j n -> (a p) (j n)")).then_inc(y_back, 16)
                act.dma_start(u_back[:], u_dram[bass.ds(b, 1)].rearrange("a p j n -> (a p) (j n)"))\
                   .then_inc(y_back, 16)
                gate(7)
                for s in range(2):
                    act.wait_ge(gate_sent[s], b * 64 + 64)
                act.wait_ge(gelu_arg, b + 1)
                nc.scalar.activation(tb[:], ta[:], ACT.Sigmoid, scale=1.5957691216057308).then_inc(gelu_sig, 1)

            load_u(0)
            with act.Fori(0, MT - 1) as b:
                batch(b, False)
            batch(MT - 1, True)
            act.wait_ge(y_done, MT)
            hi_split(y_hi[:, MT - 1, :], y_raw[:, MT - 1, :])
            for half in range(2):
                for m in range(MT):
                    n = half * MT + m
                    act.wait_ge(out_ready, OUT_GLU + n + 1)
                    if half == 1:
                        act.wait_ge(out_free, OUT_GLU + m + 1)
                    nc.scalar.activation(glu_s[:, m, :], acc[:, n % 4, :], ACT.Sigmoid, bias=bglu[:, m:m + 1])\
                      .then_inc(glu_sig, 1)
                act.wait_ge(out_ready, OUT_GLU + MT * (half + 1))
                for m in range(MT):
                    n = half * MT + m
                    act.wait_ge(out_free, OUT_GLU + n + 1)
                    hi_split(y_hi[:, m, half * HALF:(half + 1) * HALF], y_raw[:, m, half * HALF:(half + 1) * HALF])
            act.dma_start(rope[:], t["rope"].rearrange("(c p) f -> p c f", p=P)).then_inc(ret_in, 16)
            act.dma_start(gam[:], t["gam"]).then_inc(ret_in, 16)
            act.dma_start(mask[:], t["mask"]).then_inc(ret_in, 16)
            order = [(j, half, d) for j in range(2) for half in range(2) for d in range(4)]

            def load_ga(n):
                j, half, d = order[n]
                act.dma_start(ga_t[:, n % 2, :], gate_dram[4 * j + d, :, half * HALF:(half + 1) * HALF])\
                   .then_inc(ga_in[n % 2], 16)

            load_ga(0)
            load_ga(1)
            for n, (j, half, d) in enumerate(order):
                act.wait_ge(out_free, OUT_PA + n + 1)
                act.dma_start(ma_dram[4 * j + d, :, half * HALF:(half + 1) * HALF], ga_t[:, n % 2, :])\
                   .then_inc(ma_sent[n % 2], 16)
                if n + 2 < len(order):
                    act.wait_ge(ma_sent[n % 2], 16 * (n // 2 + 1))
                    load_ga(n + 2)
            act.wait_ge(lo_done, SP_YA + 8)
            act.wait_ge(ret_in, 48)

            def g_sigmoid(h, c):
                n = OUT_RET + c
                act.wait_ge(out_ready, h * 16 + (n + 1))
                act.wait_ge(out_free, h * 16 + (n - 1))
                nc.scalar.activation(sig_t[:, c % 2, :], acc[:, n % 4, 0:DV], ACT.Sigmoid).then_inc(sig_g, 1)

            def head(h, more):
                def cnt(c):
                    return h * 8 + (c + 1)

                def take_qkv(c):
                    n = OUT_RET + NCH + c
                    act.wait_ge(out_ready, h * 16 + (n + 1))
                    act.sem_inc(tick_act, 1)
                    nc.scalar.activation(qk[:, c % 2, 0, :], acc[:, n % 4, 0:DK], ACT.Copy,
                                         scale=gam[:, bass.ds(h, 1)])
                    nc.scalar.activation(qk[:, c % 2, 1, :], acc[:, n % 4, DK:2 * DK], ACT.Copy,
                                         scale=gam[:, bass.ds(h + HEADS, 1)])
                    nc.scalar.activation(vv[:, c % 2, :], acc[:, n % 4, 2 * DK:], ACT.Copy).then_inc(out_free, 1)

                def take_yb(c):
                    act.wait_ge(yb_turned, cnt(c))
                    act.sem_inc(tick_act, 1)
                    nc.scalar.activation(yb_raw[:, bass.ds(h * 2, 2), c * P:(c + 1) * P],
                                         aux[:, 0, 0:2 * P].rearrange("p (e s) -> p e s", e=2), ACT.Copy)\
                      .then_inc(yb_stored, 1)

                def square_o(c):
                    act.wait_ge(o_ready, cnt(c))
                    nc.scalar.activation(o_junk[:], aux[:, 2, 0:DV], ACT.Square, accum_out=oss[:, c % 2:c % 2 + 1])\
                      .then_inc(o_ss, 1)

                def take_qkt(c):
                    act.wait_ge(qk_turned, cnt(c))
                    nc.scalar.activation(qkt[:].rearrange("p a s -> p (a s)"), aux[:, 0, 0:2 * P], ACT.Copy)\
                      .then_inc(qkt_ready, 1)

                act.wait_ge(out_free, h * 16 + (OUT_RET + NCH))
                for s in range(1, NCH + 4):
                    if s <= NCH:
                        take_qkv(s - 1)
                    if s >= 3 and s - 3 < NCH:
                        take_yb(s - 3)
                    if 2 <= s <= NCH + 1:
                        square_o(s - 2)
                    if more and s >= NCH and s < NCH + 3:
                        g_sigmoid(h + 1, 2 * (s - NCH))
                    if s <= NCH:
                        take_qkt(s - 1)
                    if more and s >= NCH:
                        for c in ((2 * (s - NCH) + 1,) if s < NCH + 3 else (6, 7)):
                            g_sigmoid(h + 1, c)

            for c in range(NCH):
                g_sigmoid(0, c)
            for s in range(2):
                act.wait_ge(ma_sent[s], 16 * len(order) // 2)
            with act.Fori(0, HEADS - 1) as h:
                head(h, True)
            head(HEADS - 1, False)
            act.wait_ge(out_ready, OUT_PB)
            act.wait_ge(yb_stored, NCH * HEADS)
            for k in range(KT):
                hi_split(z_hi[:, k, :], yb_raw[:, k, :])
            act.wait_ge(lo_done, SP_YB + KT)
            act.dma_start(nmlp[:], t["norm_mlp"].rearrange("a (k p) -> p (a k)", p=P), allow_slow_non_contiguous=True).then_inc(nmlp_in, 16)

            def block_of(n):
                return n // 2, n % 2

            def load_gb(n):
                d, half = block_of(n)
                act.dma_start(gb_t[:, n % 2, :], gate_dram[KT + d, :, half * HALF:(half + 1) * HALF])\
                   .then_inc(gb_in[n % 2], 16)

            def load_ma(n):
                d, half = block_of(n)
                act.dma_start(ma_t[:], ma_dram[d, :, half * HALF:(half + 1) * HALF]).then_inc(ma_in, 16)

            load_gb(0)
            load_gb(1)
            load_ma(0)
            for n in range(16):
                d, half = block_of(n)
                act.wait_ge(merged, n + 1)
                if n + 1 < 16:
                    load_ma(n + 1)
                hi_split(m_hi[:, d, half * HALF:(half + 1) * HALF], gb_t[:, n % 2, :])
                if n + 2 < 16:
                    act.wait_ge(lo_done, SP_M + n + 1)
                    load_gb(n + 2)
            act.wait_ge(out_ready, OUT_OUT)
            act.wait_ge(lo_done, SP_M + 16)
            for c in range(NCH):
                act.dma_start(h_res[:, c, :], x_rows[:, c, :]).then_inc(xr_in[c], 16)

            for c in range(NCH):
                act.wait_ge(out_free, OUT_OUT + NCH + c + 1)
                if c >= 1:
                    act.wait_ge(h_ss, c)
                nc.scalar.activation(h_junk[:], h_res[:, c, :], ACT.Square, accum_out=ss2[:, c:c + 1]).then_inc(h_ss, 1)
                for b in range(2):
                    n = 2 * c + b
                    act.wait_ge(z2_normed, n + 1)
                    hi_split(m_hi[:, 4 * b:4 * b + 4, c * P:(c + 1) * P],
                             z2_tmp[:, b, :].rearrange("p (k s) -> p k s", k=4))
            act.wait_ge(lo_done, SP_Z2 + 16)

            def mlp_block(f):
                act.wait_ge(out_free, f * 24 + OUT_MLP)
                for n in range(8):
                    half, q = n // 4, n % 4
                    act.wait_ge(out_ready, f * 24 + (OUT_MLP + n + 1))
                    act.wait_ge(lo_done, f * 8 + (SP_HID + n - 1))
                    nc.scalar.activation(relu[:, n % 2, :], acc[:, n % 4, :], ACT.Relu).then_inc(out_free, 1)
                    if n >= 1:
                        hidden_hi(f, n - 1)
                hidden_hi(f, 7)

            def hidden_hi(f, n):
                half, q = n // 4, n % 4
                act.wait_ge(squared, f * 8 + (n + 1))
                act.wait_ge(out_ready, f * 24 + (OUT_MLP - 4 + 4 * half))
                hi_split(hid_hi[:, q, half * HALF:(half + 1) * HALF], relu[:, n % 2, :])

            with act.Fori(0, N_FB) as f:
                mlp_block(f)
            for c in range(NCH):
                act.wait_ge(out_free, OUT_MLP + 24 * (N_FB - 1) + 16 + c + 1)
                if c >= 1:
                    act.wait_ge(f_ss, c)
                nc.scalar.activation(h_junk[:], h_res[:, c, :], ACT.Square, accum_out=ss2[:, c:c + 1])\
                  .then_inc(f_ss, 1)

        @block.vector
        def _(dve):
            ch = Chain(dve, chain_v)
            link = ch.link
            V = nc.vector

            def lo_split(dst, src, hi):
                V.tensor_tensor(dst, src, hi.bitcast(F32), ALU.subtract).then_inc(lo_done, 1)

            def rstd(dst, a, width):
                w = dst.shape[-1]
                bits, (tmp, m, y, y2) = rs_bits[:, 0:w], [rs_tmp[:, i, 0:w] for i in range(4)]
                V.tensor_scalar(m, a, -0.5 / width, -0.5 * EPS, ALU.mult, ALU.add)
                link(V.tensor_scalar(tmp, a, 1.0 / width, EPS, ALU.mult, ALU.add))
                link(V.tensor_scalar(bits, tmp.bitcast(I32), 1, None, ALU.arith_shift_right))
                link(V.tensor_scalar(y.bitcast(I32), bits, -1.0, 1597463007.0, ALU.mult, ALU.add))
                for step in range(3):
                    if w == 1:
                        link(V.scalar_tensor_tensor(out=y2, in0=y, scalar=m, in1=y, op0=ALU.mult, op1=ALU.mult))
                    else:
                        link(V.tensor_tensor(y2, y, y, ALU.mult))
                        link(V.tensor_tensor(y2, y2, m, ALU.mult))
                    link(V.scalar_tensor_tensor(out=dst if step == 2 else y, in0=y2, scalar=1.5, in1=y,
                                                op0=ALU.add, op1=ALU.mult))

            def rstd_x(p):
                dve.wait_ge(ss_done, 2 * p + 2)
                rstd(rs1[:, 2 * p:2 * p + 2], ss1[:, 2 * p:2 * p + 2], D)

            def diag_x(c):
                V.tensor_scalar(diag1[:, c % 2, :], ident[:], rs1[:, c:c + 1], None, ALU.mult).then_inc(diag_made, 1)

            def norm_z(c):
                for b in range(2):
                    n = 2 * c + b
                    dve.wait_ge(z_turned, n + 1)
                    if n >= 4:
                        dve.wait_ge(lo_done, SP_Z + n - 3)
                    V.tensor_tensor(z_tmp[:, n % 4, :].rearrange("p (k s) -> p k s", k=4),
                                    aux[:, n % 4, :].rearrange("p (k s) -> p k s", k=4),
                                    nmix[:, 4 * b:4 * b + 4].unsqueeze(2).broadcast_to([P, 4, P]), ALU.mult)\
                     .then_inc(z_normed, 1)

            def lo_z(c):
                for b in range(2):
                    n = 2 * c + b
                    dve.wait_ge(hi_done, SP_Z + n + 1)
                    lo_split(z_lo[:, 4 * b:4 * b + 4, c * P:(c + 1) * P],
                             z_tmp[:, n % 4, :].rearrange("p (k s) -> p k s", k=4),
                             z_hi[:, 4 * b:4 * b + 4, c * P:(c + 1) * P])

            dve.wait_ge(const_in, 32)
            rstd_x(0)
            diag_x(0)
            diag_x(1)
            rstd_x(1)
            for c in range(NCH):
                norm_z(c)
                if c + 2 < NCH:
                    diag_x(c + 2)
                if c in (1, 3):
                    rstd_x((c + 3) // 2)
                if c >= 1:
                    lo_z(c - 1)
            lo_z(NCH - 1)

            dve.wait_ge(par_in, 16 * 16)
            slot_of = {"lr": 0, "li": 1, "ls": 2}

            def cf(name):
                if name not in slot_of:
                    slot_of[name] = len(slot_of)
                return coef[:, slot_of[name], :]

            def ts(dst, src, s1, s2, o1, o2=None):
                if o2 is None:
                    link(V.tensor_scalar(dst, src, s1, None, o1))
                else:
                    link(V.tensor_scalar(dst, src, s1, s2, o1, o2))

            def tt(dst, a, b, op):
                link(V.tensor_tensor(dst, a, b, op))

            def stt(dst, a, s, b, o1, o2):
                link(V.scalar_tensor_tensor(out=dst, in0=a, scalar=s, in1=b, op0=o1, op1=o2))

            def exp(dst, src):
                x, k, r, k1, k2 = cf("ex"), cf("ek"), cf("er"), cf("ek1"), cf("ek2")
                ts(x, src, -175.0, 175.0, ALU.max, ALU.min)
                ts(k, x, 1.4426950408889634, MAGIC, ALU.mult, ALU.add)
                ts(k, k, MAGIC, None, ALU.subtract)
                stt(r, k, -LN2[0], x, ALU.mult, ALU.add)
                stt(r, k, -LN2[1], r, ALU.mult, ALU.add)
                ts(x, r, 1.0 / 5040, 1.0 / 720, ALU.mult, ALU.add)
                for c in (1.0 / 120, 1.0 / 24, 1.0 / 6, 0.5, 1.0):
                    tt(x, x, r, ALU.mult)
                    ts(x, x, c, None, ALU.add)
                tt(x, x, r, ALU.mult)
                ts(x, x, 1.0, None, ALU.add)
                ts(k1, k, 0.5, MAGIC, ALU.mult, ALU.add)
                ts(k1, k1, MAGIC, None, ALU.subtract)
                tt(k2, k, k1, ALU.subtract)
                for q, kk in enumerate((k1, k2)):
                    ts(ibits[:, q, :], kk, 127.0, 8388608.0, ALU.add, ALU.mult)
                    tt(x, x, ibits[:, q, :].bitcast(F32), ALU.mult)
                link(V.tensor_copy(dst, x))

            def sincos(s_dst, c_dst, src):
                import math
                th, k, r2, sp_, cp = cf("th"), cf("sk"), cf("r2"), cf("sp"), cf("cp")
                big = 2.0 * math.pi * 1024.0
                ts(k, src, 1.0 / big, MAGIC, ALU.mult, ALU.add)
                ts(k, k, MAGIC, None, ALU.subtract)
                first = True
                for c in parts(big, 4):
                    stt(th, k, -c, src if first else th, ALU.mult, ALU.add)
                    first = False
                ts(k, th, 2.0 / math.pi, MAGIC, ALU.mult, ALU.add)
                ts(k, k, MAGIC, None, ALU.subtract)
                for c in parts(math.pi / 2, 4):
                    stt(th, k, -c, th, ALU.mult, ALU.add)
                tt(r2, th, th, ALU.mult)
                ts(sp_, r2, -1.9515295891e-4, 8.3321608736e-3, ALU.mult, ALU.add)
                tt(sp_, sp_, r2, ALU.mult)
                ts(sp_, sp_, -1.6666654611e-1, None, ALU.add)
                tt(sp_, sp_, r2, ALU.mult)
                tt(sp_, sp_, th, ALU.mult)
                tt(sp_, sp_, th, ALU.add)
                ts(cp, r2, 2.443315711809948e-5, -1.388731625493765e-3, ALU.mult, ALU.add)
                tt(cp, cp, r2, ALU.mult)
                ts(cp, cp, 4.166664568298827e-2, None, ALU.add)
                tt(cp, cp, r2, ALU.mult)
                ts(cp, cp, -0.5, None, ALU.add)
                tt(cp, cp, r2, ALU.mult)
                ts(cp, cp, 1.0, None, ALU.add)
                f, n, sg, od = cf("qf"), cf("qn"), cf("qs"), cf("qo")
                ts(f, k, 0.25, -0.375, ALU.mult, ALU.add)
                ts(f, f, MAGIC, None, ALU.add)
                ts(f, f, MAGIC, None, ALU.subtract)
                stt(n, f, -4.0, k, ALU.mult, ALU.add)
                ts(sg, n, 2.0, None, ALU.is_ge)
                stt(od, sg, -2.0, n, ALU.mult, ALU.add)
                ts(sg, sg, -2.0, 1.0, ALU.mult, ALU.add)
                tt(f, cp, sp_, ALU.subtract)
                tt(f, f, od, ALU.mult)
                tt(n, cp, sp_, ALU.add)
                tt(n, n, od, ALU.mult)
                tt(f, sp_, f, ALU.add)
                tt(n, cp, n, ALU.subtract)
                tt(s_dst, f, sg, ALU.mult)
                tt(c_dst, n, sg, ALU.mult)

            lr, li = cf("lr"), cf("li")
            step, mag, ang = cf("step"), cf("mag"), cf("ang")
            exp(step, cf("ls"))
            tt(ang, lr, step, ALU.mult)
            exp(mag, ang)
            tt(ang, li, step, ALU.mult)
            sn, cs = cf("sn"), cf("cs")
            sincos(sn, cs, ang)
            link(V.memset(pwr[:, 0, :], 1.0))
            link(V.memset(pwi[:, 0, :], 0.0))
            tt(pwr[:, 1, :], mag, cs, ALU.mult)
            tt(pwi[:, 1, :], mag, sn, ALU.mult)
            nr, den, kr, ki, tm = cf("nr"), cf("den"), cf("kr"), cf("ki"), cf("tm")
            ts(nr, pwr[:, 1, :], 1.0, None, ALU.subtract)
            tt(den, lr, lr, ALU.mult)
            tt(tm, li, li, ALU.mult)
            tt(den, den, tm, ALU.add)
            link(V.reciprocal(den, den))
            tt(kr, nr, lr, ALU.mult)
            tt(tm, pwi[:, 1, :], li, ALU.mult)
            tt(kr, kr, tm, ALU.add)
            tt(kr, kr, den, ALU.mult)
            tt(ki, pwi[:, 1, :], lr, ALU.mult)
            tt(tm, nr, li, ALU.mult)
            tt(ki, ki, tm, ALU.subtract)
            tt(ki, ki, den, ALU.mult)

            def wide(a):
                return a.unsqueeze(2).broadcast_to([P, PAIRS, CH])

            br, bi = b_raw[:, 0, :, :], b_raw[:, 1, :, :]
            tt(bbr[:], br, wide(kr), ALU.mult)
            tt(bbi[:], bi, wide(ki), ALU.mult)
            tt(bbr[:], bbr[:], bbi[:], ALU.subtract)
            tt(bbi[:], br, wide(ki), ALU.mult)
            tt(bi, bi, wide(kr), ALU.mult)
            tt(bbi[:], bbi[:], bi, ALU.add)

            def cmul(dr, di, ar, ai, xr, xi):
                t1, t2, t3, t4 = cf("m1"), cf("m2"), cf("m3"), cf("m4")
                V.tensor_tensor(t1, ar, xr, ALU.mult)
                V.tensor_tensor(t2, ai, xi, ALU.mult)
                V.tensor_tensor(t3, ar, xi, ALU.mult)
                tt(t4, ai, xr, ALU.mult)
                V.tensor_tensor(dr, t1, t2, ALU.subtract)
                tt(di, t3, t4, ALU.add)

            for k in range(2, T + 1):
                cmul(pwr[:, k, :], pwi[:, k, :], pwr[:, k - 1, :], pwi[:, k - 1, :], pwr[:, 1, :], pwi[:, 1, :])
            for k in range(T):
                V.tensor_copy(rpr[:, k, :], pwr[:, T - 1 - k, :])
                V.tensor_copy(rpi[:, k, :], pwi[:, T - 1 - k, :])
            V.tensor_copy(p8r[:, 0, :], pwr[:, T, :])
            link(V.tensor_copy(p8i[:, 0, :], pwi[:, T, :]))
            for k in range(1, T):
                cmul(p8r[:, k, :], p8i[:, k, :], p8r[:, k - 1, :], p8i[:, k - 1, :], p8r[:, 0, :], p8i[:, 0, :])
            V.tensor_copy(p64r[:, 0, :], p8r[:, T - 1, :])
            link(V.tensor_copy(p64i[:, 0, :], p8i[:, T - 1, :]))
            for k in range(1, 4):
                cmul(p64r[:, k, :], p64i[:, k, :], p64r[:, k - 1, :], p64i[:, k - 1, :],
                     p64r[:, k - 1, :], p64i[:, k - 1, :])
            dve.wait_ge(ct_ready, 1)
            link(V.memset(toep[:].rearrange("p g s -> p (g s)"), 0.0))
            link(V.memset(hst[:, :, :, 0:1], 0.0))

            def prepare(b):
                qs = bass.ds(b * QP, QP)

                def outer(dst, x, pw, n):
                    return V.tensor_tensor(dst, x[:, qs, :].unsqueeze(2).broadcast_to([P, QP, n, CH]),
                                           pw[:, 0:n, qs].rearrange("p t q -> p q t").unsqueeze(3)
                                           .broadcast_to([P, QP, n, CH]), ALU.mult)

                t_a = ta[:, 0:QP * (T + 1) * CH].rearrange("p (q t c) -> p q t c", q=QP, c=CH)
                t_b = tb[:, 0:QP * (T + 1) * CH].rearrange("p (q t c) -> p q t c", q=QP, c=CH)
                outer(car[:], ctr, pwr, T + 1)
                outer(t_a, cti, pwi, T + 1)
                outer(can[:], ctr, pwi, T + 1)
                link(outer(t_b, cti, pwr, T + 1))
                V.tensor_tensor(car[:], car[:], t_a, ALU.subtract)
                flat = can[:].rearrange("p q t c -> p (q t c)")
                link(V.scalar_tensor_tensor(out=flat, in0=tb[:, 0:QP * (T + 1) * CH], scalar=-1.0, in1=flat,
                                            op0=ALU.mult, op1=ALU.subtract))
                t_a = ta[:, 0:QP * T * CH].rearrange("p (q t c) -> p q t c", q=QP, c=CH)
                t_b = tb[:, 0:QP * T * CH].rearrange("p (q t c) -> p q t c", q=QP, c=CH)
                outer(abr[:], bbr, rpr, T)
                outer(t_a, bbi, rpi, T)
                outer(abi[:], bbr, rpi, T)
                link(outer(t_b, bbi, rpr, T))
                V.tensor_tensor(abr[:], abr[:], t_a, ALU.subtract)
                V.tensor_tensor(abi[:], abi[:], t_b, ALU.add).then_inc(prep, 1)
                dve.wait_ge(prep, b + 1)

            def scan(b):
                q0 = b * QP
                dve.wait_ge(x_state, b + 1)
                hb = hst[:, :, :, 1:NT + 1]
                link(V.tensor_copy(hb.rearrange("p r q n -> p (r q) n"),
                                   aux[:, 0:2, :].rearrange("p r (q n) -> p (r q) n", q=QP)))
                blocks = hb.rearrange("p r q (s i) -> p r q s i", i=T)

                def mac(dst, ar, ai, x, shape, n, last=False):
                    names = "abc"[:len(shape)]
                    sizes = dict(zip(names, shape))

                    def both(buf):
                        return buf[:, 0:2 * n].rearrange(f"p (r {' '.join(names)}) -> p r {' '.join(names)}", r=2, **sizes)

                    t1, t2 = both(ta), both(tb)
                    wide_ar, wide_ai = [a.unsqueeze(1).broadcast_to([P, 2] + shape) for a in (ar, ai)]
                    V.tensor_tensor(t1, x, wide_ar, ALU.mult)
                    link(V.tensor_tensor(t2, x, wide_ai, ALU.mult))
                    V.tensor_tensor(t1[:, 0], t1[:, 0], t2[:, 1], ALU.subtract)
                    link(V.tensor_tensor(t1[:, 1], t1[:, 1], t2[:, 0], ALU.add))
                    ins = V.tensor_tensor(dst, dst, t1, ALU.add)
                    if last:
                        ins.then_inc(scanned, 1)
                    else:
                        link(ins)

                a8 = [p[:, 0, bass.ds(q0, QP)].unsqueeze(2).broadcast_to([P, QP, SUP]) for p in (p8r, p8i)]
                for i in range(1, T):
                    mac(blocks[:, :, :, :, i], a8[0], a8[1], blocks[:, :, :, :, i - 1], [QP, SUP], QP * SUP)
                for lv in range(4):
                    d = 1 << lv
                    w = SUP - d
                    a64 = [p[:, lv, bass.ds(q0, QP)].unsqueeze(2).broadcast_to([P, QP, w]) for p in (p64r, p64i)]
                    mac(blocks[:, :, :, d:, T - 1], a64[0], a64[1], blocks[:, :, :, 0:w, T - 1], [QP, w], QP * w)
                for q in range(QP):
                    w = SUP - 1
                    pq = [p[:, 0:T - 1, bass.ds(q0 + q, 1)].rearrange("p i a -> p a i").broadcast_to([P, w, T - 1])
                          for p in (p8r, p8i)]
                    prev = blocks[:, :, q, 0:w, T - 1].unsqueeze(3).broadcast_to([P, 2, w, T - 1])
                    mac(blocks[:, :, q, 1:, 0:T - 1], pq[0], pq[1], prev, [w, T - 1], w * (T - 1), last=q == QP - 1)

            def gelu(b):
                dve.wait_ge(y_back, b * 32 + 32)
                y = y_blk[:].rearrange("p g s -> p (g s)")
                link(V.scalar_tensor_tensor(out=y, in0=u_back[:], scalar=dskip[:, bass.ds(b, 1)], in1=y,
                                            op0=ALU.mult, op1=ALU.add))
                link(V.tensor_tensor(ta[:], y, y, ALU.mult))
                link(V.tensor_scalar(ta[:], ta[:], 0.044715, 1.0, ALU.mult, ALU.add))
                V.tensor_tensor(ta[:], ta[:], y, ALU.mult).then_inc(gelu_arg, 1)
                dve.wait_ge(gelu_sig, b + 1)
                V.tensor_tensor(y_raw[:, bass.ds(b, 1), :].rearrange("p a (n j) -> p (a j) n", j=T),
                                y.rearrange("p (j n) -> p j n", j=T), tb[:].rearrange("p (j n) -> p j n", j=T),
                                ALU.mult).then_inc(y_done, 1)
                dve.wait_ge(y_done, b + 1)

            def lo_y(m):
                dve.wait_ge(hi_done, SP_Y + m + 1)
                lo_split(y_lo[:, m, :], y_raw[:, m, :], y_hi[:, m, :])

            prepare(0)
            with dve.Fori(0, MT - 1) as b:
                ch.enter(b, PER_BATCH)
                scan(b)
                dve.wait_ge(y_prod, b + 1)
                prepare(b + 1)
                gelu(b)
                ch.leave(MT - 1)
            scan(MT - 1)
            for m in range(MT - 1):
                lo_y(m)
            gelu(MT - 1)
            lo_y(MT - 1)
            for half in range(2):
                hs = slice(half * HALF, (half + 1) * HALF)
                for m in range(MT):
                    n = half * MT + m
                    dve.wait_ge(glu_sig, n + 1)
                    V.tensor_tensor(y_raw[:, m, hs], y_raw[:, m, hs], glu_s[:, m, :], ALU.mult).then_inc(out_free, 1)
                    dve.wait_ge(out_free, OUT_GLU + n + 1)
                for m in range(MT):
                    n = half * MT + m
                    dve.wait_ge(hi_done, SP_YA + n + 1)
                    lo_split(y_lo[:, m, hs], y_raw[:, m, hs], y_hi[:, m, hs])
            for n in range(16):
                dve.wait_ge(out_ready, OUT_PA + n + 1)
                dve.wait_ge(ga_in[n % 2], 16 * (n // 2 + 1))
                V.tensor_tensor(ga_t[:, n % 2, :], acc[:, n % 4, :], ga_t[:, n % 2, :], ALU.mult).then_inc(out_free, 1)

            dve.wait_ge(ret_in, 48)

            def g_silu(h, c):
                n = OUT_RET + c
                dve.wait_ge(sig_g, h * 8 + (c + 1))
                V.tensor_tensor(silu_g[:, c, :], acc[:, n % 4, 0:DV], sig_t[:, c % 2, :], ALU.mult)\
                 .then_inc(out_free, 1)

            def head(h, more):
                def cnt(c):
                    return h * 8 + (c + 1)

                def rotate(c):
                    dve.wait_ge(out_free, h * 16 + (OUT_RET + NCH + c + 1))
                    src = qk[:, c % 2, :, :].rearrange("p a (b d) -> p (a b) d", b=2)
                    cos = rope[:, c, 0:DK // 2].unsqueeze(1).broadcast_to([P, 4, DK // 2])
                    sin = rope[:, c, DK // 2:].unsqueeze(1).broadcast_to([P, 4, DK // 2])
                    V.tensor_tensor(rc[:].rearrange("p a b d -> p (a b) d"), src, cos, ALU.mult)
                    link(V.tensor_tensor(rsn[:].rearrange("p a b d -> p (a b) d"), src, sin, ALU.mult))
                    for a, dst in ((0, rot[:, 0, :, :]),
                                   (1, kvk[:, c % 2, :].rearrange("p (b d) -> p b d", b=2))):
                        V.tensor_tensor(dst[:, 0, :], rc[:, a, 0, :], rsn[:, a, 1, :], ALU.subtract)
                        ins = V.tensor_tensor(dst[:, 1, :], rsn[:, a, 0, :], rc[:, a, 1, :], ALU.add)
                    ins.then_inc(rotated, 1)

                def decay(c):
                    dve.wait_ge(scores, cnt(c))
                    V.tensor_tensor(prob[:], aux[:, 1, 0:P], mask[:, bass.ds(h, 1), :].rearrange("p a s -> p (a s)"),
                                    ALU.mult).then_inc(prob_ready, 1)

                def norm_o(c):
                    dve.wait_ge(o_ready, cnt(c))
                    if c == 0:
                        V.tensor_copy(state[:], aux[:, 3, 0:DV]).then_inc(state_ready, 1)
                    else:
                        V.scalar_tensor_tensor(out=state[:], in0=state[:], scalar=gam[:, bass.ds(h + 2 * HEADS, 1)],
                                               in1=aux[:, 3, 0:DV], op0=ALU.mult, op1=ALU.add).then_inc(state_ready, 1)
                    dve.wait_ge(o_ss, cnt(c))
                    rstd(ors[:, 0:1], oss[:, c % 2:c % 2 + 1], DV)
                    V.scalar_tensor_tensor(out=yb[:], in0=aux[:, 2, 0:DV], scalar=ors[:, 0:1], in1=silu_g[:, c, :],
                                           op0=ALU.mult, op1=ALU.mult).then_inc(yb_ready, 1)
                    dve.wait_ge(yb_ready, cnt(c))

                for s in range(1, NCH + 2):
                    if s <= NCH:
                        rotate(s - 1)
                    if s >= 2:
                        norm_o(s - 2)
                    if more and s >= NCH:
                        g_silu(h + 1, 2 * (s - NCH))
                    if s <= NCH:
                        decay(s - 1)
                    if more and s >= NCH:
                        g_silu(h + 1, 2 * (s - NCH) + 1)
                if more:
                    for c in range(4, NCH):
                        g_silu(h + 1, c)

            for c in range(NCH):
                g_silu(0, c)
            with dve.Fori(0, HEADS - 1) as h:
                ch.enter(h, PER_HEAD)
                head(h, True)
                ch.leave(HEADS - 1)
            head(HEADS - 1, False)
            for k in range(KT):
                dve.wait_ge(hi_done, SP_YB + k + 1)
                lo_split(z_lo[:, k, :], yb_raw[:, k, :], z_hi[:, k, :])
            dve.wait_ge(out_free, OUT_PB)
            for n in range(16):
                d, half = n // 2, n % 2
                hs = slice(half * HALF, (half + 1) * HALF)
                dve.wait_ge(out_ready, OUT_PB + n + 1)
                dve.wait_ge(gb_in[n % 2], 16 * (n // 2 + 1))
                V.tensor_tensor(gb_t[:, n % 2, :], acc[:, n % 4, :], gb_t[:, n % 2, :], ALU.mult).then_inc(out_free, 1)
                dve.wait_ge(out_free, OUT_PB + n + 1)
                dve.wait_ge(ma_in, 16 * (n + 1))
                V.tensor_tensor(gb_t[:, n % 2, :], gb_t[:, n % 2, :], ma_t[:], ALU.add).then_inc(merged, 1)
                dve.wait_ge(hi_done, SP_M + n + 1)
                lo_split(m_lo[:, d, hs], gb_t[:, n % 2, :], m_hi[:, d, hs])
            def add_h(n, c, j):
                dve.wait_ge(out_ready, n + 1)
                hs = slice(j * HALF, (j + 1) * HALF)
                return V.tensor_tensor(h_res[:, c, hs], h_res[:, c, hs], acc[:, n % 4, :], ALU.add)

            for c in range(NCH):
                dve.wait_ge(xr_in[c], 16)
                add_h(OUT_OUT + c, c, 0).then_inc(out_free, 1)
            dve.wait_ge(nmlp_in, 16)

            def norm_z2(c):
                for b in range(2):
                    n = 2 * c + b
                    dve.wait_ge(z2_turned, n + 1)
                    if n >= 2:
                        dve.wait_ge(lo_done, SP_Z2 + n - 1)
                    V.tensor_tensor(z2_tmp[:, b, :].rearrange("p (k s) -> p k s", k=4),
                                    aux[:, n % 4, :].rearrange("p (k s) -> p k s", k=4),
                                    nmlp[:, 4 * b:4 * b + 4].unsqueeze(2).broadcast_to([P, 4, P]), ALU.mult)\
                     .then_inc(z2_normed, 1)
                for b in range(2):
                    n = 2 * c + b
                    dve.wait_ge(hi_done, SP_Z2 + n + 1)
                    lo_split(m_lo[:, 4 * b:4 * b + 4, c * P:(c + 1) * P],
                             z2_tmp[:, b, :].rearrange("p (k s) -> p k s", k=4),
                             m_hi[:, 4 * b:4 * b + 4, c * P:(c + 1) * P])

            for c in range(NCH):
                if c >= 1:
                    norm_z2(c - 1)
                add_h(OUT_OUT + NCH + c, c, 1).then_inc(out_free, 1)
                dve.wait_ge(h_ss, c + 1)
                rstd(rs2[:, c:c + 1], ss2[:, c:c + 1], D)
                V.tensor_scalar(diag2[:], ident[:], rs2[:, c:c + 1], None, ALU.mult).then_inc(diag2_made, 1)
            norm_z2(NCH - 1)

            def mlp_block(f, last):
                dve.wait_ge(out_free, f * 24 + OUT_MLP)
                for n in range(8):
                    half, q = n // 4, n % 4
                    hs = slice(half * HALF, (half + 1) * HALF)
                    dve.wait_ge(out_free, f * 24 + (OUT_MLP + n + 1))
                    V.tensor_tensor(relu[:, n % 2, :], relu[:, n % 2, :], relu[:, n % 2, :], ALU.mult)\
                     .then_inc(squared, 1)
                    dve.wait_ge(hi_done, f * 8 + (SP_HID + n + 1))
                    lo_split(hid_lo[:, q, hs], relu[:, n % 2, :], hid_hi[:, q, hs])
                for j in range(2):
                    for c in range(NCH):
                        n = OUT_MLP + 8 + 8 * j + c
                        dve.wait_ge(out_ready, f * 24 + (n + 1))
                        hs = slice(j * HALF, (j + 1) * HALF)
                        V.tensor_tensor(h_res[:, c, hs], h_res[:, c, hs], acc[:, n % 4, :], ALU.add)\
                         .then_inc(out_free, 1)
                        if last and j == 1 and c % 2 == 1 and c >= 3:
                            last_norm(c // 2 - 1)

            def last_norm(p):
                dve.wait_ge(f_ss, 2 * p + 2)
                rstd(rs2[:, 2 * p:2 * p + 2], ss2[:, 2 * p:2 * p + 2], D)
                if p == 0:
                    dve.wait_ge(nf_in, 16)
                for c in (2 * p, 2 * p + 1):
                    V.scalar_tensor_tensor(out=h_res[:, c, :], in0=h_res[:, c, :], scalar=rs2[:, c:c + 1], in1=nf,
                                           op0=ALU.mult, op1=ALU.mult).then_inc(f_done, 1)

            with dve.Fori(0, N_FB - 1) as f:
                mlp_block(f, False)
            mlp_block(N_FB - 1, True)
            last_norm(NCH // 2 - 1)


_INS = ["x", "w_in", "lam_re", "lam_im", "b_re", "b_im", "c_re", "c_im", "d_skip", "log_step", "w_glu", "b_glu",
        "w_proj_ssm", "w_proj_ret", "w_out", "norm_mix", "norm_mlp", "w_up", "w_down", "norm_final"]


def tables():
    import numpy as np
    inv = (10000.0 ** (-np.arange(0, DK, 2, dtype=np.float64) / DK)).astype(np.float32)
    ang = (np.arange(SEQ, dtype=np.float32)[:, None] * inv[None, :]).astype(np.float64)
    rope = np.concatenate([np.cos(ang), np.sin(ang)], axis=1).astype(np.float32)
    lg = np.log(1.0 - 2.0 ** (-5.0 - np.arange(HEADS, dtype=np.float64)))
    idx = np.arange(P, dtype=np.float64)[:, None]
    gam = np.concatenate([np.exp((idx + 1) * lg), np.exp((P - 1 - idx) * lg) * DK ** -0.5,
                          np.exp(P * lg) * np.ones((P, 1))], axis=1).astype(np.float32)
    causal = (np.arange(P)[None, :] >= np.arange(P)[:, None]).astype(np.float64)
    mask = (causal[:, None, :] * np.exp(-P * lg)[None, :, None]).astype(np.float32)
    return {"rope": rope, "gam": gam, "mask": mask, "ident": np.eye(P, dtype=np.float32)}


def kernel(**inputs):
    import numpy as np
    import concourse.bacc as bacc
    from concourse.bass_utils import run_bass_kernel_spmd

    nc = bacc.Bacc("TRN2", target_bir_lowering=False, num_devices=1)
    arrays = {name: np.ascontiguousarray(inputs[name]) for name in _INS}
    arrays.update(tables())
    t = {name: nc.dram_tensor("in_" + name, a.shape, mybir.dt.from_np(a.dtype), kind="ExternalInput").ap()
         for name, a in arrays.items()}
    t["out"] = nc.dram_tensor("out", (1, SEQ, D), F32, kind="ExternalOutput").ap()
    build(nc, t)
    return run_bass_kernel_spmd(nc, [{"in_" + name: a for name, a in arrays.items()}], core_ids=[0]).results[0]["out"]
```

```python
from contextlib import ExitStack

import concourse.bass as bass
from concourse import mybir

F32 = mybir.dt.float32
F32R = mybir.dt.float32r
BF16 = mybir.dt.bfloat16
I32 = mybir.dt.int32
ALU = mybir.AluOpType
ACT = mybir.ActivationFunctionType

P = 128
SEQ = 1024
D = 1024
KT = D // P
NCH = SEQ // P
HALF = 512
FF = 4096
FB = 512
N_FB = FF // FB
SSM = 512
GROUPS, STATE, CH = 32, 64, 16
T = P // CH
NT = SEQ // T
MT = SSM // P
PAIRS = GROUPS // 2
QP = PAIRS // MT
GB = 2 * QP
SUP = NT // T
HEADS, DK, DV = 4, 128, 256
EPS = 1e-6
GA = MT + 2

COL_Q = SSM
COL_K = COL_Q + HEADS * DK
COL_V = COL_K + HEADS * DK
COL_G = COL_V + HEADS * DV
COL_GATE = COL_G + HEADS * DV

LD_U, LD_GATE, LD_GLU, LD_PA, LD_RET, LD_PB, LD_OUT, LD_MLP = 0, 4, 20, 22, 26, 50, 58, 66
GR_U, GR_GATE, GR_GLU, GR_PA, GR_RET, GR_PB, GR_OUT, GR_MLP = 0, 1, 5, 6, 8, 16, 18, 20
OUT_U, OUT_GATE, OUT_GLU, OUT_PA, OUT_RET, OUT_PB, OUT_OUT, OUT_MLP = 0, 8, 40, 48, 64, 128, 144, 160
SP_Z, SP_Y, SP_YA, SP_YB, SP_M, SP_Z2, SP_HID = 0, 16, 20, 28, 36, 52, 68

STEPS_FIRST, STEPS_MID, STEPS_LAST = (2, 3, 7), (1, 2, 6), (0, 1, 5)

LN2 = (0.693359375, -2.12194440e-4)
MAGIC = 12582912.0


def parts(value, n):
    import math
    out = []
    for _ in range(n):
        if value == 0.0:
            out.append(0.0)
            continue
        e = math.floor(math.log2(abs(value))) - 10
        q = round(value / 2.0 ** e) * 2.0 ** e
        out.append(q)
        value -= q
    return out


PER_BATCH = 51
PER_HEAD = 10 * NCH


class Chain:

    def __init__(self, eng, sem):
        self.eng, self.sem, self.n, self.off, self.mark = eng, sem, 0, 0, 0

    def link(self, ins):
        self.n += 1
        ins.then_inc(self.sem, 1)
        self.eng.wait_ge(self.sem, self.off + self.n)

    def enter(self, i, per):
        self.off, self.mark, self.per = i * per, self.n, per

    def leave(self, trips):
        assert self.n - self.mark == self.per, (self.n - self.mark, self.per)
        self.n += (trips - 1) * self.per
        self.off = 0


def build(nc, t):
    with ExitStack() as ctx:
        def sb(name, shape, dt=F32, where=ctx):
            return where.enter_context(nc.sbuf_tensor(name, shape, dt))

        def sem(name):
            return ctx.enter_context(nc.semaphore(name))

        ident = sb("ident", [P, P])
        rs_bits = sb("rs_bits", [P, 4], I32)
        rs_tmp = sb("rs_tmp", [P, 4, 4])
        stage = sb("stage", [P, 2, 2 * HALF])
        w_hi = sb("w_hi", [P, 2, KT, HALF], F32R)
        w_lo = sb("w_lo", [P, 2, KT, HALF], F32R)
        with ExitStack() as r:
            z_hi = sb("z_hi", [P, KT, SEQ], F32R, r)
            z_lo = sb("z_lo", [P, KT, SEQ], F32R, r)
        with ExitStack() as r:
            h_res = sb("h_res", [P, NCH, D], F32, r)
            hid_hi = sb("hid_hi", [P, FB // P, SEQ], F32R, r)
            hid_lo = sb("hid_lo", [P, FB // P, SEQ], F32R, r)
        ctx.enter_context(nc.sbuf_tensor("region1", [P, 2 * KT * SEQ], F32))

        ph = ExitStack()
        bbr = sb("bbr", [P, PAIRS, CH], F32, ph)
        bbi = sb("bbi", [P, PAIRS, CH], F32, ph)
        ctr = sb("ctr", [P, PAIRS, CH], F32, ph)
        cti = sb("cti", [P, PAIRS, CH], F32, ph)
        pwr = sb("pwr", [P, T + 1, PAIRS], F32, ph)
        pwi = sb("pwi", [P, T + 1, PAIRS], F32, ph)
        rpr = sb("rpr", [P, T, PAIRS], F32, ph)
        rpi = sb("rpi", [P, T, PAIRS], F32, ph)
        p8r = sb("p8r", [P, T, PAIRS], F32, ph)
        p8i = sb("p8i", [P, T, PAIRS], F32, ph)
        p64r = sb("p64r", [P, 4, PAIRS], F32, ph)
        p64i = sb("p64i", [P, 4, PAIRS], F32, ph)
        dskip = sb("dskip", [P, MT], F32, ph)
        bglu = sb("bglu", [P, MT], F32, ph)
        with ExitStack() as r:
            x_in = sb("x_in", [P, NCH, D], F32, r)
        with ExitStack() as r:
            u_all = sb("u_all", [P, MT, T, NT], F32, r)
        y_raw = sb("y_raw", [P, MT, SEQ], F32, ph)
        with ExitStack() as r:
            sb("x_upper", [P, NCH // 2, D], F32, r)
            z_tmp = sb("z_tmp", [P, 4, HALF], F32, r)
            x_junk = sb("x_junk", [P, D], BF16, r)
            ss1 = sb("ss1", [P, NCH], F32, r)
            rs1 = sb("rs1", [P, NCH], F32, r)
            nmix = sb("nmix", [P, KT], F32, r)
            c_raw = sb("c_raw", [P, 2, MT, P], F32, r)
            b_raw = sb("b_raw", [P, 2, PAIRS, CH], F32, r)
            coef = sb("coef", [P, 56, PAIRS], F32, r)
            ibits = sb("ibits", [P, 2, PAIRS], I32, r)
        with ExitStack() as r:
            u_blk = sb("u_blk", [P, GB, NT], F32, r)
            toep = sb("toep", [P, GB, P], F32, r)
            car = sb("car", [P, QP, T + 1, CH], F32, r)
            can = sb("can", [P, QP, T + 1, CH], F32, r)
            abr = sb("abr", [P, QP, T, CH], F32, r)
            abi = sb("abi", [P, QP, T, CH], F32, r)
            abt = sb("abt", [P, 2, QP, P], F32, r)
            hst = sb("hst", [P, 2, QP, NT + 1], F32, r)
            y_blk = sb("y_blk", [P, GB, NT], F32, r)
            u_back = sb("u_back", [P, SEQ], F32, r)
            ta = sb("ta", [P, SEQ], F32, r)
            tb = sb("tb", [P, SEQ], F32, r)
            gate_t = sb("gate_t", [P, 2, HALF], F32, r)
        with ExitStack() as r:
            y_hl = sb("y_hl", [P, MT, 2, SEQ], F32R, r)
            y_hi, y_lo = y_hl[:, :, 0, :], y_hl[:, :, 1, :]
            ga_t = sb("ga_t", [P, GA, HALF], F32, r)
            glu_s = ga_t[:, 0:MT, :]
        ph.close()
        with ExitStack() as r:
            rope = sb("rope", [P, NCH, P], F32, r)
            gam = sb("gam", [P, 3 * HEADS], F32, r)
            mask = sb("mask", [P, HEADS, P], F32, r)
            silu_g = sb("silu_g", [P, NCH, DV], F32, r)
            sig_t = sb("sig_t", [P, 2, DV], F32, r)
            qk = sb("qk", [P, 2, 2, DK], F32, r)
            vv = sb("vv", [P, 2, DV], F32, r)
            rot = sb("rot", [P, 2, 2, DK // 2], F32, r)
            rc = sb("rc", [P, 2, 2, DK // 2], F32, r)
            rsn = sb("rsn", [P, 2, 2, DK // 2], F32, r)
            kvk = sb("kvk", [P, 2, DK], F32, r)
            qkt = sb("qkt", [P, 2, P], F32, r)
            prob = sb("prob", [P, P], F32, r)
            state = sb("state", [P, DV], F32, r)
            yb = sb("yb", [P, DV], F32, r)
            o_junk = sb("o_junk", [P, DV], BF16, r)
            oss = sb("oss", [P, 2], F32, r)
            ors = sb("ors", [P, 1], F32, r)
            yb_raw = sb("yb_raw", [P, KT, SEQ], F32, r)
        with ExitStack() as r:
            m_hi = sb("m_hi", [P, KT, SEQ], F32R, r)
            m_lo = sb("m_lo", [P, KT, SEQ], F32R, r)
            nmlp = sb("nmlp", [P, KT], F32, r)
            ss2 = sb("ss2", [P, NCH], F32, r)
            rs2 = sb("rs2", [P, NCH], F32, r)
            with ExitStack() as q:
                gb_t = sb("gb_t", [P, 2, HALF], F32, q)
                ma_t = sb("ma_t", [P, HALF], F32, q)
            with ExitStack() as q:
                zb = sb("zb", [P, D], F32, q)
            with ExitStack() as q:
                h_junk = sb("h_junk", [P, D], BF16, q)
                relu = sb("relu", [P, 2, HALF], F32, q)
        acc = ctx.enter_context(nc.psum_tensor("acc", [P, 4, HALF], F32))
        aux = ctx.enter_context(nc.psum_tensor("aux", [P, 4, HALF], F32))

        u_dram = nc.dram_tensor("u_dram", (MT, P, T, NT), F32, kind="Internal").ap()
        y_dram = nc.dram_tensor("y_dram", (MT, P, T, NT), F32, kind="Internal").ap()
        gate_dram = nc.dram_tensor("gate_dram", (2 * KT, P, SEQ), F32, kind="Internal").ap()
        ma_dram = nc.dram_tensor("ma_dram", (KT, P, SEQ), F32, kind="Internal").ap()
        out_rows = t["out"][0].rearrange("(c p) d -> p c d", p=P)
        x_rows = t["x"][0].rearrange("(c p) d -> p c d", p=P)

        const_in = sem("const_in")
        par_in = sem("par_in")
        ret_in = sem("ret_in")
        x_ready = [sem(f"x_ready{i}") for i in range(NCH)]
        raw = [sem(f"raw{i}") for i in range(2)]
        raw_qkv = [sem(f"raw_qkv{i}") for i in range(2)]
        hi_pool = sem("hi_pool")
        w_ready = sem("w_ready")
        out_ready = sem("out_ready")
        out_free = sem("out_free")
        hi_done = sem("hi_done")
        hi_part = sem("hi_part")
        lo_done = sem("lo_done")
        chain_v = sem("chain_v")
        tick_pool = sem("tick_pool")
        tick_act = sem("tick_act")
        ss_done = sem("ss_done")
        x_rstd = sem("x_rstd")
        x_scaled = sem("x_scaled")
        z_turned = sem("z_turned")
        z_normed = sem("z_normed")
        u_out = sem("u_out")
        ct_turned = sem("ct_turned")
        ct_ready = sem("ct_ready")
        prep = sem("prep")
        ab_turned = sem("ab_turned")
        ab_ready = sem("ab_ready")
        kern = sem("kern")
        kern_ready = sem("kern_ready")
        toep_in = sem("toep_in")
        u_blk_in = sem("u_blk_in")
        x_state = sem("x_state")
        scanned = sem("scanned")
        y_prod = sem("y_prod")
        y_copied = sem("y_copied")
        y_sent = sem("y_sent")
        y_back = sem("y_back")
        gelu_arg = sem("gelu_arg")
        gelu_sig = sem("gelu_sig")
        y_done = sem("y_done")
        gate_sent = [sem(f"gate_sent{i}") for i in range(2)]
        glu_sig = sem("glu_sig")
        ga_in = [sem(f"ga_in{i}") for i in range(GA)]
        ma_sent = [sem(f"ma_sent{i}") for i in range(GA)]
        sig_g = sem("sig_g")
        rotated = sem("rotated")
        qk_turned = sem("qk_turned")
        qkt_ready = sem("qkt_ready")
        scores = sem("scores")
        prob_ready = sem("prob_ready")
        state_ready = sem("state_ready")
        o_ready = sem("o_ready")
        o_ss = sem("o_ss")
        yb_ready = sem("yb_ready")
        yb_turned = sem("yb_turned")
        yb_stored = sem("yb_stored")
        nmlp_in = sem("nmlp_in")
        gb_in = [sem(f"gb_in{i}") for i in range(2)]
        ma_in = sem("ma_in")
        merged = sem("merged")
        xr_in = [sem(f"xr_in{i}") for i in range(NCH)]
        h_ss = sem("h_ss")
        h_rstd = sem("h_rstd")
        z2_scaled = sem("z2_scaled")
        z2_turned = sem("z2_turned")
        z2_normed = sem("z2_normed")
        squared = sem("squared")
        nf_in = sem("nf_in")
        f_ss = sem("f_ss")
        f_done = sem("f_done")
        f_rstd = sem("f_rstd")
        f_scaled = sem("f_scaled")
        f_done_pool = sem("f_done_pool")
        stored = sem("stored")

        nf = stage[:, 0, :]

        block = ctx.enter_context(nc.Block())

        @block.sync
        def _(sp):
            def load(n, src, k=2, waits=None):
                s = n % 2 if waits is None else waits[1]
                if waits is not None:
                    sp.wait_ge(w_ready, waits[0])
                elif n >= 2:
                    sp.wait_ge(w_ready, n - 1)
                sp.dma_start(stage[:, s, :].rearrange("p (k c) -> p k c", k=k), src).then_inc(raw[s], 16)

            w_in = t["w_in"][0].rearrange("(k p) c -> p k c", p=P)

            sp.dma_start(x_in[:, 0, :], x_rows[:, 0, :]).then_inc(x_ready[0], 16)
            sp.dma_start(ident[:], t["ident"]).then_inc(const_in, 16)
            sp.dma_start(nmix[:], t["norm_mix"].rearrange("a (k p) -> p (a k)", p=P), allow_slow_non_contiguous=True).then_inc(const_in, 16)
            for c in range(1, NCH):
                sp.dma_start(x_in[:, c, :], x_rows[:, c, :]).then_inc(x_ready[c], 16)
                if c in (1, 3):
                    i = c // 2
                    load(i, w_in[:, 2 * i:2 * i + 2, 0:HALF])
            for gp in range(2):
                rows = slice(gp * STATE, (gp + 1) * STATE)
                sp.dma_start(coef[rows, 0, :], t["lam_re"][0, gp::2, :].rearrange("g p -> p g"),
                             allow_slow_non_contiguous=True).then_inc(par_in, 16)
                sp.dma_start(coef[rows, 1, :], t["lam_im"][0, gp::2, :].rearrange("g p -> p g"),
                             allow_slow_non_contiguous=True).then_inc(par_in, 16)
                ls = t["log_step"]
                sp.dma_start(coef[rows, 2, :], bass.AP(tensor=ls.tensor, offset=gp, ap=[[0, STATE], [2, PAIRS]]),
                             allow_slow_non_contiguous=True).then_inc(par_in, 16)
                for ri, name in enumerate(("b_re", "b_im")):
                    sp.dma_start(b_raw[rows, ri, :, :], t[name][0, gp::2, :, :].rearrange("g p c -> p g c"))\
                      .then_inc(par_in, 16)
                for ri, name in enumerate(("c_re", "c_im")):
                    sp.dma_start(c_raw[:, ri, :, gp * STATE:(gp + 1) * STATE],
                                 t[name][0].rearrange("(m g) c p -> (g c) m p", m=MT)).then_inc(par_in, 16)
            sp.dma_start(dskip[:], t["d_skip"].rearrange("a (m p) -> p (a m)", p=P), allow_slow_non_contiguous=True).then_inc(par_in, 16)
            sp.dma_start(bglu[:], t["b_glu"].rearrange("a (m p) -> p (a m)", p=P), allow_slow_non_contiguous=True).then_inc(par_in, 16)
            for i in range(2, 4):
                load(i, w_in[:, 2 * i:2 * i + 2, 0:HALF])
            with sp.Fori(0, MT) as b:
                for i in range(4):
                    n = LD_GATE + i
                    load(n, w_in[:, 4 * (i % 2):4 * (i % 2) + 4,
                                 bass.ds(b * HALF + (COL_GATE + i // 2 * (HALF // 2)), HALF // 2)],
                         k=4, waits=(b * 4 + (n - 1), n % 2))
            w_glu = t["w_glu"][0].rearrange("(k p) c -> p k c", p=P)
            for i in range(2):
                load(LD_GLU + i, w_glu[:, 2 * i:2 * i + 2, :])
            w_pa = t["w_proj_ssm"][0].rearrange("(k p) c -> p k c", p=P)
            for j in range(2):
                for i in range(2):
                    load(LD_PA + 2 * j + i, w_pa[:, 2 * i:2 * i + 2, j * HALF:(j + 1) * HALF])
            with sp.Fori(0, HEADS) as h:
                for i in range(2):
                    n = LD_RET + i
                    load(n, w_in[:, 4 * i:4 * i + 4, bass.ds(COL_G + h * DV, DV)], k=4,
                         waits=(h * 6 + (n - 1), n % 2))
                for i in range(4):
                    n = LD_RET + 2 + i
                    sp.wait_ge(w_ready, h * 6 + (n - 1))
                    dst = stage[:, n % 2, :].rearrange("p (k c) -> p k c", k=2)
                    for d0, c0, w in ((0, COL_Q, DK), (DK, COL_K, DK), (2 * DK, COL_V, DV)):
                        sp.dma_start(dst[:, :, d0:d0 + w], w_in[:, 2 * i:2 * i + 2, bass.ds(c0 + h * w, w)])\
                          .then_inc(raw_qkv[n % 2], 16)
            w_pb = t["w_proj_ret"][0].rearrange("(k p) c -> p k c", p=P)
            w_o = t["w_out"][0].rearrange("(k p) c -> p k c", p=P)
            for base, w in ((LD_PB, w_pb), (LD_OUT, w_o)):
                for j in range(2):
                    for i in range(4):
                        load(base + 4 * j + i, w[:, 2 * i:2 * i + 2, j * HALF:(j + 1) * HALF])
            w_up = t["w_up"][0].rearrange("(k p) c -> p k c", p=P)
            w_dn = t["w_down"][0].rearrange("(k p) c -> p k c", p=P)
            with sp.Fori(0, N_FB) as f:
                for i in range(4):
                    n = LD_MLP + i
                    load(n, w_up[:, 2 * i:2 * i + 2, bass.ds(f * FB, FB)], waits=(f * 8 + (n - 1), n % 2))
                for i in range(4):
                    n = LD_MLP + 4 + i
                    load(n, w_dn[:, bass.ds(f * (FB // P) + i, 1), :], k=1, waits=(f * 8 + (n - 1), n % 2))
            sp.wait_ge(w_ready, LD_MLP + 8 * N_FB)
            nfin = t["norm_final"]
            sp.dma_start(nf, bass.AP(tensor=nfin.tensor, offset=0, ap=[[0, P], [1, D]])).then_inc(nf_in, 16)
            for c in range(NCH):
                if c % 2 == 0 or c == NCH - 1:
                    sp.wait_ge(f_done, (c + 1) // 2 + 1)
                else:
                    sp.wait_ge(f_done_pool, c // 2 + 1)
                sp.dma_start(out_rows[:, c, :], h_res[:, c, :]).then_inc(stored, 16)
            sp.wait_ge(stored, 16 * NCH)

        @block.gpsimd
        def _(pool):
            def split(ready, count, s, slot, u0, n_done, freed=None):
                if freed is not None:
                    pool.wait_ge(out_ready, freed)
                pool.wait_ge(ready, count)
                if not isinstance(n_done, int):
                    pool.sem_inc(tick_pool, 1)
                dst_hi = w_hi[:, slot, u0:u0 + 2, :].rearrange("p k c -> p (k c)")
                dst_lo = w_lo[:, slot, u0:u0 + 2, :].rearrange("p k c -> p (k c)")
                nc.gpsimd.tensor_copy(dst_hi, stage[:, s, :]).then_inc(hi_pool, 1)
                pool.wait_ge(hi_pool, n_done)
                nc.gpsimd.tensor_tensor(dst_lo, stage[:, s, :], dst_hi.bitcast(F32), ALU.subtract)\
                  .then_inc(w_ready, 1)

            def regular(n, gr, i, seen, freed):
                split(raw[n % 2], 16 * (seen + 1), n % 2, gr % 2, 2 * i, n + 1, freed=freed if i == 0 else None)

            for i in range(4):
                regular(LD_U + i, GR_U, i, i // 2, None)
            with pool.Fori(0, MT) as b:
                for i in range(4):
                    n = LD_GATE + i
                    freed = b * 8 + (OUT_GATE - 4 if i < 2 else OUT_GATE)
                    split(raw[n % 2], b * 32 + 16 * (n // 2 + 1), n % 2, (GR_GATE + i // 2) % 2, 2 * (i % 2),
                          b * 4 + (n + 1), freed=freed if i % 2 == 0 else None)
            for i in range(2):
                regular(LD_GLU + i, GR_GLU, i, (LD_GLU + i) // 2, OUT_GLU - 4)
            for j in range(2):
                for i in range(2):
                    n = LD_PA + 2 * j + i
                    regular(n, GR_PA + j, i, n // 2, OUT_GLU + 8 * j)
            with pool.Fori(0, HEADS) as h:
                for i in range(2):
                    n = LD_RET + i
                    split(raw[n % 2], h * 16 + 16 * (LD_RET // 2 + 1), n % 2, GR_RET % 2, 2 * i, h * 6 + (n + 1),
                          freed=h * 16 + (OUT_RET - 8) if i == 0 else None)
                for i in range(4):
                    n = LD_RET + 2 + i
                    split(raw_qkv[n % 2], h * 96 + 48 * (i // 2 + 1), n % 2, (GR_RET + 1) % 2, 2 * i, h * 6 + (n + 1),
                          freed=h * 16 + OUT_RET if i == 0 else None)
            g_slot = LD_RET // 2 + HEADS
            for base, gr in ((LD_PB, GR_PB), (LD_OUT, GR_OUT)):
                for j in range(2):
                    for i in range(4):
                        n = base + 4 * j + i
                        regular(n, gr + j, i, g_slot + (n - LD_PB) // 2, OUT_PB + 8 * (gr + j - GR_PB) - 8)
            with pool.Fori(0, N_FB) as f:
                for b in range(2):
                    for i in range(4):
                        n = LD_MLP + 4 * b + i
                        split(raw[n % 2], f * 64 + 16 * (g_slot + (n - LD_PB) // 2 + 1), n % 2, (GR_MLP + b) % 2,
                              2 * i, f * 8 + (n + 1), freed=f * 24 + (OUT_MLP - 8 + 8 * b) if i == 0 else None)

            pool.wait_ge(nf_in, 16)
            for p, c in enumerate((1, 3, 5)):
                pool.wait_ge(f_scaled, p + 1)
                nc.gpsimd.tensor_tensor(h_res[:, c, :], h_res[:, c, :], nf, ALU.mult).then_inc(f_done_pool, 1)

        @block.tensor
        def _(pe):
            def three(out, s_hi, s_lo, m_hi_, m_lo_, first, last):
                nc.tensor.matmul(out, s_hi, m_hi_, start=first, stop=False)
                nc.tensor.matmul(out, s_hi, m_lo_, start=False, stop=False)
                return nc.tensor.matmul(out, s_lo, m_hi_, start=False, stop=last)

            def wait_bank(n):
                pe.wait_ge(out_free, n - 3)

            def features(n, slot, units, col, a_hi, a_lo, half, w_wait=None):
                if n >= 4:
                    wait_bank(n)
                for k in range(units):
                    if w_wait is not None and k % 2 == 0:
                        pe.wait_ge(w_ready, w_wait + k // 2)
                    mm = three(acc[:, n % 4, :], w_hi[:, slot, k, col:col + P], w_lo[:, slot, k, col:col + P],
                               a_hi[:, k, half * HALF:(half + 1) * HALF], a_lo[:, k, half * HALF:(half + 1) * HALF],
                               k == 0, k == units - 1)
                mm.then_inc(out_ready, 1)
                return mm

            def quad(n0, slot, units, a_hi, a_lo, half, w_wait, a_wait=None, hooks={}):
                for k in range(units):
                    if k % 2 == 0:
                        pe.wait_ge(w_ready, w_wait + k // 2)
                    if a_wait is not None:
                        pe.wait_ge(lo_done, a_wait + k)
                    for m in range(4):
                        if k == 0 and n0 >= 4:
                            wait_bank(n0 + m)
                        mm = three(acc[:, (n0 + m) % 4, :], w_hi[:, slot, k, m * P:(m + 1) * P],
                                   w_lo[:, slot, k, m * P:(m + 1) * P], a_hi[:, k, half * HALF:(half + 1) * HALF],
                                   a_lo[:, k, half * HALF:(half + 1) * HALF], k == 0, k == units - 1)
                        if k == units - 1:
                            mm.then_inc(out_ready, 1)
                    for c in hooks.get(k, ()):
                        turn_x(c)

            def turn_x(c):
                pe.wait_ge(x_scaled, c + 1)
                for b in range(2):
                    n = 2 * c + b
                    if n >= 4:
                        pe.wait_ge(z_normed, n - 3)
                    for q in range(4):
                        k = 4 * b + q
                        mm = nc.tensor.transpose(aux[:, n % 4, q * P:(q + 1) * P], x_in[:, c, k * P:(k + 1) * P],
                                                 ident[:])
                    mm.then_inc(z_turned, 1)

            for c in range(4):
                turn_x(c)

            pe.wait_ge(lo_done, SP_Z + 8)
            quad(OUT_U, GR_U % 2, KT, z_hi, z_lo, 0, LD_U + 1, hooks={1: (4, 5), 4: (6, 7)})
            for m in range(MT):
                if m == 0:
                    pe.wait_ge(lo_done, SP_Z + 16)
                features(OUT_U + MT + m, GR_U % 2, KT, m * P, z_hi, z_lo, 1)

            pe.wait_ge(par_in, 16 * 16)
            pe.wait_ge(z_normed, 2 * NCH)
            for ri in range(2):
                for m in range(MT):
                    mm = nc.tensor.transpose(aux[:, ri, m * P:(m + 1) * P], c_raw[:, ri, m, :], ident[:])
            mm.then_inc(ct_turned, 1)

            def batch(b, steps):
                def gate(o):
                    d, half = o // 2, o % 2
                    n = OUT_GATE + o
                    slot = (GR_GATE + o // 4) % 2
                    wg = [w[:, slot, 0:4, :].rearrange("p u (a c) -> p (u a) c", a=2) for w in (w_hi, w_lo)]
                    cs = slice(d % 2 * P, (d % 2 + 1) * P)
                    pe.wait_ge(out_free, b * 8 + (n - 3))
                    for k in range(KT):
                        if o % 4 == 0 and k % 4 == 0:
                            pe.wait_ge(w_ready, b * 4 + (LD_GATE + o // 4 * 2 + k // 4 + 1))
                        mm = three(acc[:, n % 4, :], wg[0][:, k, cs], wg[1][:, k, cs],
                                   z_hi[:, k, half * HALF:(half + 1) * HALF],
                                   z_lo[:, k, half * HALF:(half + 1) * HALF], k == 0, k == KT - 1)
                    mm.then_inc(out_ready, 1)

                def turn_ab():
                    pe.wait_ge(prep, b + 1)
                    for ri, src in enumerate((abr, abi)):
                        for q in range(QP):
                            mm = nc.tensor.transpose(aux[:, ri, q * P:(q + 1) * P],
                                                     src[:, q, :, :].rearrange("p t c -> p (t c)"), ident[:])
                    mm.then_inc(ab_turned, 1)

                def impulse():
                    for g in range(GB):
                        q, gp = g // 2, g % 2
                        rows = slice(gp * STATE, (gp + 1) * STATE)
                        out = aux[0:CH, 2 + gp, q * P:(q + 1) * P]
                        nc.tensor.matmul(out, abr[rows, q, T - 1, :],
                                         car[rows, q, 0:T, :].rearrange("p t c -> p (t c)"), start=True, stop=False)
                        mm = nc.tensor.matmul(out, abi[rows, q, T - 1, :],
                                              can[rows, q, 0:T, :].rearrange("p t c -> p (t c)"),
                                              start=False, stop=True)
                    mm.then_inc(kern, 1)

                def add_state():
                    pe.wait_ge(ab_ready, b + 1)
                    pe.wait_ge(u_blk_in, b * 128 + 128)
                    for g in range(GB):
                        q, gp = g // 2, g % 2
                        for ri in range(2):
                            mm = nc.tensor.matmul(aux[gp * STATE:(gp + 1) * STATE, ri, q * P:(q + 1) * P],
                                                  abt[:, ri, q, gp * STATE:(gp + 1) * STATE], u_blk[:, g, :],
                                                  start=True, stop=True)
                    mm.then_inc(x_state, 1)

                def outputs():
                    pe.wait_ge(scanned, b + 1)
                    pe.wait_ge(toep_in, b * 112 + 112)
                    for g in range(GB):
                        q, gp = g // 2, g % 2
                        rows = slice(gp * STATE, (gp + 1) * STATE)
                        out = aux[:, 2 + gp, q * P:(q + 1) * P]
                        nc.tensor.matmul(out, toep[:, gp * QP + q, :], u_blk[:, g, :], start=True, stop=False)
                        nc.tensor.matmul(out, car[rows, q, 1:T + 1, :].rearrange("p t c -> p (t c)"),
                                         hst[rows, 0, q, 0:NT], start=False, stop=False)
                        mm = nc.tensor.matmul(out, can[rows, q, 1:T + 1, :].rearrange("p t c -> p (t c)"),
                                              hst[rows, 1, q, 0:NT], start=False, stop=True)
                    mm.then_inc(y_prod, 1)

                for o in range(8):
                    gate(o)
                    if o == steps[0]:
                        turn_ab()
                    if o == steps[1]:
                        add_state()
                        impulse()
                    if o == steps[2]:
                        outputs()

            batch(0, STEPS_FIRST)
            with pe.Fori(1, MT - 1) as b:
                batch(b, STEPS_MID)
            batch(MT - 1, STEPS_LAST)

            quad(OUT_GLU, GR_GLU % 2, MT, y_hi, y_lo, 0, LD_GLU + 1, a_wait=SP_Y + 1)
            for m in range(MT):
                features(OUT_GLU + MT + m, GR_GLU % 2, MT, m * P, y_hi, y_lo, 1)
            for j in range(2):
                for half in range(2):
                    for d in range(4):
                        n = OUT_PA + 8 * j + 4 * half + d
                        if j == 0 and d == 0:
                            pe.wait_ge(lo_done, SP_YA + 4 * (half + 1))
                        features(n, (GR_PA + j) % 2, MT, d * P, y_hi, y_lo, half,
                                 w_wait=LD_PA + 2 * j + 1 if half == 0 and d == 0 else None)

            sg, sq = GR_RET % 2, (GR_RET + 1) % 2
            wg_hi = w_hi[:, sg, 0:4, :].rearrange("p u (a c) -> p (u a) c", a=2)
            wg_lo = w_lo[:, sg, 0:4, :].rearrange("p u (a c) -> p (u a) c", a=2)

            def g_part(h, c, k):
                n = OUT_RET + c
                if k == 0:
                    pe.wait_ge(out_free, h * 16 + (n - 3))
                if c == 0 and k % 4 == 0:
                    pe.wait_ge(w_ready, h * 6 + (LD_RET + k // 4 + 1))
                mm = three(acc[:, n % 4, 0:DV], z_hi[:, k, c * P:(c + 1) * P], z_lo[:, k, c * P:(c + 1) * P],
                           wg_hi[:, k, :], wg_lo[:, k, :], k == 0, k == KT - 1)
                if k == KT - 1:
                    mm.then_inc(out_ready, 1)

            def qkv_part(h, c, k):
                n = OUT_RET + NCH + c
                if k == 0:
                    pe.wait_ge(out_free, h * 16 + (n - 3))
                if c == 0 and k % 2 == 0:
                    pe.wait_ge(w_ready, h * 6 + (LD_RET + 2 + k // 2 + 1))
                mm = three(acc[:, n % 4, :], z_hi[:, k, c * P:(c + 1) * P], z_lo[:, k, c * P:(c + 1) * P],
                           w_hi[:, sq, k, :], w_lo[:, sq, k, :], k == 0, k == KT - 1)
                if k == KT - 1:
                    mm.then_inc(out_ready, 1)

            def pb_quad(k):
                slot = GR_PB % 2
                pe.wait_ge(lo_done, SP_YB + k + 1)
                if k % 2 == 0:
                    pe.wait_ge(w_ready, LD_PB + k // 2 + 1)
                for o in range(4):
                    d, half = o // 2, o % 2
                    if k == 0:
                        wait_bank(OUT_PB + o)
                    mm = three(acc[:, (OUT_PB + o) % 4, :], w_hi[:, slot, k, d * P:(d + 1) * P],
                               w_lo[:, slot, k, d * P:(d + 1) * P], z_hi[:, k, half * HALF:(half + 1) * HALF],
                               z_lo[:, k, half * HALF:(half + 1) * HALF], k == 0, k == KT - 1)
                    if k == KT - 1:
                        mm.then_inc(out_ready, 1)

            def head(h, more):
                def cnt(c):
                    return h * 8 + (c + 1)

                def turn_qk(c):
                    pe.wait_ge(rotated, cnt(c))
                    if c >= 2:
                        pe.wait_ge(yb_stored, cnt(c - 2))
                    nc.tensor.transpose(aux[:, 0, 0:P], rot[:, 0, :, :].rearrange("p a b -> p (a b)"), ident[:])
                    nc.tensor.transpose(aux[:, 0, P:2 * P], kvk[:, c % 2, :], ident[:]).then_inc(qk_turned, 1)

                def score(c):
                    pe.wait_ge(qkt_ready, cnt(c))
                    nc.tensor.matmul(aux[:, 1, 0:P], qkt[:, 1, :], qkt[:, 0, :], start=True, stop=True)\
                      .then_inc(scores, 1)
                    if 1 <= c < NCH - 1:
                        pe.wait_ge(state_ready, h * (NCH - 1) + c)
                    if c < NCH - 1:
                        nc.tensor.matmul(aux[:, 3, 0:DV], kvk[:, c % 2, :], vv[:, c % 2, :], start=True, stop=True)

                def attend(c):
                    pe.wait_ge(prob_ready, cnt(c))
                    if c >= 1:
                        pe.wait_ge(yb_ready, cnt(c - 1))
                    mm = nc.tensor.matmul(aux[:, 2, 0:DV], prob[:], vv[:, c % 2, :], start=True, stop=(c == 0))
                    if c >= 1:
                        pe.wait_ge(state_ready, h * (NCH - 1) + c)
                        mm = nc.tensor.matmul(aux[:, 2, 0:DV], qkt[:, 0, :], state[:], start=False, stop=True)
                    mm.then_inc(o_ready, 1)

                def turn_yb(c):
                    pe.wait_ge(yb_ready, cnt(c))
                    for e in range(2):
                        mm = nc.tensor.transpose(aux[:, 0, e * P:(e + 1) * P], yb[:, e * P:(e + 1) * P], ident[:])
                    mm.then_inc(yb_turned, 1)

                for s in range(NCH + 3):
                    for k in range(KT):
                        if s < NCH:
                            qkv_part(h, s, k)
                        elif more:
                            for i in (2 * k, 2 * k + 1):
                                c = 2 * (s - NCH) + i // KT
                                g_part(h + 1, c, i % KT)
                        elif k in (2, 5, 7) and s < NCH + 2:
                            if 3 * (s - NCH) + k // 3 == 5:
                                turn_yb(NCH - 1)
                            pb_quad(3 * (s - NCH) + k // 3)
                        if k == 0 and s >= 3 and (more or s < NCH + 2):
                            turn_yb(s - 3)
                        if k == 1 and 2 <= s <= NCH + 1:
                            attend(s - 2)
                        if k == 4 and 1 <= s <= NCH:
                            turn_qk(s - 1)
                        if k == 6 and 1 <= s <= NCH:
                            score(s - 1)
                if more:
                    for c in (6, 7):
                        for k in range(KT):
                            g_part(h + 1, c, k)
                else:
                    pb_quad(6)
                    pb_quad(7)

            for c in range(NCH):
                for k in range(KT):
                    g_part(0, c, k)
            with pe.Fori(0, HEADS - 1) as h:
                head(h, True)
            head(HEADS - 1, False)

            for j in range(2):
                for d in range(4):
                    for half in range(2):
                        n = OUT_PB + 8 * j + 2 * d + half
                        if n < OUT_PB + 4:
                            continue
                        slot = (GR_PB + j) % 2
                        wait_bank(n)
                        for k in range(KT):
                            if d == 0 and half == 0 and k % 2 == 0:
                                pe.wait_ge(w_ready, LD_PB + 4 * j + k // 2 + 1)
                            mm = three(acc[:, n % 4, :], w_hi[:, slot, k, d * P:(d + 1) * P],
                                       w_lo[:, slot, k, d * P:(d + 1) * P], z_hi[:, k, half * HALF:(half + 1) * HALF],
                                       z_lo[:, k, half * HALF:(half + 1) * HALF], k == 0, k == KT - 1)
                        mm.then_inc(out_ready, 1)

            def turn_z2(c):
                pe.wait_ge(z2_scaled, c + 1)
                for b in range(2):
                    n = 2 * c + b
                    if n >= 4:
                        pe.wait_ge(lo_done, SP_Z2 + n - 3)
                    for q in range(4):
                        k = 4 * b + q
                        mm = nc.tensor.transpose(aux[:, n % 4, q * P:(q + 1) * P], zb[:, k * P:(k + 1) * P], ident[:])
                    mm.then_inc(z2_turned, 1)

            for j in range(2):
                for c in range(NCH):
                    n = OUT_OUT + 8 * j + c
                    slot = (GR_OUT + j) % 2
                    wait_bank(n)
                    for k in range(KT):
                        if n == OUT_OUT:
                            pe.wait_ge(lo_done, SP_M + 2 * k + 2)
                        if c == 0 and k % 2 == 0:
                            pe.wait_ge(w_ready, LD_OUT + 4 * j + k // 2 + 1)
                        mm = three(acc[:, n % 4, :], m_hi[:, k, c * P:(c + 1) * P], m_lo[:, k, c * P:(c + 1) * P],
                                   w_hi[:, slot, k, :], w_lo[:, slot, k, :], k == 0, k == KT - 1)
                    mm.then_inc(out_ready, 1)
                    if j == 1 and c >= 1:
                        turn_z2(c - 1)

            def mlp_block(f, first):
                pe.wait_ge(lo_done, SP_Z2 + 8)
                for half in range(2):
                    for q in range(FB // P):
                        n = OUT_MLP + 4 * half + q
                        slot = GR_MLP % 2
                        if first and n == OUT_MLP + 1:
                            turn_z2(NCH - 1)
                        if half == 1 and q == 0:
                            pe.wait_ge(lo_done, SP_Z2 + 16)
                        pe.wait_ge(out_free, f * 24 + (n - 3))
                        for k in range(KT):
                            if half == 0 and q == 0 and k % 2 == 0:
                                pe.wait_ge(w_ready, f * 8 + (LD_MLP + k // 2 + 1))
                            mm = three(acc[:, n % 4, :], w_hi[:, slot, k, q * P:(q + 1) * P],
                                       w_lo[:, slot, k, q * P:(q + 1) * P], m_hi[:, k, half * HALF:(half + 1) * HALF],
                                       m_lo[:, k, half * HALF:(half + 1) * HALF], k == 0, k == KT - 1)
                        mm.then_inc(out_ready, 1)
                for j in range(2):
                    for c in range(NCH):
                        n = OUT_MLP + 8 + 8 * j + c
                        slot = (GR_MLP + 1) % 2
                        pe.wait_ge(out_free, f * 24 + (n - 3))
                        if j == 0 and c % 4 == 0:
                            pe.wait_ge(lo_done, f * 8 + (SP_HID + c + 4))
                        for q in range(FB // P):
                            if j == 0 and c == 0:
                                pe.wait_ge(w_ready, f * 8 + (LD_MLP + 4 + q + 1))
                            mm = three(acc[:, n % 4, :], hid_hi[:, q, c * P:(c + 1) * P],
                                       hid_lo[:, q, c * P:(c + 1) * P], w_hi[:, slot, 2 * q + j, :],
                                       w_lo[:, slot, 2 * q + j, :], q == 0, q == FB // P - 1)
                        mm.then_inc(out_ready, 1)

            mlp_block(0, True)
            with pe.Fori(1, N_FB) as f:
                mlp_block(f, False)

        @block.scalar
        def _(act):
            def hi_split(dst, src):
                nc.scalar.activation(dst, src, ACT.Copy).then_inc(hi_done, 1)

            def square_x(c):
                act.wait_ge(x_ready[c], 16)
                if c >= 1:
                    act.wait_ge(ss_done, c)
                nc.scalar.activation(x_junk[:], x_in[:, c, :], ACT.Square, accum_out=ss1[:, c:c + 1])\
                  .then_inc(ss_done, 1)

            def scale_x(c):
                act.wait_ge(x_rstd, c + 1)
                nc.scalar.activation(x_in[:, c, :], x_in[:, c, :], ACT.Copy, scale=rs1[:, c:c + 1])\
                  .then_inc(x_scaled, 1)

            def hi_z(c):
                for b in range(2):
                    n = 2 * c + b
                    act.wait_ge(z_normed, n + 1)
                    hi_split(z_hi[:, 4 * b:4 * b + 4, c * P:(c + 1) * P],
                             z_tmp[:, n % 4, :].rearrange("p (k s) -> p k s", k=4))

            square_x(0)
            square_x(1)
            scale_x(0)
            square_x(2)
            scale_x(1)
            square_x(3)
            hi_z(0)
            scale_x(2)
            scale_x(3)
            hi_z(1)
            square_x(4)
            hi_z(2)
            square_x(5)
            hi_z(3)
            square_x(6)
            square_x(7)
            for c in range(4, NCH):
                scale_x(c)
            for c in range(4, NCH):
                hi_z(c)
            for n in range(8):
                half, m = n // MT, n % MT
                act.wait_ge(out_ready, OUT_U + n + 1)
                w = NT // 2
                ch_ins = nc.scalar.activation(u_all[:, m, :, half * w:(half + 1) * w],
                                              acc[:, n % 4, :].rearrange("p (c j) -> p j c", j=T), ACT.Copy)
                ch_ins.then_inc(out_free, 1)
                if half == 1:
                    act.wait_ge(out_free, OUT_U + n + 1)
                    act.dma_start(u_dram[m], u_all[:, m, :, :]).then_inc(u_out, 16)
            act.wait_ge(ct_turned, 1)
            for ri, dst in enumerate((ctr, cti)):
                for gp in range(2):
                    rows = slice(gp * STATE, (gp + 1) * STATE)
                    src = aux[rows, ri, :].rearrange("p (m q e c) -> p m q e c", q=QP, e=2, c=CH)[:, :, :, gp, :]
                    ins = nc.scalar.activation(dst[rows, :, :].rearrange("p (m q) c -> p m q c", m=MT), src, ACT.Copy)
                    ins.then_inc(ct_ready, 1) if ri == 1 and gp == 1 else None
            act.wait_ge(u_out, 16 * MT)
            def load_u(b):
                for j in range(T):
                    act.dma_start(u_blk[j * CH:(j + 1) * CH, :, :],
                                  u_dram[bass.ds(b, 1), :, j, :].rearrange("a (g c) n -> (a c) g n", c=CH))\
                       .then_inc(u_blk_in, 16)

            def batch(b, steps):
                def gate(o):
                    d, half = o // 2, o % 2
                    act.wait_ge(out_ready, b * 8 + (OUT_GATE + o + 1))
                    if o >= 2 or steps is not STEPS_FIRST:
                        act.wait_ge(gate_sent[o % 2], b * 64 + 16 * (o // 2))
                    nc.scalar.activation(gate_t[:, o % 2, :], acc[:, o % 4, :], ACT.Sigmoid).then_inc(out_free, 1)
                    act.wait_ge(out_free, b * 8 + (OUT_GATE + o + 1))
                    act.dma_start(gate_dram[bass.ds(b * 4 + d, 1), :, half * HALF:(half + 1) * HALF]
                                  .rearrange("a p s -> p (a s)"), gate_t[:, o % 2, :]).then_inc(gate_sent[o % 2], 16)

                def store_y():
                    act.wait_ge(y_prod, b + 1)
                    nc.scalar.activation(y_blk[:].rearrange("p (q e) s -> p e q s", e=2),
                                         aux[:, 2:4, :].rearrange("p e (q s) -> p e q s", q=QP), ACT.Copy)\
                      .then_inc(y_copied, 1)
                    act.wait_ge(y_copied, b + 1)
                    for j in range(T):
                        act.dma_start(y_dram[bass.ds(b, 1), :, j, :].rearrange("a (g c) n -> (a c) g n", c=CH),
                                      y_blk[j * CH:(j + 1) * CH, :, :]).then_inc(y_sent, 16)

                    act.dma_start(u_back[:], u_dram[bass.ds(b, 1)].rearrange("a p j n -> (a p) (j n)"))\
                       .then_inc(y_back, 16)

                for o in range(8):
                    gate(o)
                    if o == steps[0]:
                        act.wait_ge(ab_turned, b + 1)
                        nc.scalar.activation(abt[:].rearrange("p r q s -> p r (q s)"), aux[:, 0:2, :], ACT.Copy)\
                          .then_inc(ab_ready, 1)
                        if steps is not STEPS_FIRST:
                            gelu_sigmoid(b - 1)
                    if o == steps[1]:
                        act.wait_ge(kern, b + 1)
                        nc.scalar.activation(toep[0:CH, :, :].rearrange("p (b g) s -> p b (g s)", b=2),
                                             aux[0:CH, 2:4, :], ACT.Copy).then_inc(kern_ready, 1)
                        act.wait_ge(kern_ready, b + 1)
                        for j in range(1, T):
                            act.dma_start(toep[j * CH:(j + 1) * CH, :, j * CH:P], toep[0:CH, :, 0:P - j * CH])\
                               .then_inc(toep_in, 16)
                    if o == steps[2]:
                        store_y()
                        if steps is STEPS_LAST:
                            act.wait_ge(y_done, MT - 1)
                            for m in range(MT - 1):
                                hi_split(y_hi[:, m, :], y_raw[:, m, :])
                        act.wait_ge(y_sent, b * 128 + 128)
                        act.dma_start(y_blk[:].rearrange("p g s -> p (g s)"),
                                      y_dram[bass.ds(b, 1)].rearrange("a p j n -> (a p) (j n)")).then_inc(y_back, 16)
                        if steps is not STEPS_LAST:
                            load_u(b + 1)

            def gelu_sigmoid(b):
                act.wait_ge(gelu_arg, b + 1)
                nc.scalar.activation(tb[:], ta[:], ACT.Sigmoid, scale=1.5957691216057308).then_inc(gelu_sig, 1)

            load_u(0)
            batch(0, STEPS_FIRST)
            with act.Fori(1, MT - 1) as b:
                batch(b, STEPS_MID)
            batch(MT - 1, STEPS_LAST)
            gelu_sigmoid(MT - 1)
            for i in range(2):
                act.wait_ge(gate_sent[i], 64 * MT)
            act.wait_ge(y_done, MT)
            hi_split(y_hi[:, MT - 1, :], y_raw[:, MT - 1, :])
            for half in range(2):
                for m in range(MT):
                    n = half * MT + m
                    act.wait_ge(out_ready, OUT_GLU + n + 1)
                    if half == 1:
                        act.wait_ge(out_free, OUT_GLU + m + 1)
                    nc.scalar.activation(glu_s[:, m, :], acc[:, n % 4, :], ACT.Sigmoid, bias=bglu[:, m:m + 1])\
                      .then_inc(glu_sig, 1)
                act.wait_ge(out_ready, OUT_GLU + MT * (half + 1))
                for m in range(MT):
                    n = half * MT + m
                    act.wait_ge(out_free, OUT_GLU + n + 1)
                    hi_split(y_hi[:, m, half * HALF:(half + 1) * HALF], y_raw[:, m, half * HALF:(half + 1) * HALF])
            act.dma_start(rope[:], t["rope"].rearrange("(c p) f -> p c f", p=P)).then_inc(ret_in, 16)
            act.dma_start(gam[:], t["gam"]).then_inc(ret_in, 16)
            act.dma_start(mask[:], t["mask"]).then_inc(ret_in, 16)
            order = [(j, half, d) for j in range(2) for half in range(2) for d in range(4)]

            def load_ga(n):
                j, half, d = order[n]
                i = (n + MT) % GA
                act.dma_start(ga_t[:, i, :], gate_dram[4 * j + d, :, half * HALF:(half + 1) * HALF])\
                   .then_inc(ga_in[i], 16)

            load_ga(0)
            load_ga(1)
            act.wait_ge(out_free, OUT_GLU + 8)
            for n in range(2, GA):
                load_ga(n)
            for n, (j, half, d) in enumerate(order):
                i = (n + MT) % GA
                act.wait_ge(out_free, OUT_PA + n + 1)
                act.dma_start(ma_dram[4 * j + d, :, half * HALF:(half + 1) * HALF], ga_t[:, i, :])\
                   .then_inc(ma_sent[i], 16)
                if n >= 2 and n - 2 + GA < len(order):
                    act.wait_ge(ma_sent[(n - 2 + MT) % GA], 16 * ((n - 2) // GA + 1))
                    load_ga(n - 2 + GA)
            act.wait_ge(lo_done, SP_YA + 8)
            act.wait_ge(ret_in, 48)

            def g_sigmoid(h, c):
                n = OUT_RET + c
                act.wait_ge(out_ready, h * 16 + (n + 1))
                act.wait_ge(out_free, h * 16 + (n - 1))
                nc.scalar.activation(sig_t[:, c % 2, :], acc[:, n % 4, 0:DV], ACT.Sigmoid).then_inc(sig_g, 1)

            def head(h, more):
                def cnt(c):
                    return h * 8 + (c + 1)

                def take_qkv(c):
                    n = OUT_RET + NCH + c
                    act.wait_ge(out_ready, h * 16 + (n + 1))
                    act.sem_inc(tick_act, 1)
                    nc.scalar.activation(qk[:, c % 2, 0, :], acc[:, n % 4, 0:DK], ACT.Copy,
                                         scale=gam[:, bass.ds(h, 1)])
                    nc.scalar.activation(qk[:, c % 2, 1, :], acc[:, n % 4, DK:2 * DK], ACT.Copy,
                                         scale=gam[:, bass.ds(h + HEADS, 1)])
                    nc.scalar.activation(vv[:, c % 2, :], acc[:, n % 4, 2 * DK:], ACT.Copy).then_inc(out_free, 1)

                def take_yb(c):
                    act.wait_ge(yb_turned, cnt(c))
                    act.sem_inc(tick_act, 1)
                    nc.scalar.activation(yb_raw[:, bass.ds(h * 2, 2), c * P:(c + 1) * P],
                                         aux[:, 0, 0:2 * P].rearrange("p (e s) -> p e s", e=2), ACT.Copy)\
                      .then_inc(yb_stored, 1)

                def square_o(c):
                    act.wait_ge(o_ready, cnt(c))
                    nc.scalar.activation(o_junk[:], aux[:, 2, 0:DV], ACT.Square, accum_out=oss[:, c % 2:c % 2 + 1])\
                      .then_inc(o_ss, 1)

                def take_qkt(c):
                    act.wait_ge(qk_turned, cnt(c))
                    nc.scalar.activation(qkt[:].rearrange("p a s -> p (a s)"), aux[:, 0, 0:2 * P], ACT.Copy)\
                      .then_inc(qkt_ready, 1)

                def hi_yb(k, cols=slice(0, SEQ)):
                    dst, src = z_hi[:, k, cols], yb_raw[:, k, cols]
                    if cols.stop < SEQ:
                        nc.scalar.activation(dst, src, ACT.Copy).then_inc(hi_part, 1)
                    else:
                        hi_split(dst, src)

                act.wait_ge(out_free, h * 16 + (OUT_RET + NCH))
                for s in range(1, NCH + 4):
                    if s <= NCH:
                        take_qkv(s - 1)
                    if s == NCH and not more:
                        act.wait_ge(out_ready, OUT_PB)
                        hi_yb(0)
                    if s >= 3 and s - 3 < NCH:
                        take_yb(s - 3)
                    if 2 <= s <= NCH + 1:
                        square_o(s - 2)
                    if more and s >= NCH and s < NCH + 3:
                        g_sigmoid(h + 1, 2 * (s - NCH))
                    if s == NCH and not more:
                        hi_yb(1)
                    if s <= NCH:
                        take_qkt(s - 1)
                    if s >= NCH and not more:
                        if s == NCH:
                            for k in range(2, KT - 2):
                                hi_yb(k)
                        elif s == NCH + 1:
                            act.wait_ge(yb_stored, NCH * HEADS - 1)
                            for k in (KT - 2, KT - 1):
                                hi_yb(k, slice(0, SEQ - P))
                        elif s == NCH + 2:
                            act.wait_ge(yb_stored, NCH * HEADS)
                            for k in (KT - 2, KT - 1):
                                hi_yb(k, slice(SEQ - P, SEQ))
                    if more and s >= NCH:
                        for c in ((2 * (s - NCH) + 1,) if s < NCH + 3 else (6, 7)):
                            g_sigmoid(h + 1, c)

            for c in range(NCH):
                g_sigmoid(0, c)
            for i in range(GA):
                act.wait_ge(ma_sent[i], 16 * len([n for n in range(len(order)) if (n + MT) % GA == i]))
            act.dma_start(nmlp[:], t["norm_mlp"].rearrange("a (k p) -> p (a k)", p=P), allow_slow_non_contiguous=True)\
               .then_inc(nmlp_in, 16)

            def block_of(n):
                return n // 2, n % 2

            def load_gb(n):
                d, half = block_of(n)
                act.dma_start(gb_t[:, n % 2, :], gate_dram[KT + d, :, half * HALF:(half + 1) * HALF])\
                   .then_inc(gb_in[n % 2], 16)

            def load_ma(n):
                d, half = block_of(n)
                act.dma_start(ma_t[:], ma_dram[d, :, half * HALF:(half + 1) * HALF]).then_inc(ma_in, 16)

            load_gb(0)
            load_gb(1)
            load_ma(0)
            with act.Fori(0, HEADS - 1) as h:
                head(h, True)
            head(HEADS - 1, False)
            for n in range(16):
                d, half = block_of(n)
                act.wait_ge(merged, n + 1)
                if n + 1 < 16:
                    load_ma(n + 1)
                hi_split(m_hi[:, d, half * HALF:(half + 1) * HALF], gb_t[:, n % 2, :])
                if n + 2 < 16:
                    act.wait_ge(lo_done, SP_M + n + 1)
                    load_gb(n + 2)
            act.wait_ge(out_ready, OUT_OUT)
            act.wait_ge(lo_done, SP_M + 16)
            for c in range(NCH):
                act.dma_start(h_res[:, c, :], x_rows[:, c, :]).then_inc(xr_in[c], 16)

            def hi_z2(c):
                for b in range(2):
                    n = 2 * c + b
                    act.wait_ge(z2_normed, n + 1)
                    hi_split(m_hi[:, 4 * b:4 * b + 4, c * P:(c + 1) * P],
                             aux[:, n % 4, :].rearrange("p (k s) -> p k s", k=4))

            for c in range(NCH):
                act.wait_ge(out_free, OUT_OUT + NCH + c + 1)
                if c >= 1:
                    act.wait_ge(z2_turned, 2 * c)
                nc.scalar.activation(zb[:], h_res[:, c, :], ACT.Square, accum_out=ss2[:, c:c + 1]).then_inc(h_ss, 1)
                if c >= 1:
                    hi_z2(c - 1)
                act.wait_ge(h_rstd, c + 1)
                nc.scalar.activation(zb[:], h_res[:, c, :], ACT.Copy, scale=rs2[:, c:c + 1]).then_inc(z2_scaled, 1)
            hi_z2(NCH - 1)

            def mlp_block(f):
                act.wait_ge(out_free, f * 24 + OUT_MLP)
                for n in range(8):
                    half, q = n // 4, n % 4
                    act.wait_ge(out_ready, f * 24 + (OUT_MLP + n + 1))
                    act.wait_ge(lo_done, f * 8 + (SP_HID + n - 1))
                    nc.scalar.activation(relu[:, n % 2, :], acc[:, n % 4, :], ACT.Relu).then_inc(out_free, 1)
                    if n >= 1:
                        hidden_hi(f, n - 1)
                hidden_hi(f, 7)

            def hidden_hi(f, n):
                half, q = n // 4, n % 4
                act.wait_ge(squared, f * 8 + (n + 1))
                act.wait_ge(out_ready, f * 24 + (OUT_MLP - 4 + 4 * half))
                hi_split(hid_hi[:, q, half * HALF:(half + 1) * HALF], relu[:, n % 2, :])

            with act.Fori(0, N_FB) as f:
                mlp_block(f)
            for c in range(NCH):
                act.wait_ge(out_free, OUT_MLP + 24 * (N_FB - 1) + 16 + c + 1)
                if c >= 1:
                    act.wait_ge(f_ss, c)
                nc.scalar.activation(h_junk[:], h_res[:, c, :], ACT.Square, accum_out=ss2[:, c:c + 1])\
                  .then_inc(f_ss, 1)
                for s, after in ((1, 4), (3, 5), (5, 7)):
                    if c == after:
                        act.wait_ge(f_rstd, 1 if s < 4 else 2)
                        nc.scalar.activation(h_res[:, s, :], h_res[:, s, :], ACT.Copy, scale=rs2[:, s:s + 1])\
                          .then_inc(f_scaled, 1)

        @block.vector
        def _(dve):
            ch = Chain(dve, chain_v)
            link = ch.link
            V = nc.vector

            def lo_split(dst, src, hi):
                V.tensor_tensor(dst, src, hi.bitcast(F32), ALU.subtract).then_inc(lo_done, 1)

            def rstd(dst, a, width, done=None):
                w = dst.shape[-1]
                bits, (tmp, m, y, y2) = rs_bits[:, 0:w], [rs_tmp[:, i, 0:w] for i in range(4)]
                V.tensor_scalar(m, a, -0.5 / width, -0.5 * EPS, ALU.mult, ALU.add)
                link(V.tensor_scalar(tmp, a, 1.0 / width, EPS, ALU.mult, ALU.add))
                link(V.tensor_scalar(bits, tmp.bitcast(I32), 1, None, ALU.arith_shift_right))
                link(V.tensor_scalar(y.bitcast(I32), bits, -1.0, 1597463007.0, ALU.mult, ALU.add))
                for step in range(3):
                    if w == 1:
                        link(V.scalar_tensor_tensor(out=y2, in0=y, scalar=m, in1=y, op0=ALU.mult, op1=ALU.mult))
                    else:
                        link(V.tensor_tensor(y2, y, y, ALU.mult))
                        link(V.tensor_tensor(y2, y2, m, ALU.mult))
                    ins = V.scalar_tensor_tensor(out=dst if step == 2 else y, in0=y2, scalar=1.5, in1=y,
                                                 op0=ALU.add, op1=ALU.mult)
                    if step == 2 and done is not None:
                        ins.then_inc(done, 1)
                    else:
                        link(ins)

            def rstd_x(c, n):
                dve.wait_ge(ss_done, c + n)
                rstd(rs1[:, c:c + n], ss1[:, c:c + n], D)
                dve.sem_inc(x_rstd, n)

            def norm_z(c):
                for b in range(2):
                    n = 2 * c + b
                    dve.wait_ge(z_turned, n + 1)
                    if n >= 4:
                        dve.wait_ge(lo_done, SP_Z + n - 3)
                    V.tensor_tensor(z_tmp[:, n % 4, :].rearrange("p (k s) -> p k s", k=4),
                                    aux[:, n % 4, :].rearrange("p (k s) -> p k s", k=4),
                                    nmix[:, 4 * b:4 * b + 4].unsqueeze(2).broadcast_to([P, 4, P]), ALU.mult)\
                     .then_inc(z_normed, 1)

            def lo_z(c):
                for b in range(2):
                    n = 2 * c + b
                    dve.wait_ge(hi_done, SP_Z + n + 1)
                    lo_split(z_lo[:, 4 * b:4 * b + 4, c * P:(c + 1) * P],
                             z_tmp[:, n % 4, :].rearrange("p (k s) -> p k s", k=4),
                             z_hi[:, 4 * b:4 * b + 4, c * P:(c + 1) * P])

            rstd_x(0, 1)
            rstd_x(1, 1)
            dve.wait_ge(const_in, 32)
            norm_z(0)
            rstd_x(2, 2)
            lo_z(0)
            for c in range(1, 4):
                norm_z(c)
                lo_z(c)
            rstd_x(4, 4)

            dve.wait_ge(par_in, 16 * 16)
            slot_of = {"lr": 0, "li": 1, "ls": 2}

            def cf(name):
                if name not in slot_of:
                    slot_of[name] = len(slot_of)
                return coef[:, slot_of[name], :]

            def ts(dst, src, s1, s2, o1, o2=None):
                if o2 is None:
                    link(V.tensor_scalar(dst, src, s1, None, o1))
                else:
                    link(V.tensor_scalar(dst, src, s1, s2, o1, o2))

            def tt(dst, a, b, op):
                link(V.tensor_tensor(dst, a, b, op))

            def stt(dst, a, s, b, o1, o2):
                link(V.scalar_tensor_tensor(out=dst, in0=a, scalar=s, in1=b, op0=o1, op1=o2))

            def exp(dst, src):
                x, k, r, k1, k2 = cf("ex"), cf("ek"), cf("er"), cf("ek1"), cf("ek2")
                ts(x, src, -175.0, 175.0, ALU.max, ALU.min)
                ts(k, x, 1.4426950408889634, MAGIC, ALU.mult, ALU.add)
                ts(k, k, MAGIC, None, ALU.subtract)
                stt(r, k, -LN2[0], x, ALU.mult, ALU.add)
                stt(r, k, -LN2[1], r, ALU.mult, ALU.add)
                ts(x, r, 1.0 / 5040, 1.0 / 720, ALU.mult, ALU.add)
                for c in (1.0 / 120, 1.0 / 24, 1.0 / 6, 0.5, 1.0):
                    tt(x, x, r, ALU.mult)
                    ts(x, x, c, None, ALU.add)
                tt(x, x, r, ALU.mult)
                ts(x, x, 1.0, None, ALU.add)
                ts(k1, k, 0.5, MAGIC, ALU.mult, ALU.add)
                ts(k1, k1, MAGIC, None, ALU.subtract)
                tt(k2, k, k1, ALU.subtract)
                for q, kk in enumerate((k1, k2)):
                    ts(ibits[:, q, :], kk, 127.0, 8388608.0, ALU.add, ALU.mult)
                    tt(x, x, ibits[:, q, :].bitcast(F32), ALU.mult)
                link(V.tensor_copy(dst, x))

            def sincos(s_dst, c_dst, src):
                import math
                th, k, r2, sp_, cp = cf("th"), cf("sk"), cf("r2"), cf("sp"), cf("cp")
                big = 2.0 * math.pi * 1024.0
                ts(k, src, 1.0 / big, MAGIC, ALU.mult, ALU.add)
                ts(k, k, MAGIC, None, ALU.subtract)
                first = True
                for c in parts(big, 4):
                    stt(th, k, -c, src if first else th, ALU.mult, ALU.add)
                    first = False
                ts(k, th, 2.0 / math.pi, MAGIC, ALU.mult, ALU.add)
                ts(k, k, MAGIC, None, ALU.subtract)
                for c in parts(math.pi / 2, 4):
                    stt(th, k, -c, th, ALU.mult, ALU.add)
                tt(r2, th, th, ALU.mult)
                ts(sp_, r2, -1.9515295891e-4, 8.3321608736e-3, ALU.mult, ALU.add)
                tt(sp_, sp_, r2, ALU.mult)
                ts(sp_, sp_, -1.6666654611e-1, None, ALU.add)
                tt(sp_, sp_, r2, ALU.mult)
                tt(sp_, sp_, th, ALU.mult)
                tt(sp_, sp_, th, ALU.add)
                ts(cp, r2, 2.443315711809948e-5, -1.388731625493765e-3, ALU.mult, ALU.add)
                tt(cp, cp, r2, ALU.mult)
                ts(cp, cp, 4.166664568298827e-2, None, ALU.add)
                tt(cp, cp, r2, ALU.mult)
                ts(cp, cp, -0.5, None, ALU.add)
                tt(cp, cp, r2, ALU.mult)
                ts(cp, cp, 1.0, None, ALU.add)
                f, n, sg, od = cf("qf"), cf("qn"), cf("qs"), cf("qo")
                ts(f, k, 0.25, -0.375, ALU.mult, ALU.add)
                ts(f, f, MAGIC, None, ALU.add)
                ts(f, f, MAGIC, None, ALU.subtract)
                stt(n, f, -4.0, k, ALU.mult, ALU.add)
                ts(sg, n, 2.0, None, ALU.is_ge)
                stt(od, sg, -2.0, n, ALU.mult, ALU.add)
                ts(sg, sg, -2.0, 1.0, ALU.mult, ALU.add)
                tt(f, cp, sp_, ALU.subtract)
                tt(f, f, od, ALU.mult)
                tt(n, cp, sp_, ALU.add)
                tt(n, n, od, ALU.mult)
                tt(f, sp_, f, ALU.add)
                tt(n, cp, n, ALU.subtract)
                tt(s_dst, f, sg, ALU.mult)
                tt(c_dst, n, sg, ALU.mult)

            lr, li = cf("lr"), cf("li")
            step, mag, ang = cf("step"), cf("mag"), cf("ang")
            exp(step, cf("ls"))
            tt(ang, lr, step, ALU.mult)
            exp(mag, ang)
            for c in range(4, NCH):
                norm_z(c)
                if c >= 5:
                    lo_z(c - 1)
            lo_z(NCH - 1)
            tt(ang, li, step, ALU.mult)
            sn, cs = cf("sn"), cf("cs")
            sincos(sn, cs, ang)
            link(V.memset(pwr[:, 0, :], 1.0))
            link(V.memset(pwi[:, 0, :], 0.0))
            tt(pwr[:, 1, :], mag, cs, ALU.mult)
            tt(pwi[:, 1, :], mag, sn, ALU.mult)
            nr, den, kr, ki, tm = cf("nr"), cf("den"), cf("kr"), cf("ki"), cf("tm")
            ts(nr, pwr[:, 1, :], 1.0, None, ALU.subtract)
            tt(den, lr, lr, ALU.mult)
            tt(tm, li, li, ALU.mult)
            tt(den, den, tm, ALU.add)
            link(V.reciprocal(den, den))
            tt(kr, nr, lr, ALU.mult)
            tt(tm, pwi[:, 1, :], li, ALU.mult)
            tt(kr, kr, tm, ALU.add)
            tt(kr, kr, den, ALU.mult)
            tt(ki, pwi[:, 1, :], lr, ALU.mult)
            tt(tm, nr, li, ALU.mult)
            tt(ki, ki, tm, ALU.subtract)
            tt(ki, ki, den, ALU.mult)

            def wide(a):
                return a.unsqueeze(2).broadcast_to([P, PAIRS, CH])

            br, bi = b_raw[:, 0, :, :], b_raw[:, 1, :, :]
            tt(bbr[:], br, wide(kr), ALU.mult)
            tt(bbi[:], bi, wide(ki), ALU.mult)
            tt(bbr[:], bbr[:], bbi[:], ALU.subtract)
            tt(bbi[:], br, wide(ki), ALU.mult)
            tt(bi, bi, wide(kr), ALU.mult)
            tt(bbi[:], bbi[:], bi, ALU.add)

            def powers(pr, pi, i0, count):
                n = 1
                while n < count:
                    src, dst, top = slice(i0, i0 + n), slice(i0 + n, i0 + 2 * n), slice(i0 + n - 1, i0 + n)
                    t1, t2, t3, t4 = [coef[:, 40 + 4 * i:40 + 4 * i + n, :] for i in range(4)]
                    xr, xi = [p[:, top, :].broadcast_to([P, n, PAIRS]) for p in (pr, pi)]
                    V.tensor_tensor(t1, pr[:, src, :], xr, ALU.mult)
                    V.tensor_tensor(t2, pi[:, src, :], xi, ALU.mult)
                    V.tensor_tensor(t3, pr[:, src, :], xi, ALU.mult)
                    link(V.tensor_tensor(t4, pi[:, src, :], xr, ALU.mult))
                    V.tensor_tensor(pr[:, dst, :], t1, t2, ALU.subtract)
                    link(V.tensor_tensor(pi[:, dst, :], t3, t4, ALU.add))
                    n *= 2

            powers(pwr, pwi, 1, T)
            for k in range(T):
                V.tensor_copy(rpr[:, k, :], pwr[:, T - 1 - k, :])
                V.tensor_copy(rpi[:, k, :], pwi[:, T - 1 - k, :])
            V.tensor_copy(p8r[:, 0, :], pwr[:, T, :])
            link(V.tensor_copy(p8i[:, 0, :], pwi[:, T, :]))
            powers(p8r, p8i, 0, T)
            V.tensor_copy(p64r[:, 0, :], p8r[:, T - 1, :])
            link(V.tensor_copy(p64i[:, 0, :], p8i[:, T - 1, :]))
            for k in range(1, 4):
                t1, t2, t3 = [coef[:, 40 + 4 * i, :] for i in range(3)]
                xr, xi = p64r[:, k - 1, :], p64i[:, k - 1, :]
                V.tensor_tensor(t1, xr, xr, ALU.mult)
                V.tensor_tensor(t2, xi, xi, ALU.mult)
                link(V.tensor_tensor(t3, xr, xi, ALU.mult))
                V.tensor_tensor(p64r[:, k, :], t1, t2, ALU.subtract)
                link(V.tensor_tensor(p64i[:, k, :], t3, t3, ALU.add))
            dve.wait_ge(ct_ready, 1)
            link(V.memset(toep[:].rearrange("p g s -> p (g s)"), 0.0))
            link(V.memset(hst[:, :, :, 0:1], 0.0))

            def prepare(b):
                qs = bass.ds(b * QP, QP)

                def outer(dst, x, pw, n):
                    return V.tensor_tensor(dst, x[:, qs, :].unsqueeze(2).broadcast_to([P, QP, n, CH]),
                                           pw[:, 0:n, qs].rearrange("p t q -> p q t").unsqueeze(3)
                                           .broadcast_to([P, QP, n, CH]), ALU.mult)

                t_a = ta[:, 0:QP * (T + 1) * CH].rearrange("p (q t c) -> p q t c", q=QP, c=CH)
                t_b = tb[:, 0:QP * (T + 1) * CH].rearrange("p (q t c) -> p q t c", q=QP, c=CH)
                outer(car[:], ctr, pwr, T + 1)
                outer(t_a, cti, pwi, T + 1)
                outer(can[:], ctr, pwi, T + 1)
                link(outer(t_b, cti, pwr, T + 1))
                V.tensor_tensor(car[:], car[:], t_a, ALU.subtract)
                flat = can[:].rearrange("p q t c -> p (q t c)")
                link(V.scalar_tensor_tensor(out=flat, in0=tb[:, 0:QP * (T + 1) * CH], scalar=-1.0, in1=flat,
                                            op0=ALU.mult, op1=ALU.subtract))
                t_a = ta[:, 0:QP * T * CH].rearrange("p (q t c) -> p q t c", q=QP, c=CH)
                t_b = tb[:, 0:QP * T * CH].rearrange("p (q t c) -> p q t c", q=QP, c=CH)
                outer(abr[:], bbr, rpr, T)
                outer(t_a, bbi, rpi, T)
                outer(abi[:], bbr, rpi, T)
                link(outer(t_b, bbi, rpr, T))
                V.tensor_tensor(abr[:], abr[:], t_a, ALU.subtract)
                V.tensor_tensor(abi[:], abi[:], t_b, ALU.add).then_inc(prep, 1)
                dve.wait_ge(prep, b + 1)

            def scan(b):
                q0 = b * QP
                dve.wait_ge(x_state, b + 1)
                hb = hst[:, :, :, 1:NT + 1]
                link(V.tensor_copy(hb.rearrange("p r q n -> p (r q) n"),
                                   aux[:, 0:2, :].rearrange("p r (q n) -> p (r q) n", q=QP)))
                blocks = hb.rearrange("p r q (s i) -> p r q s i", i=T)

                def mac(dst, ar, ai, x, shape, n, last=False):
                    names = "abc"[:len(shape)]
                    sizes = dict(zip(names, shape))

                    def both(buf):
                        return buf[:, 0:2 * n].rearrange(f"p (r {' '.join(names)}) -> p r {' '.join(names)}", r=2, **sizes)

                    t1, t2 = both(ta), both(tb)
                    wide_ar, wide_ai = [a.unsqueeze(1).broadcast_to([P, 2] + shape) for a in (ar, ai)]
                    V.tensor_tensor(t1, x, wide_ar, ALU.mult)
                    link(V.tensor_tensor(t2, x, wide_ai, ALU.mult))
                    V.tensor_tensor(t1[:, 0], t1[:, 0], t2[:, 1], ALU.subtract)
                    link(V.tensor_tensor(t1[:, 1], t1[:, 1], t2[:, 0], ALU.add))
                    ins = V.tensor_tensor(dst, dst, t1, ALU.add)
                    if last:
                        ins.then_inc(scanned, 1)
                    else:
                        link(ins)

                a8 = [p[:, 0, bass.ds(q0, QP)].unsqueeze(2).broadcast_to([P, QP, SUP]) for p in (p8r, p8i)]
                for i in range(1, T):
                    mac(blocks[:, :, :, :, i], a8[0], a8[1], blocks[:, :, :, :, i - 1], [QP, SUP], QP * SUP)
                for lv in range(4):
                    d = 1 << lv
                    w = SUP - d
                    a64 = [p[:, lv, bass.ds(q0, QP)].unsqueeze(2).broadcast_to([P, QP, w]) for p in (p64r, p64i)]
                    mac(blocks[:, :, :, d:, T - 1], a64[0], a64[1], blocks[:, :, :, 0:w, T - 1], [QP, w], QP * w)
                for q in range(QP):
                    w = SUP - 1
                    pq = [p[:, 0:T - 1, bass.ds(q0 + q, 1)].rearrange("p i a -> p a i").broadcast_to([P, w, T - 1])
                          for p in (p8r, p8i)]
                    prev = blocks[:, :, q, 0:w, T - 1].unsqueeze(3).broadcast_to([P, 2, w, T - 1])
                    mac(blocks[:, :, q, 1:, 0:T - 1], pq[0], pq[1], prev, [w, T - 1], w * (T - 1), last=q == QP - 1)

            def gelu(b):
                dve.wait_ge(y_back, b * 32 + 32)
                y = y_blk[:].rearrange("p g s -> p (g s)")
                link(V.scalar_tensor_tensor(out=y, in0=u_back[:], scalar=dskip[:, bass.ds(b, 1)], in1=y,
                                            op0=ALU.mult, op1=ALU.add))
                link(V.tensor_tensor(ta[:], y, y, ALU.mult))
                link(V.tensor_scalar(ta[:], ta[:], 0.044715, 1.0, ALU.mult, ALU.add))
                V.tensor_tensor(ta[:], ta[:], y, ALU.mult).then_inc(gelu_arg, 1)
                dve.wait_ge(gelu_sig, b + 1)
                V.tensor_tensor(y_raw[:, bass.ds(b, 1), :].rearrange("p a (n j) -> p (a j) n", j=T),
                                y.rearrange("p (j n) -> p j n", j=T), tb[:].rearrange("p (j n) -> p j n", j=T),
                                ALU.mult).then_inc(y_done, 1)
                dve.wait_ge(y_done, b + 1)

            def lo_y(m):
                dve.wait_ge(hi_done, SP_Y + m + 1)
                lo_split(y_lo[:, m, :], y_raw[:, m, :], y_hi[:, m, :])

            prepare(0)
            with dve.Fori(0, MT - 1) as b:
                ch.enter(b, PER_BATCH)
                scan(b)
                dve.wait_ge(y_prod, b + 1)
                prepare(b + 1)
                gelu(b)
                ch.leave(MT - 1)
            scan(MT - 1)
            for m in range(MT - 1):
                lo_y(m)
            gelu(MT - 1)
            lo_y(MT - 1)
            for half in range(2):
                hs = slice(half * HALF, (half + 1) * HALF)
                for m in range(MT):
                    n = half * MT + m
                    dve.wait_ge(glu_sig, n + 1)
                    V.tensor_tensor(y_raw[:, m, hs], y_raw[:, m, hs], glu_s[:, m, :], ALU.mult).then_inc(out_free, 1)
                    dve.wait_ge(out_free, OUT_GLU + n + 1)
                for m in range(MT):
                    n = half * MT + m
                    dve.wait_ge(hi_done, SP_YA + n + 1)
                    lo_split(y_lo[:, m, hs], y_raw[:, m, hs], y_hi[:, m, hs])
            for n in range(16):
                i = (n + MT) % GA
                dve.wait_ge(out_ready, OUT_PA + n + 1)
                dve.wait_ge(ga_in[i], 16 * (n // GA + 1))
                V.tensor_tensor(ga_t[:, i, :], acc[:, n % 4, :], ga_t[:, i, :], ALU.mult).then_inc(out_free, 1)

            dve.wait_ge(ret_in, 48)

            def g_silu(h, c):
                n = OUT_RET + c
                dve.wait_ge(sig_g, h * 8 + (c + 1))
                V.tensor_tensor(silu_g[:, c, :], acc[:, n % 4, 0:DV], sig_t[:, c % 2, :], ALU.mult)\
                 .then_inc(out_free, 1)

            def head(h, more):
                def cnt(c):
                    return h * 8 + (c + 1)

                def rotate(c):
                    dve.wait_ge(out_free, h * 16 + (OUT_RET + NCH + c + 1))
                    src = qk[:, c % 2, :, :].rearrange("p a (b d) -> p (a b) d", b=2)
                    cos = rope[:, c, 0:DK // 2].unsqueeze(1).broadcast_to([P, 4, DK // 2])
                    sin = rope[:, c, DK // 2:].unsqueeze(1).broadcast_to([P, 4, DK // 2])
                    V.tensor_tensor(rc[:].rearrange("p a b d -> p (a b) d"), src, cos, ALU.mult)
                    link(V.tensor_tensor(rsn[:].rearrange("p a b d -> p (a b) d"), src, sin, ALU.mult))
                    for a, dst in ((0, rot[:, 0, :, :]),
                                   (1, kvk[:, c % 2, :].rearrange("p (b d) -> p b d", b=2))):
                        V.tensor_tensor(dst[:, 0, :], rc[:, a, 0, :], rsn[:, a, 1, :], ALU.subtract)
                        ins = V.tensor_tensor(dst[:, 1, :], rsn[:, a, 0, :], rc[:, a, 1, :], ALU.add)
                    ins.then_inc(rotated, 1)

                def decay(c):
                    dve.wait_ge(scores, cnt(c))
                    V.tensor_tensor(prob[:], aux[:, 1, 0:P], mask[:, bass.ds(h, 1), :].rearrange("p a s -> p (a s)"),
                                    ALU.mult).then_inc(prob_ready, 1)

                def norm_o(c):
                    dve.wait_ge(o_ready, cnt(c))
                    if c == NCH - 1:
                        pass
                    elif c == 0:
                        V.tensor_copy(state[:], aux[:, 3, 0:DV]).then_inc(state_ready, 1)
                    else:
                        V.scalar_tensor_tensor(out=state[:], in0=state[:], scalar=gam[:, bass.ds(h + 2 * HEADS, 1)],
                                               in1=aux[:, 3, 0:DV], op0=ALU.mult, op1=ALU.add).then_inc(state_ready, 1)
                    dve.wait_ge(o_ss, cnt(c))
                    rstd(ors[:, 0:1], oss[:, c % 2:c % 2 + 1], DV)
                    V.scalar_tensor_tensor(out=yb[:], in0=aux[:, 2, 0:DV], scalar=ors[:, 0:1], in1=silu_g[:, c, :],
                                           op0=ALU.mult, op1=ALU.mult).then_inc(yb_ready, 1)
                    dve.wait_ge(yb_ready, cnt(c))

                def lo_yb(k):
                    dve.wait_ge(hi_done, SP_YB + k + 1)
                    lo_split(z_lo[:, k, :], yb_raw[:, k, :], z_hi[:, k, :])

                for s in range(1, NCH + 2):
                    if s <= NCH:
                        rotate(s - 1)
                    if s == NCH and not more:
                        lo_yb(0)
                    if s >= 2:
                        norm_o(s - 2)
                    if more and s >= NCH:
                        g_silu(h + 1, 2 * (s - NCH))
                    if s == NCH and not more:
                        lo_yb(1)
                        lo_yb(2)
                    if s <= NCH:
                        decay(s - 1)
                    if more and s >= NCH:
                        g_silu(h + 1, 2 * (s - NCH) + 1)
                    if s == NCH and not more:
                        for k in range(3, KT - 2):
                            lo_yb(k)
                if more:
                    for c in range(4, NCH):
                        g_silu(h + 1, c)
                else:
                    for i, k in enumerate((KT - 2, KT - 1)):
                        cols = slice(0, SEQ - P)
                        dve.wait_ge(hi_part, i + 1)
                        V.tensor_tensor(z_lo[:, k, cols], yb_raw[:, k, cols], z_hi[:, k, cols].bitcast(F32),
                                        ALU.subtract)
                    for k in (KT - 2, KT - 1):
                        cols = slice(SEQ - P, SEQ)
                        dve.wait_ge(hi_done, SP_YB + k + 1)
                        lo_split(z_lo[:, k, cols], yb_raw[:, k, cols], z_hi[:, k, cols])

            for c in range(NCH):
                g_silu(0, c)
            with dve.Fori(0, HEADS - 1) as h:
                ch.enter(h, PER_HEAD)
                head(h, True)
                ch.leave(HEADS - 1)
            head(HEADS - 1, False)
            dve.wait_ge(out_free, OUT_PB)
            for n in range(16):
                d, half = n // 2, n % 2
                hs = slice(half * HALF, (half + 1) * HALF)
                dve.wait_ge(out_ready, OUT_PB + n + 1)
                dve.wait_ge(gb_in[n % 2], 16 * (n // 2 + 1))
                V.tensor_tensor(gb_t[:, n % 2, :], acc[:, n % 4, :], gb_t[:, n % 2, :], ALU.mult).then_inc(out_free, 1)
                dve.wait_ge(out_free, OUT_PB + n + 1)
                dve.wait_ge(ma_in, 16 * (n + 1))
                V.tensor_tensor(gb_t[:, n % 2, :], gb_t[:, n % 2, :], ma_t[:], ALU.add).then_inc(merged, 1)
                dve.wait_ge(hi_done, SP_M + n + 1)
                lo_split(m_lo[:, d, hs], gb_t[:, n % 2, :], m_hi[:, d, hs])
            def add_h(n, c, j):
                dve.wait_ge(out_ready, n + 1)
                hs = slice(j * HALF, (j + 1) * HALF)
                return V.tensor_tensor(h_res[:, c, hs], h_res[:, c, hs], acc[:, n % 4, :], ALU.add)

            for c in range(NCH):
                dve.wait_ge(xr_in[c], 16)
                add_h(OUT_OUT + c, c, 0).then_inc(out_free, 1)
            dve.wait_ge(nmlp_in, 16)

            def norm_z2(c):
                for b in range(2):
                    n = 2 * c + b
                    dve.wait_ge(z2_turned, n + 1)
                    V.tensor_tensor(aux[:, n % 4, :].rearrange("p (k s) -> p k s", k=4),
                                    aux[:, n % 4, :].rearrange("p (k s) -> p k s", k=4),
                                    nmlp[:, 4 * b:4 * b + 4].unsqueeze(2).broadcast_to([P, 4, P]), ALU.mult)\
                     .then_inc(z2_normed, 1)

            def lo_z2(c):
                for b in range(2):
                    n = 2 * c + b
                    dve.wait_ge(hi_done, SP_Z2 + n + 1)
                    lo_split(m_lo[:, 4 * b:4 * b + 4, c * P:(c + 1) * P],
                             aux[:, n % 4, :].rearrange("p (k s) -> p k s", k=4),
                             m_hi[:, 4 * b:4 * b + 4, c * P:(c + 1) * P])

            for c in range(NCH):
                add_h(OUT_OUT + NCH + c, c, 1).then_inc(out_free, 1)
                if c >= 1:
                    norm_z2(c - 1)
                dve.wait_ge(h_ss, c + 1)
                rstd(rs2[:, c:c + 1], ss2[:, c:c + 1], D, done=h_rstd)
                if c >= 1:
                    lo_z2(c - 1)
            norm_z2(NCH - 1)
            lo_z2(NCH - 1)

            def mlp_block(f, last):
                dve.wait_ge(out_free, f * 24 + OUT_MLP)
                for n in range(8):
                    half, q = n // 4, n % 4
                    hs = slice(half * HALF, (half + 1) * HALF)
                    dve.wait_ge(out_free, f * 24 + (OUT_MLP + n + 1))
                    V.tensor_tensor(relu[:, n % 2, :], relu[:, n % 2, :], relu[:, n % 2, :], ALU.mult)\
                     .then_inc(squared, 1)
                    dve.wait_ge(hi_done, f * 8 + (SP_HID + n + 1))
                    lo_split(hid_lo[:, q, hs], relu[:, n % 2, :], hid_hi[:, q, hs])
                for j in range(2):
                    for c in range(NCH):
                        n = OUT_MLP + 8 + 8 * j + c
                        dve.wait_ge(out_ready, f * 24 + (n + 1))
                        hs = slice(j * HALF, (j + 1) * HALF)
                        V.tensor_tensor(h_res[:, c, hs], h_res[:, c, hs], acc[:, n % 4, :], ALU.add)\
                         .then_inc(out_free, 1)
                        if last and j == 1 and c == 4:
                            last_rstd(0, 4)
                            dve.wait_ge(f_rstd, 1)
                            dve.wait_ge(nf_in, 16)
                            last_norm(0)
                            last_norm(2)
                        if last and j == 1 and c == 6:
                            last_rstd(4, 2)
                            dve.wait_ge(f_rstd, 2)

            def last_rstd(c, n):
                dve.wait_ge(f_ss, c + n)
                rstd(rs2[:, c:c + n], ss2[:, c:c + n], D, done=f_rstd)

            def last_norm(c):
                V.scalar_tensor_tensor(out=h_res[:, c, :], in0=h_res[:, c, :], scalar=rs2[:, c:c + 1], in1=nf,
                                       op0=ALU.mult, op1=ALU.mult).then_inc(f_done, 1)

            with dve.Fori(0, N_FB - 1) as f:
                mlp_block(f, False)
            mlp_block(N_FB - 1, True)
            last_norm(4)
            last_rstd(6, 2)
            dve.wait_ge(f_rstd, 3)
            last_norm(6)
            last_norm(7)


_INS = ["x", "w_in", "lam_re", "lam_im", "b_re", "b_im", "c_re", "c_im", "d_skip", "log_step", "w_glu", "b_glu",
        "w_proj_ssm", "w_proj_ret", "w_out", "norm_mix", "norm_mlp", "w_up", "w_down", "norm_final"]


def tables():
    import numpy as np
    inv = (10000.0 ** (-np.arange(0, DK, 2, dtype=np.float64) / DK)).astype(np.float32)
    ang = (np.arange(SEQ, dtype=np.float32)[:, None] * inv[None, :]).astype(np.float64)
    rope = np.concatenate([np.cos(ang), np.sin(ang)], axis=1).astype(np.float32)
    lg = np.log(1.0 - 2.0 ** (-5.0 - np.arange(HEADS, dtype=np.float64)))
    idx = np.arange(P, dtype=np.float64)[:, None]
    gam = np.concatenate([np.exp((idx + 1) * lg), np.exp((P - 1 - idx) * lg) * DK ** -0.5,
                          np.exp(P * lg) * np.ones((P, 1))], axis=1).astype(np.float32)
    causal = (np.arange(P)[None, :] >= np.arange(P)[:, None]).astype(np.float64)
    mask = (causal[:, None, :] * np.exp(-P * lg)[None, :, None]).astype(np.float32)
    return {"rope": rope, "gam": gam, "mask": mask, "ident": np.eye(P, dtype=np.float32)}


def kernel(**inputs):
    import numpy as np
    import concourse.bacc as bacc
    from concourse.bass_utils import run_bass_kernel_spmd

    nc = bacc.Bacc("TRN2", target_bir_lowering=False, num_devices=1)
    arrays = {name: np.ascontiguousarray(inputs[name]) for name in _INS}
    arrays.update(tables())
    t = {name: nc.dram_tensor("in_" + name, a.shape, mybir.dt.from_np(a.dtype), kind="ExternalInput").ap()
         for name, a in arrays.items()}
    t["out"] = nc.dram_tensor("out", (1, SEQ, D), F32, kind="ExternalOutput").ap()
    build(nc, t)
    return run_bass_kernel_spmd(nc, [{"in_" + name: a for name, a in arrays.items()}], core_ids=[0]).results[0]["out"]
```
